# Optimizing a Trainium2 kernel written in Bass

```python
import jax
import jax.numpy as jnp
from jax import lax
import numpy as np
import jax, jax.numpy as jnp

D_MODEL = 1024
BATCH = 1
SEQ = 256
DEPTH = 2

GRID_W = 64
CTX_LEN = 256
N_EVEN = (DEPTH + 1) // 2
N_ODD = DEPTH // 2
D_FF = 4 * D_MODEL
N_MOD = 6
EPS = 1e-6
F32 = jnp.float32

MLA_HEADS = 8
MLA_NOPE = 64
MLA_ROPE = 32
MLA_V = 64
MLA_QK = MLA_NOPE + MLA_ROPE
MLA_Q_RANK = 3 * D_MODEL // 8
MLA_KV_RANK = D_MODEL // 4
ROPE_THETA = 10000.0
Q_BLOCK = 128

GLA_HEADS = 4
GLA_DK = 64
GLA_DV = 128
GLA_GATE_RANK = 16
GLA_GATE_NORM = 16.0
GLA_CHUNK = 64

GDN_HEADS = 8
GDN_DK = 64
GDN_DV = 128
GDN_CONV = 3
GDN_CHUNK = 64

EVEN_SPLITS = (MLA_Q_RANK, MLA_KV_RANK, MLA_ROPE,
               GLA_HEADS * GLA_DK, GLA_HEADS * GLA_DK, GLA_HEADS * GLA_DV, GLA_HEADS * GLA_DV,
               2 * GLA_GATE_RANK)
EVEN_IN = 2240
MIX_WIDTH = MLA_HEADS * MLA_V + GLA_HEADS * GLA_DV
GDN_QKV = 2 * GDN_HEADS * GDN_DK + GDN_HEADS * GDN_DV
ODD_SPLITS = (GDN_QKV, GDN_HEADS * GDN_DV, 2 * GDN_HEADS, 2 * GDN_HEADS)
ODD_IN = 3104
GDN_WIDTH = GDN_HEADS * GDN_DV


def rms_norm(x, w):
    xf = x.astype(F32)
    y = xf * lax.rsqrt(jnp.mean(xf * xf, axis=-1, keepdims=True) + EPS)
    return (y * w.astype(F32)).astype(x.dtype)

def l2norm(t):
    tf = t.astype(F32)
    return (tf * lax.rsqrt(jnp.sum(tf * tf, axis=-1, keepdims=True) + EPS)).astype(t.dtype)

def split_cols(y, sizes):
    out, start = [], 0
    for s in sizes:
        out.append(y[..., start:start + s])
        start += s
    return out

def modulate(h, shift, scale):
    return h * (1.0 + scale) + shift

def flip_seq(ts):
    return tuple(jnp.flip(t, axis=2) for t in ts)

def axial_rope_tables(n_tokens):
    rows = n_tokens // GRID_W
    row = jnp.repeat(jnp.arange(rows, dtype=F32), GRID_W)
    col = jnp.tile(jnp.arange(GRID_W, dtype=F32), rows)
    axis_dim = MLA_ROPE // 2
    inv_freq = ROPE_THETA ** (-jnp.arange(0, axis_dim, 2, dtype=F32) / axis_dim)
    ang = jnp.concatenate([row[:, None] * inv_freq, col[:, None] * inv_freq], axis=-1)
    return jnp.cos(ang), jnp.sin(ang)

def apply_axial_rope(x, cos, sin):
    shp = x.shape
    nf = MLA_ROPE // 4
    xf = x.astype(F32).reshape(shp[:-1] + (2, 2, nf))
    x1, x2 = xf[..., 0, :], xf[..., 1, :]
    cos = cos.reshape(-1, 2, nf)
    sin = sin.reshape(-1, 2, nf)
    out = jnp.stack([x1 * cos - x2 * sin, x2 * cos + x1 * sin], axis=-2)
    return out.reshape(shp).astype(x.dtype)

def mla_attend(q, k, v):
    B, H, Lq, D = q.shape
    scale = MLA_QK ** -0.5
    nb = Lq // Q_BLOCK
    qb = jnp.moveaxis(q.reshape(B, H, nb, Q_BLOCK, D), 2, 0)

    def one(qblk):
        s = jnp.einsum('bhqd,bhkd->bhqk', qblk, k).astype(F32) * scale
        p = jax.nn.softmax(s, axis=-1).astype(v.dtype)
        return jnp.einsum('bhqk,bhkv->bhqv', p, v)

    o = lax.map(one, qb)
    return jnp.moveaxis(o, 0, 2).reshape(B, H, Lq, v.shape[-1])

def gla_chunked(q, k, v, logg, s0):
    out_dtype = v.dtype
    q, k, v, logg = (t.astype(F32) for t in (q, k, v, logg))
    B, H, L, DK = q.shape
    DV = v.shape[-1]
    C = GLA_CHUNK
    n = L // C
    q = q.reshape(B, H, n, C, DK) * DK ** -0.5
    k = k.reshape(B, H, n, C, DK)
    v = v.reshape(B, H, n, C, DV)
    b = jnp.cumsum(logg.reshape(B, H, n, C, DK), axis=3)
    q_dec = q * jnp.exp(b)
    k_inv = k * jnp.exp(-b)
    k_end = k * jnp.exp(b[..., -1:, :] - b)
    g_end = jnp.exp(b[..., -1, :])
    incl = jnp.tril(jnp.ones((C, C), bool))
    a = jnp.where(incl, jnp.einsum('bhnid,bhnjd->bhnij', q_dec, k_inv), 0.0)
    o_intra = jnp.einsum('bhnij,bhnjv->bhniv', a, v)

    def step(s, xs):
        qd_c, ke_c, v_c, ge_c = xs
        o = jnp.einsum('bhcd,bhdv->bhcv', qd_c, s)
        s = s * ge_c[..., None] + jnp.einsum('bhcd,bhcv->bhdv', ke_c, v_c)
        return s, o

    xs = tuple(jnp.moveaxis(t, 2, 0) for t in (q_dec, k_end, v, g_end))
    s_fin, o_inter = lax.scan(step, s0, xs)
    o = o_intra + jnp.moveaxis(o_inter, 0, 2)
    return o.reshape(B, H, L, DV).astype(out_dtype), s_fin

def gdn_chunked(q, k, v, log_a, beta, s0):
    out_dtype = v.dtype
    q, k, v, log_a, beta = (t.astype(F32) for t in (q, k, v, log_a, beta))
    B, H, L, DK = q.shape
    DV = v.shape[-1]
    C = GDN_CHUNK
    n = L // C
    q = q.reshape(B, H, n, C, DK) * DK ** -0.5
    k = k.reshape(B, H, n, C, DK)
    v = v.reshape(B, H, n, C, DV)
    beta = beta.reshape(B, H, n, C)[..., None]
    g = jnp.cumsum(log_a.reshape(B, H, n, C), axis=-1)
    incl = jnp.tril(jnp.ones((C, C), bool))
    strict = jnp.tril(jnp.ones((C, C), bool), -1)
    diff = g[..., :, None] - g[..., None, :]
    decay = jnp.where(incl, jnp.exp(jnp.where(incl, diff, 0.0)), 0.0)
    kb = k * beta
    a_mat = jnp.where(strict, jnp.einsum('bhnid,bhnjd->bhnij', kb, k) * decay, 0.0) + jnp.eye(C, dtype=F32)
    rhs = jnp.concatenate([v * beta, kb * jnp.exp(g)[..., None]], axis=-1)
    sol = lax.linalg.triangular_solve(a_mat, rhs, left_side=True, lower=True)
    u, w = sol[..., :DV], sol[..., DV:]
    qk = jnp.einsum('bhnid,bhnjd->bhnij', q, k) * decay
    q_dec = q * jnp.exp(g)[..., None]
    k_end = k * jnp.exp(g[..., -1:] - g)[..., None]
    g_end = jnp.exp(g[..., -1])

    def step(s, xs):
        qk_c, qd_c, w_c, u_c, ke_c, ge_c = xs
        v_new = u_c - jnp.einsum('bhcd,bhdv->bhcv', w_c, s)
        o = jnp.einsum('bhcd,bhdv->bhcv', qd_c, s) + jnp.einsum('bhcs,bhsv->bhcv', qk_c, v_new)
        s = s * ge_c[..., None, None] + jnp.einsum('bhcd,bhcv->bhdv', ke_c, v_new)
        return s, o

    xs = tuple(jnp.moveaxis(t, 2, 0) for t in (qk, q_dec, w, u, k_end, g_end))
    s_fin, o = lax.scan(step, s0, xs)
    o = jnp.moveaxis(o, 0, 2).reshape(B, H, L, DV)
    return o.astype(out_dtype), s_fin

def bidir_scan(scan_fn, ctx_f, ctx_b, lat_f, lat_b, s0):
    o_cf, s_f = scan_fn(*ctx_f, s0)
    o_cb, s_b = scan_fn(*flip_seq(ctx_b), s0)
    o_lf, _ = scan_fn(*lat_f, s_f)
    o_lb, _ = scan_fn(*flip_seq(lat_b), s_b)
    return o_lf + jnp.flip(o_lb, axis=2), (o_cf, o_cb)

def even_project(y, q_norm, w_uq, kv_norm, w_ukv, gate_up, gate_bias, rope):
    cq, ckv, kpe, gq, gk, gv, gg, glow = split_cols(y, EVEN_SPLITS)
    B, L, _ = y.shape
    q = (rms_norm(cq, q_norm) @ w_uq).reshape(B, L, MLA_HEADS, MLA_QK).transpose(0, 2, 1, 3)
    q_nope, q_pe = q[..., :MLA_NOPE], q[..., MLA_NOPE:]
    kv = (rms_norm(ckv, kv_norm) @ w_ukv).reshape(B, L, MLA_HEADS, MLA_NOPE + MLA_V).transpose(0, 2, 1, 3)
    k_nope, mv = kv[..., :MLA_NOPE], kv[..., MLA_NOPE:]
    if rope is not None:
        q_pe = apply_axial_rope(q_pe, *rope)
        kpe = apply_axial_rope(kpe, *rope)
    mq = jnp.concatenate([q_nope, q_pe], axis=-1)
    mk = jnp.concatenate([k_nope, jnp.broadcast_to(kpe[:, None], (B, MLA_HEADS, L, MLA_ROPE))], axis=-1)
    glow = glow.reshape(B, L, 2, GLA_GATE_RANK)
    logit = jnp.einsum('blzr,zrk->zblk', glow, gate_up) + gate_bias[:, None, None, :]
    logg = jax.nn.log_sigmoid(logit.astype(F32)) / GLA_GATE_NORM
    logg = logg.reshape(2, B, L, GLA_HEADS, GLA_DK).transpose(0, 1, 3, 2, 4)
    heads = lambda t, d: t.reshape(B, L, -1, d).transpose(0, 2, 1, 3)
    return (mq, mk, mv, heads(gq, GLA_DK), heads(gk, GLA_DK), heads(gv, GLA_DV), gg, logg[0], logg[1])

def even_merge(att, gla, gg, o_norm, w_out):
    B, _, L, _ = att.shape
    att = att.transpose(0, 2, 1, 3).reshape(B, L, MLA_HEADS * MLA_V)
    gla = rms_norm(gla.transpose(0, 2, 1, 3), o_norm) * jax.nn.silu(gg.reshape(B, L, GLA_HEADS, GLA_DV))
    return jnp.concatenate([att, gla.reshape(B, L, GLA_HEADS * GLA_DV)], axis=-1) @ w_out

def even_mixer(a_lat, a_ctx, w_in, q_norm, w_uq, kv_norm, w_ukv, gate_up, gate_bias, o_norm, w_out, rope, need_ctx):
    mq_l, mk_l, mv_l, gq_l, gk_l, gv_l, gg_l, lf_l, lb_l = even_project(
        a_lat @ w_in, q_norm, w_uq, kv_norm, w_ukv, gate_up, gate_bias, rope)
    mq_c, mk_c, mv_c, gq_c, gk_c, gv_c, gg_c, lf_c, lb_c = even_project(
        a_ctx @ w_in, q_norm, w_uq, kv_norm, w_ukv, gate_up, gate_bias, None)
    att_l = mla_attend(mq_l, jnp.concatenate([mk_l, mk_c], axis=2), jnp.concatenate([mv_l, mv_c], axis=2))
    B = a_lat.shape[0]
    s0 = jnp.zeros((B, GLA_HEADS, GLA_DK, GLA_DV), F32)
    gla_l, (o_cf, o_cb) = bidir_scan(gla_chunked, (gq_c, gk_c, gv_c, lf_c), (gq_c, gk_c, gv_c, lb_c),
                                     (gq_l, gk_l, gv_l, lf_l), (gq_l, gk_l, gv_l, lb_l), s0)
    o_lat = even_merge(att_l, gla_l, gg_l, o_norm, w_out)
    o_ctx = None
    if need_ctx:
        att_c = mla_attend(mq_c, mk_c, mv_c)
        o_ctx = even_merge(att_c, o_cf + jnp.flip(o_cb, axis=2), gg_c, o_norm, w_out)
    return o_lat, o_ctx

def short_conv(x, w):
    ch = x.shape[-1]
    y = lax.conv_general_dilated(x, w[:, None, :], window_strides=(1,),
                                 padding=[((GDN_CONV - 1) // 2, GDN_CONV // 2)],
                                 dimension_numbers=('NWC', 'WIO', 'NWC'), feature_group_count=ch)
    return jax.nn.silu(y)

def odd_project(a, w_in, conv_w, a_log, dt_bias):
    B, L, _ = a.shape
    qkv, g, a_in, b_in = split_cols(a @ w_in, ODD_SPLITS)
    q, k, v = split_cols(short_conv(qkv, conv_w), (GDN_HEADS * GDN_DK, GDN_HEADS * GDN_DK, GDN_HEADS * GDN_DV))
    heads = lambda t, d: t.reshape(B, L, GDN_HEADS, d).transpose(0, 2, 1, 3)
    q = l2norm(heads(q, GDN_DK))
    k = l2norm(heads(k, GDN_DK))
    v = heads(v, GDN_DV)
    a_in = a_in.reshape(B, L, 2, GDN_HEADS).astype(F32)
    log_a = -jnp.exp(a_log.astype(F32)) * jax.nn.softplus(a_in + dt_bias.astype(F32))
    beta = jax.nn.sigmoid(b_in.reshape(B, L, 2, GDN_HEADS).astype(F32))
    return q, k, v, g, log_a.transpose(2, 0, 3, 1), beta.transpose(2, 0, 3, 1)

def odd_merge(o, g, o_norm, w_out):
    B, _, L, _ = o.shape
    o = rms_norm(o.transpose(0, 2, 1, 3), o_norm) * jax.nn.silu(g.reshape(B, L, GDN_HEADS, GDN_DV))
    return o.reshape(B, L, GDN_WIDTH) @ w_out

def odd_mixer(a_lat, a_ctx, w_in, conv_w, a_log, dt_bias, o_norm, w_out, need_ctx):
    lq, lk, lv, lg, lla, lbe = odd_project(a_lat, w_in, conv_w, a_log, dt_bias)
    cq, ck, cv, cg, cla, cbe = odd_project(a_ctx, w_in, conv_w, a_log, dt_bias)
    B = a_lat.shape[0]
    s0 = jnp.zeros((B, GDN_HEADS, GDN_DK, GDN_DV), F32)
    o_l, (o_cf, o_cb) = bidir_scan(gdn_chunked, (cq, ck, cv, cla[0], cbe[0]), (cq, ck, cv, cla[1], cbe[1]),
                                   (lq, lk, lv, lla[0], lbe[0]), (lq, lk, lv, lla[1], lbe[1]), s0)
    o_lat = odd_merge(o_l, lg, o_norm, w_out)
    o_ctx = None
    if need_ctx:
        o_ctx = odd_merge(o_cf + jnp.flip(o_cb, axis=2), cg, o_norm, w_out)
    return o_lat, o_ctx

def sq_relu_mlp(h, w1, w2):
    return jnp.square(jax.nn.relu(h @ w1)) @ w2

def first_inputs(seed: int = 0) -> dict:
    key = jax.random.key(seed)
    ks = iter(jax.random.split(key, 40))
    nrm = lambda shape, scale: jax.random.normal(next(ks), shape, F32) * scale
    gain = lambda shape: 1.0 + 0.05 * jax.random.normal(next(ks), shape, F32)
    d = D_MODEL
    dt = jnp.exp(jax.random.uniform(next(ks), (N_ODD, 2, GDN_HEADS), F32, np.log(1e-3), np.log(1e-1)))
    return {
        "x": nrm((BATCH, SEQ, d), 1.0),
        "c": nrm((BATCH, d), 1.0),
        "ctx": nrm((BATCH, CTX_LEN, d), 1.0),
        "c_ctx": nrm((d,), 1.0),
        "ada_w": nrm((DEPTH, d, N_MOD * d), 0.5 * d ** -0.5),
        "ada_b": nrm((DEPTH, N_MOD * d), 0.02),
        "norm1_w": gain((DEPTH, d)),
        "norm2_w": gain((DEPTH, d)),
        "mlp_w1": nrm((DEPTH, d, D_FF), d ** -0.5),
        "mlp_w2": nrm((DEPTH, D_FF, d), D_FF ** -0.5),
        "even_w_in": nrm((N_EVEN, d, EVEN_IN), d ** -0.5),
        "mla_q_norm": gain((N_EVEN, MLA_Q_RANK)),
        "mla_w_uq": nrm((N_EVEN, MLA_Q_RANK, MLA_HEADS * MLA_QK), MLA_Q_RANK ** -0.5),
        "mla_kv_norm": gain((N_EVEN, MLA_KV_RANK)),
        "mla_w_ukv": nrm((N_EVEN, MLA_KV_RANK, MLA_HEADS * (MLA_NOPE + MLA_V)), MLA_KV_RANK ** -0.5),
        "gla_gate_up": nrm((N_EVEN, 2, GLA_GATE_RANK, GLA_HEADS * GLA_DK), GLA_GATE_RANK ** -0.5),
        "gla_gate_bias": nrm((N_EVEN, 2, GLA_HEADS * GLA_DK), 0.1),
        "gla_o_norm": gain((N_EVEN, GLA_DV)),
        "even_w_out": nrm((N_EVEN, MIX_WIDTH, d), MIX_WIDTH ** -0.5),
        "gdn_w_in": nrm((N_ODD, d, ODD_IN), d ** -0.5),
        "gdn_conv_w": nrm((N_ODD, GDN_CONV, GDN_QKV), GDN_CONV ** -0.5),
        "gdn_a_log": jnp.log(jax.random.uniform(next(ks), (N_ODD, 2, GDN_HEADS), F32, 1.0, 16.0)),
        "gdn_dt_bias": dt + jnp.log(-jnp.expm1(-dt)),
        "gdn_o_norm": gain((N_ODD, GDN_DV)),
        "gdn_w_out": nrm((N_ODD, GDN_WIDTH, d), GDN_WIDTH ** -0.5),
        "final_norm": gain((d,)),
    }

def first_block(x, c, ctx, c_ctx, ada_w, ada_b, norm1_w, norm2_w, mlp_w1, mlp_w2,
              even_w_in, mla_q_norm, mla_w_uq, mla_kv_norm, mla_w_ukv, gla_gate_up, gla_gate_bias,
              gla_o_norm, even_w_out, gdn_w_in, gdn_conv_w, gdn_a_log, gdn_dt_bias, gdn_o_norm,
              gdn_w_out, final_norm):
    rope = axial_rope_tables(x.shape[1])
    h_lat, h_ctx = x, ctx
    for layer in range(DEPTH):
        need_ctx = layer < DEPTH - 1
        ml = [m[:, None, :] for m in jnp.split(jax.nn.silu(c) @ ada_w[layer] + ada_b[layer], N_MOD, axis=-1)]
        mc = jnp.split(jax.nn.silu(c_ctx) @ ada_w[layer] + ada_b[layer], N_MOD, axis=-1)
        a_lat = modulate(rms_norm(h_lat, norm1_w[layer]), ml[0], ml[1])
        a_ctx = modulate(rms_norm(h_ctx, norm1_w[layer]), mc[0], mc[1])
        i = layer // 2
        if layer % 2 == 0:
            o_lat, o_ctx = even_mixer(a_lat, a_ctx, even_w_in[i], mla_q_norm[i], mla_w_uq[i], mla_kv_norm[i],
                                      mla_w_ukv[i], gla_gate_up[i], gla_gate_bias[i], gla_o_norm[i],
                                      even_w_out[i], rope, need_ctx)
        else:
            o_lat, o_ctx = odd_mixer(a_lat, a_ctx, gdn_w_in[i], gdn_conv_w[i], gdn_a_log[i], gdn_dt_bias[i],
                                     gdn_o_norm[i], gdn_w_out[i], need_ctx)
        h_lat = h_lat + ml[2] * o_lat
        h_lat = h_lat + ml[5] * sq_relu_mlp(modulate(rms_norm(h_lat, norm2_w[layer]), ml[3], ml[4]),
                                            mlp_w1[layer], mlp_w2[layer])
        if need_ctx:
            h_ctx = h_ctx + mc[2] * o_ctx
            h_ctx = h_ctx + mc[5] * sq_relu_mlp(modulate(rms_norm(h_ctx, norm2_w[layer]), mc[3], mc[4]),
                                                mlp_w1[layer], mlp_w2[layer])
    return rms_norm(h_lat, final_norm)


N_A_LAYERS = DEPTH // 2
N_B_LAYERS = DEPTH - N_A_LAYERS
HEAD_DIM = 64
MIX_WIDTH_2 = D_MODEL
MEM_HEADS = 4
MEM_WIDTH = MEM_HEADS * HEAD_DIM
N_MEM = 256
LRU_WIDTH = MIX_WIDTH_2 - MEM_WIDTH
LRU_BLOCKS = 6
LRU_BLOCK = LRU_WIDTH // LRU_BLOCKS
CONV_WIDTH = 4
LRU_C = 8.0
SWA_Q_HEADS = (MIX_WIDTH_2 - MEM_WIDTH) // HEAD_DIM
SWA_KV_HEADS = 4
SWA_GROUP = SWA_Q_HEADS // SWA_KV_HEADS
KV_WIDTH = SWA_KV_HEADS * HEAD_DIM
WINDOW = 128
BLOCK = 128
ROPE_DIM = HEAD_DIM // 4
ROPE_THETA_2 = 500000.0
D_FF_2 = -(-8 * D_MODEL // (3 * 256)) * 256
A_IN_WIDTH = 2 * LRU_WIDTH + MEM_WIDTH
B_IN_WIDTH = SWA_Q_HEADS * HEAD_DIM + MEM_WIDTH
NEG_INF = -1e30


def rms_norm_2(x, g):
    xf = x.astype(jnp.float32)
    y = xf * lax.rsqrt(jnp.mean(xf * xf, axis=-1, keepdims=True) + EPS)
    return (y * g.astype(jnp.float32)).astype(x.dtype)

def rope_tables(seq):
    inv_freq = 1.0 / (ROPE_THETA_2 ** (jnp.arange(0, ROPE_DIM, 2, dtype=jnp.float32) / ROPE_DIM))
    ang = jnp.arange(seq, dtype=jnp.float32)[:, None] * inv_freq[None, :]
    return jnp.cos(ang), jnp.sin(ang)

def apply_partial_rope(x, cos, sin):
    half = ROPE_DIM // 2
    xr = x[..., :ROPE_DIM].astype(jnp.float32)
    x1, x2 = xr[..., :half], xr[..., half:]
    c = cos[None, :, None, :]
    s = sin[None, :, None, :]
    rot = jnp.concatenate([x1 * c - x2 * s, x2 * c + x1 * s], axis=-1).astype(x.dtype)
    return jnp.concatenate([rot, x[..., ROPE_DIM:]], axis=-1)

def causal_depthwise_conv(x, w, b):
    c = x.shape[-1]
    y = lax.conv_general_dilated(
        x, w[:, None, :].astype(x.dtype), window_strides=(1,),
        padding=[(CONV_WIDTH - 1, 0)], dimension_numbers=("NWC", "WIO", "NWC"),
        feature_group_count=c)
    return y + b

def _linear_recurrence_combine(left, right):
    a1, b1 = left
    a2, b2 = right
    return a1 * a2, a2 * b1 + b2

def rg_lru(x, w_r, b_r, w_i, b_i, lam):
    bsz, seq, width = x.shape
    xb = x.reshape(bsz, seq, LRU_BLOCKS, LRU_BLOCK)
    r = jax.nn.sigmoid(jnp.einsum("bshi,hij->bshj", xb, w_r)
                       + b_r.reshape(LRU_BLOCKS, LRU_BLOCK)).reshape(bsz, seq, width)
    i = jax.nn.sigmoid(jnp.einsum("bshi,hij->bshj", xb, w_i)
                       + b_i.reshape(LRU_BLOCKS, LRU_BLOCK)).reshape(bsz, seq, width)
    log_a = LRU_C * r.astype(jnp.float32) * jax.nn.log_sigmoid(lam.astype(jnp.float32))
    a = jnp.exp(log_a)
    mult = jnp.sqrt(jnp.maximum(1.0 - jnp.exp(2.0 * log_a), 0.0))
    first = (jnp.arange(seq) == 0)[None, :, None]
    mult = jnp.where(first, 1.0, mult)
    u = mult * (i * x).astype(jnp.float32)
    _, h = lax.associative_scan(_linear_recurrence_combine, (a, u), axis=1)
    return h.astype(x.dtype)

def sliding_window_attention_with_sinks(q, k, v, sinks):
    bsz, seq = q.shape[0], q.shape[1]
    nb = seq // BLOCK
    qb = q.reshape(bsz, nb, BLOCK, SWA_KV_HEADS, SWA_GROUP, HEAD_DIM)

    def band(t):
        cur = t.reshape(bsz, nb, BLOCK, SWA_KV_HEADS, HEAD_DIM)
        prev = jnp.concatenate([jnp.zeros_like(cur[:, :1]), cur[:, :-1]], axis=1)
        return jnp.concatenate([prev, cur], axis=2)

    kb, vb = band(k), band(v)
    scores = jnp.einsum("bnqkgd,bnckd->bnkgqc", qb, kb).astype(jnp.float32) * (HEAD_DIM ** -0.5)
    qi = jnp.arange(BLOCK)[:, None] + BLOCK
    ci = jnp.arange(2 * BLOCK)[None, :]
    rel = qi - ci
    in_window = (rel >= 0) & (rel < WINDOW)
    has_prev = (jnp.arange(nb) > 0)[:, None, None] | (ci >= BLOCK)[None]
    mask = in_window[None] & has_prev
    scores = jnp.where(mask[None, :, None, None], scores, NEG_INF)
    sink = sinks.astype(jnp.float32).reshape(1, 1, SWA_KV_HEADS, SWA_GROUP, 1, 1)
    m = jnp.maximum(jnp.max(scores, axis=-1, keepdims=True), sink)
    e = jnp.exp(scores - m)
    probs = e / (jnp.sum(e, axis=-1, keepdims=True) + jnp.exp(sink - m))
    out = jnp.einsum("bnkgqc,bnckd->bnqkgd", probs.astype(v.dtype), vb)
    return out.reshape(bsz, seq, SWA_Q_HEADS * HEAD_DIM)

def memory_attention(q, mk, mv):
    bsz, seq = q.shape[0], q.shape[1]
    s = jnp.einsum("bshd,bmhd->bhsm", q, mk).astype(jnp.float32) * (HEAD_DIM ** -0.5)
    p = jax.nn.softmax(s, axis=-1).astype(mv.dtype)
    o = jnp.einsum("bhsm,bmhd->bshd", p, mv)
    return o.reshape(bsz, seq, MEM_WIDTH)

def swiglu_ffn(x, w_in, w_out):
    gu = x @ w_in
    g, u = gu[..., :D_FF_2], gu[..., D_FF_2:]
    return (jax.nn.silu(g) * u) @ w_out

def second_inputs(seed: int = 0) -> dict:
    key = jax.random.key(seed)
    ks = jax.random.split(key, 24)

    def nrm(k, shape, scale):
        return jax.random.normal(k, shape, dtype=jnp.float32) * scale

    def gain(k, shape):
        return 1.0 + 0.05 * jax.random.normal(k, shape, dtype=jnp.float32)

    u = jax.random.uniform(ks[14], (N_A_LAYERS, LRU_WIDTH), dtype=jnp.float32,
                           minval=0.81, maxval=0.998)
    a0 = jnp.sqrt(u)
    lru_lambda = jnp.log(a0) - jnp.log1p(-a0)
    return {
        "x": nrm(ks[0], (BATCH, SEQ, D_MODEL), 1.0),
        "mem": nrm(ks[1], (BATCH, N_MEM, D_MODEL), 1.0),
        "norm_mix_pre": gain(ks[2], (DEPTH, D_MODEL)),
        "norm_mix_post": gain(ks[3], (DEPTH, D_MODEL)),
        "norm_ffn_pre": gain(ks[4], (DEPTH, D_MODEL)),
        "norm_ffn_post": gain(ks[5], (DEPTH, D_MODEL)),
        "mem_norm": gain(ks[6], (D_MODEL,)),
        "w_mem_kv": nrm(ks[7], (DEPTH, D_MODEL, 2 * MEM_WIDTH), D_MODEL ** -0.5),
        "w_in_a": nrm(ks[8], (N_A_LAYERS, D_MODEL, A_IN_WIDTH), D_MODEL ** -0.5),
        "conv_w": nrm(ks[9], (N_A_LAYERS, CONV_WIDTH, LRU_WIDTH), CONV_WIDTH ** -0.5),
        "conv_b": nrm(ks[10], (N_A_LAYERS, LRU_WIDTH), 0.02),
        "w_gate_r": nrm(ks[11], (N_A_LAYERS, LRU_BLOCKS, LRU_BLOCK, LRU_BLOCK), LRU_BLOCK ** -0.5),
        "b_gate_r": nrm(ks[12], (N_A_LAYERS, LRU_WIDTH), 0.02),
        "w_gate_i": nrm(ks[13], (N_A_LAYERS, LRU_BLOCKS, LRU_BLOCK, LRU_BLOCK), LRU_BLOCK ** -0.5),
        "b_gate_i": nrm(ks[15], (N_A_LAYERS, LRU_WIDTH), 0.02),
        "lru_lambda": lru_lambda,
        "norm_kv": gain(ks[16], (D_MODEL,)),
        "w_kv_shared": nrm(ks[17], (D_MODEL, 2 * KV_WIDTH), D_MODEL ** -0.5),
        "w_in_b": nrm(ks[18], (N_B_LAYERS, D_MODEL, B_IN_WIDTH), D_MODEL ** -0.5),
        "sinks": nrm(ks[19], (N_B_LAYERS, SWA_Q_HEADS), 1.0),
        "w_out": nrm(ks[20], (DEPTH, MIX_WIDTH_2, D_MODEL), MIX_WIDTH_2 ** -0.5),
        "w_ffn_in": nrm(ks[21], (DEPTH, D_MODEL, 2 * D_FF_2), D_MODEL ** -0.5),
        "w_ffn_out": nrm(ks[22], (DEPTH, D_FF_2, D_MODEL), D_FF_2 ** -0.5),
    }

def second_block(x, mem, norm_mix_pre, norm_mix_post, norm_ffn_pre, norm_ffn_post, mem_norm,
              w_mem_kv, w_in_a, conv_w, conv_b, w_gate_r, b_gate_r, w_gate_i, b_gate_i,
              lru_lambda, norm_kv, w_kv_shared, w_in_b, sinks, w_out, w_ffn_in, w_ffn_out):
    bsz, seq = x.shape[0], x.shape[1]
    n_mem = mem.shape[1]
    cos, sin = rope_tables(seq)
    mem_n = rms_norm_2(mem, mem_norm)
    h = x
    shared_k = None
    shared_v = None
    for l in range(DEPTH):
        hn = rms_norm_2(h, norm_mix_pre[l])
        mkv = mem_n @ w_mem_kv[l]
        mk = mkv[..., :MEM_WIDTH].reshape(bsz, n_mem, MEM_HEADS, HEAD_DIM)
        mv = mkv[..., MEM_WIDTH:].reshape(bsz, n_mem, MEM_HEADS, HEAD_DIM)
        if l < N_A_LAYERS:
            a = l
            proj = hn @ w_in_a[a]
            xr = proj[..., :LRU_WIDTH]
            gate = proj[..., LRU_WIDTH:2 * LRU_WIDTH]
            mq = proj[..., 2 * LRU_WIDTH:].reshape(bsz, seq, MEM_HEADS, HEAD_DIM)
            xr = causal_depthwise_conv(xr, conv_w[a], conv_b[a])
            y = rg_lru(xr, w_gate_r[a], b_gate_r[a], w_gate_i[a], b_gate_i[a], lru_lambda[a])
            y = y * jax.nn.gelu(gate)
        else:
            b = l - N_A_LAYERS
            proj = hn @ w_in_b[b]
            q = proj[..., :SWA_Q_HEADS * HEAD_DIM].reshape(bsz, seq, SWA_Q_HEADS, HEAD_DIM)
            mq = proj[..., SWA_Q_HEADS * HEAD_DIM:].reshape(bsz, seq, MEM_HEADS, HEAD_DIM)
            q = apply_partial_rope(q, cos, sin)
            y = sliding_window_attention_with_sinks(q, shared_k, shared_v, sinks[b])
        m_out = memory_attention(mq, mk, mv)
        mixed = jnp.concatenate([y, m_out], axis=-1) @ w_out[l]
        h = h + rms_norm_2(mixed, norm_mix_post[l])
        f = swiglu_ffn(rms_norm_2(h, norm_ffn_pre[l]), w_ffn_in[l], w_ffn_out[l])
        h = h + rms_norm_2(f, norm_ffn_post[l])
        if l == N_A_LAYERS - 1:
            kv = rms_norm_2(h, norm_kv) @ w_kv_shared
            shared_k = apply_partial_rope(
                kv[..., :KV_WIDTH].reshape(bsz, seq, SWA_KV_HEADS, HEAD_DIM), cos, sin)
            shared_v = kv[..., KV_WIDTH:].reshape(bsz, seq, SWA_KV_HEADS, HEAD_DIM)
    return h


def setup_inputs(seed=0):
    out = dict(first_inputs(seed))
    for name, value in second_inputs(seed + 1).items():
        if name != "x":
            out[name + "_2"] = value
    return out


def reference(
    x, c, ctx, c_ctx, ada_w, ada_b, norm1_w, norm2_w, mlp_w1, mlp_w2, even_w_in, mla_q_norm,
    mla_w_uq, mla_kv_norm, mla_w_ukv, gla_gate_up, gla_gate_bias, gla_o_norm, even_w_out,
    gdn_w_in, gdn_conv_w, gdn_a_log, gdn_dt_bias, gdn_o_norm, gdn_w_out, final_norm, mem_2,
    norm_mix_pre_2, norm_mix_post_2, norm_ffn_pre_2, norm_ffn_post_2, mem_norm_2, w_mem_kv_2,
    w_in_a_2, conv_w_2, conv_b_2, w_gate_r_2, b_gate_r_2, w_gate_i_2, b_gate_i_2, lru_lambda_2,
    norm_kv_2, w_kv_shared_2, w_in_b_2, sinks_2, w_out_2, w_ffn_in_2, w_ffn_out_2,
):
    x = first_block(
        x, c, ctx, c_ctx, ada_w, ada_b, norm1_w, norm2_w, mlp_w1, mlp_w2, even_w_in, mla_q_norm,
        mla_w_uq, mla_kv_norm, mla_w_ukv, gla_gate_up, gla_gate_bias, gla_o_norm, even_w_out,
        gdn_w_in, gdn_conv_w, gdn_a_log, gdn_dt_bias, gdn_o_norm, gdn_w_out, final_norm,
    )
    return second_block(
        x, mem_2, norm_mix_pre_2, norm_mix_post_2, norm_ffn_pre_2, norm_ffn_post_2, mem_norm_2,
        w_mem_kv_2, w_in_a_2, conv_w_2, conv_b_2, w_gate_r_2, b_gate_r_2, w_gate_i_2,
        b_gate_i_2, lru_lambda_2, norm_kv_2, w_kv_shared_2, w_in_b_2, sinks_2, w_out_2,
        w_ffn_in_2, w_ffn_out_2,
    )


_drawn_inputs = setup_inputs


def setup_inputs(seed=0):
    import zlib

    import numpy as np

    out = dict(_drawn_inputs(seed))
    spreads = {}
    factors = {'mla_q_norm': 8.0,
     'mla_kv_norm': 6.1,
     'gla_gate_bias': 5.291,
     'gla_o_norm': 4.798,
     'gdn_o_norm': 3.016,
     'mem_norm_2': 4.318,
     'b_gate_r_2': 42.192,
     'b_gate_i_2': 8.0,
     'sinks_2': 11.147,
     'norm_kv_2': 8.0}
    for name, (base, spread) in spreads.items():
        noise = np.random.default_rng([zlib.crc32(name.encode()), seed]).standard_normal(out[name].shape)
        drawn = base * np.exp(spread * noise) if base else spread * noise
        out[name] = jnp.asarray(drawn.astype(out[name].dtype))
    for name, factor in factors.items():
        out[name] = (out[name] * factor).astype(out[name].dtype)
    return out
```

```python
import numpy as np
import concourse.bass as bass
from concourse import mybir
from contextlib import ExitStack

F32 = mybir.dt.float32
ALU = mybir.AluOpType
ACT = mybir.ActivationFunctionType
AX = mybir.AxisListType

P = 128
D = 1024
KB = D // P
LAT = 256
CTX = 256
T = LAT + CTX
TB = T // P
NMOD = 6
FF = 4 * D
FB = FF // P
EPS = 1e-6

MH, NOPE, ROPE, MV = 8, 64, 32, 64
MQK = NOPE + ROPE
QR, KVR = 3 * D // 8, D // 4
QB, KVB = QR // P, KVR // P
GH, GDK, GDV, GRANK = 4, 64, 128, 16
GFB = GH * GDK // P
C = 64
NCH = T // C
E_KV, E_KPE = QR, QR + KVR
E_GQ = E_KPE + ROPE
E_GK = E_GQ + GH * GDK
E_GV = E_GK + GH * GDK
E_GG = E_GV + GH * GDV
E_GLOW = E_GG + GH * GDV
EVEN_IN = E_GLOW + 2 * GRANK

NH, NDK, NDV = 8, 64, 128
QKB = NH * NDK // P
VB = NH * NDV // P
O_G = 2 * NH * NDK + NH * NDV
O_AB = O_G + NH * NDV
ODD_IN = O_AB + 4 * NH
NPAIR = 2

HD = 64
LW = 768
LB = LW // P
MEMH = 4
NMEM = 256
SQH, SKH = 12, 4
FF2 = 2816
F2B = FF2 // P
A_IN = 2 * LW + MEMH * HD
B_IN = SQH * HD + MEMH * HD

SLOTS = 4
SLOT = KB * 288
UNITS = 12
ARENA = 24576


class Signal:

    def __init__(self, nc, ctx, name):
        self.sem = ctx.enter_context(nc.semaphore(name))
        self.total = 0

    def take(self, n=1):
        base = self.total
        self.total += n
        return base



def constant_tables():
    t = {}
    i = np.arange(P)
    t["ident"] = np.eye(P)
    t["ones"] = np.ones((P, P))
    same = (i[:, None] // C) == (i[None, :] // C)
    t["ones_half"] = same.astype(float)
    t["upto"] = np.stack([same & (i[:, None] <= i[None, :]), same & (i[:, None] >= i[None, :])], 1).reshape(P, -1)
    r, c = (i % C)[:, None], np.arange(C)[None, :]
    t["strict"] = np.stack([c < r, c > r], 1).reshape(P, -1)
    lev = []
    for s in (2, 4, 8, 16, 32):
        pair, jh, ih = (r // (2 * s)) == (c // (2 * s)), (r // s) % 2, (c // s) % 2
        lev.append(np.stack([pair & (jh == 0) & (ih == 1), pair & (jh == 1) & (ih == 0)], 1))
    t["levels"] = np.stack(lev, 2).reshape(P, -1)
    pair = (r // 2) == (c // 2)
    t["pairs"] = np.stack([pair & (c < r), pair & (c > r)], 1).reshape(P, -1)
    t["eye64"] = (r == c).astype(float)
    t["upto64"] = np.stack([r <= c, r >= c], 1).reshape(P, -1)
    nf = ROPE // 4
    inv = 10000.0 ** (-np.arange(0, ROPE // 2, 2, dtype=np.float32) / np.float32(ROPE // 2))
    tok = np.arange(LAT)
    ang = np.stack([(tok // 64).astype(np.float32)[None, :] * inv[:, None],
                    (tok % 64).astype(np.float32)[None, :] * inv[:, None]], 0)
    cos = np.broadcast_to(np.cos(ang)[:, None], (2, 2, nf, LAT)).reshape(ROPE, LAT)
    sin = np.broadcast_to(np.sin(ang)[:, None], (2, 2, nf, LAT)).reshape(ROPE, LAT)
    rot = np.zeros((ROPE, ROPE))
    for a in range(2):
        for f in range(nf):
            x1, x2 = a * 2 * nf + f, a * 2 * nf + nf + f
            rot[x2, x1], rot[x1, x2] = -1.0, 1.0
    m = np.zeros((P, 2 * LAT + ROPE))
    m[64:96] = np.concatenate([cos, sin, rot], 1)
    t["mla_rope"] = m
    half = HD // 8
    inv = (1.0 / (np.float32(500000.0) ** (np.arange(0, 2 * half, 2, dtype=np.float32) / np.float32(2 * half)))).astype(np.float32)
    ang = tok.astype(np.float32)[None, :] * inv[:, None]
    cos, sin, rot = np.ones((P, LAT)), np.zeros((P, LAT)), np.zeros((P, P))
    for h in (0, HD):
        for b in (0, half):
            cos[h + b:h + b + half], sin[h + b:h + b + half] = np.cos(ang), np.sin(ang)
        for f in range(half):
            rot[h + half + f, h + f], rot[h + f, h + half + f] = -1.0, 1.0
    t["swa_rope"] = np.concatenate([cos, sin, rot], 1)
    q, k = i[:, None], i[None, :]
    t["window"] = np.concatenate([np.where(k > q, 0.0, -1e30), np.where(k <= q, 0.0, -1e30)], 1)
    return {n: np.ascontiguousarray(a, dtype=np.float32) for n, a in t.items()}


TABLES = constant_tables()

VECTORS = [("c", 2 * KB), ("ada_b", 2 * NMOD * KB), ("norm1_w", 2 * KB), ("norm2_w", 2 * KB), ("final_norm", KB),
           ("mla_q_norm", QB), ("mla_kv_norm", KVB), ("gla_o_norm", 1), ("gdn_conv_w", 3 * 16), ("gdn_o_norm", 1),
           ("norm_mix_pre_2", 2 * KB), ("norm_mix_post_2", 2 * KB), ("norm_ffn_pre_2", 2 * KB),
           ("norm_ffn_post_2", 2 * KB), ("mem_norm_2", KB), ("conv_w_2", 4 * LB), ("conv_b_2", LB),
           ("b_gate_r_2", LB), ("b_gate_i_2", LB), ("lru_lambda_2", LB), ("norm_kv_2", KB),
           ("gdn_a_log", 16), ("gdn_dt_bias", 16), ("sinks_2", SQH), ("eps", 1)]


def columns(sizes):
    at, out = 0, {}
    for name, n in sizes:
        out[name] = (at, n)
        at += n
    return out, at


VCOL, NVEC = columns(VECTORS)
TCOL, NTAB = columns([(n, a.shape[1]) for n, a in TABLES.items()])


def two_block_kernel(nc, d, out):
    ctx = ExitStack()
    with ctx:
        def sb(name, shape):
            return ctx.enter_context(nc.sbuf_tensor(name, shape, F32))

        def sig(name):
            return Signal(nc, ctx, name)

        tab = sb("tables", [P, NTAB])
        vec = sb("vectors", [P, NVEC])
        glg = sb("gla_gate", [GRANK + 1, 2, GH * GDK])
        ring = sb("ring", [P, SLOTS, SLOT])
        h = sb("h", [P, KB, T])
        a = sb("a", [P, KB, T])
        mix = sb("mix", [P, KB, T])
        mod = sb("mod", [P, 2, NMOD * KB, 2])
        gain = sb("gain", [P, 2, 2, KB, 2])
        silu_c = sb("silu_c", [P, KB, 2])
        root = sb("root", [P, T])
        rstd = sb("rstd", [P, T])
        tmp = sb("tmp", [P, 2, T])
        arena = sb("arena", [P, ARENA])
        bank = [ctx.enter_context(nc.psum_tensor(f"bank{i}", [P, 512], F32)) for i in range(8)]
        BSUM, BADA = bank[4], bank[5]

        def table(name):
            at, n = TCOL[name]
            return tab[:, at:at + n]

        def vector(name):
            at, n = VCOL[name]
            return vec[:, at:at + n]

        ident, ones, ones_half = table("ident"), table("ones"), table("ones_half")
        upto = table("upto").rearrange("p (z i) -> p z i", z=2)

        class Carve:

            def __init__(self):
                self.at = 0

            def __call__(self, *shape):
                n = int(np.prod(shape))
                v = arena[:, self.at:self.at + n]
                self.at += n
                assert self.at <= ARENA, self.at
                if len(shape) == 1:
                    return v
                names = "abcdef"[:len(shape)]
                return v.rearrange(f"p ({' '.join(names)}) -> p {' '.join(names)}",
                                   **{x: s for x, s in zip(names[1:], shape[1:])})

        loaded = sig("loaded")
        here = [sig(f"weights_here{s}") for s in range(SLOTS)]
        block_done = sig("block_done")
        evac_act, evac_dve = sig("evac_act"), sig("evac_dve")
        sq_act, sq_dve = sig("squares_act"), sig("squares_dve")
        sums_done, root_done, rstd_done, normed = sig("sums_done"), sig("root_done"), sig("rstd_done"), sig("normed")
        ada_mm, gains_done, silu_done = sig("ada_mm"), sig("gains_done"), sig("silu_done")
        chain = sig("dve_chain")

        def link(eng, ins):
            chain.total += 1
            ins.then_inc(chain.sem, 1)
            eng.wait_ge(chain.sem, chain.total)

        class Tiles:
            count = 0
            every = []

            def __init__(self, n, source, kb, cols, loop=False):
                self.n, self.source, self.kb, self.cols, self.loop = n, source, kb, cols, loop
                self.first = Tiles.count
                Tiles.count += n
                Tiles.every.append(self)
                self.source_in = lambda i, t: self.source(i * SLOTS + t)
                assert kb * cols <= SLOT

            def view(self, t):
                s = (self.first + t) % SLOTS
                return ring[:, s, 0:self.kb * self.cols].rearrange("p (k c) -> p k c", k=self.kb)

            def wait(self, pe, t, loops=0):
                at = self.first + t
                pe.wait_ge(here[at % SLOTS].sem, 16 * (at // SLOTS + 1) + 16 * loops)

            def done(self, t, block=UNITS - 1):
                return UNITS * (self.first + t) + block + 1

        def cols_of(w, c0, n, r0=0, kb=KB):
            return w[r0:r0 + kb * P, c0:c0 + n].rearrange("(k p) c -> p k c", p=P)

        def dyn(w, c0, n, kb=KB):
            return w[0:kb * P, bass.ds(c0, n)].rearrange("(k p) c -> p k c", p=P)

        class Linear:
            last = None

            def __init__(self, evac, n, banks=2, first=0):
                self.before, self.evac, self.base, self.banks, self.first = Linear.last, evac, evac.take(n), banks, first
                Linear.last = (evac, evac.total)

            def bank(self, n):
                return bank[self.first + n % self.banks]

            def free(self, pe, n, past=None):
                if n == 0 and past is None and self.before is not None:
                    pe.wait_ge(self.before[0].sem, self.before[1])
                if past is not None:
                    pe.wait_ge(self.evac.sem, self.base + n - self.banks + 1 + past)
                elif n >= self.banks:
                    pe.wait_ge(self.evac.sem, self.base + n - self.banks + 1)

        def product(pe, dst, lhs, rhs, nk, start=True, stop=True, before=None):
            for k in range(nk):
                if before is not None:
                    before(k)
                last = pe.matmul(dst, lhs(k), rhs(k), start=start and k == 0, stop=stop and k == nk - 1)
            return last

        class Norm:

            def __init__(self, src, sq, nk, width, features):
                self.src, self.sq, self.nk, self.w, self.n = src, sq, nk, width, features
                self.sa, self.sd = sq_act.take((nk + 1) // 2), sq_dve.take(nk // 2)
                self.sum, self.root, self.rstd = sums_done.take(), root_done.take(), rstd_done.take()

            def act_squares(self, act, ready=None):
                for k in range(0, self.nk, 2):
                    if ready is not None:
                        ready(act, k)
                    nc.scalar.activation(self.sq(k), self.src(k), ACT.Square).then_inc(sq_act.sem, 1)

            def dve_squares(self, dve, ready=None):
                for k in range(1, self.nk, 2):
                    if ready is not None:
                        ready(dve, k)
                    nc.vector.tensor_tensor(self.sq(k), self.src(k), self.src(k), ALU.mult).then_inc(sq_dve.sem, 1)

            def pe_sums(self, pe):
                for k in range(self.nk):
                    if k % 2 == 0:
                        pe.wait_ge(sq_act.sem, self.sa + k // 2 + 1)
                    else:
                        pe.wait_ge(sq_dve.sem, self.sd + k // 2 + 1)
                    last = pe.matmul(BSUM[:, 0:self.w], ones, self.sq(k), start=k == 0, stop=k == self.nk - 1)
                last.then_inc(sums_done.sem, 1)

            def act_root(self, act):
                act.wait_ge(sums_done.sem, self.sum + 1)
                nc.scalar.activation(root[:, 0:self.w], BSUM[:, 0:self.w], ACT.Ln, scale=1.0 / self.n,
                                     bias=eps_col).then_inc(root_done.sem, 1)
                act.wait_ge(root_done.sem, self.root + 1)
                nc.scalar.activation(rstd[:, 0:self.w], root[:, 0:self.w], ACT.Exp, scale=-0.5)\
                    .then_inc(rstd_done.sem, 1)

            def wait(self, eng):
                eng.wait_ge(rstd_done.sem, self.rstd + 1)

        scaled = sig("scaled")
        eps_col = vec[:, NVEC - 1:NVEC]

        class Modulated:

            def __init__(self, layer, which, width):
                self.l, self.which, self.w = layer, which, width
                self.parts = 2 if width == T else 1
                self.norm = Norm(lambda k: h[:, k, 0:width], lambda k: a[:, k, 0:width], KB, width, D)
                self.scaled, self.normed = scaled.take(KB), normed.take(KB)

            def dve(self, dve):
                dve.wait_ge(gains_done.sem, 2 * self.l + self.which + 1)
                self.norm.wait(dve)
                for k in range(KB):
                    for z in range(self.parts):
                        s = slice(z * LAT, (z + 1) * LAT)
                        ins = nc.vector.scalar_tensor_tensor(
                            out=a[:, k, s], in0=h[:, k, s], scalar=gain[:, self.l, self.which, k, z:z + 1],
                            in1=rstd[:, s], op0=ALU.mult, op1=ALU.mult)
                    ins.then_inc(scaled.sem, 1)

            def act(self, act):
                for k in range(KB):
                    act.wait_ge(scaled.sem, self.scaled + k + 1)
                    for z in range(self.parts):
                        s = slice(z * LAT, (z + 1) * LAT)
                        j = 3 * self.which * KB + k
                        ins = nc.scalar.activation(a[:, k, s], a[:, k, s], ACT.Identity, bias=mod[:, self.l, j, z:z + 1])
                    ins.then_inc(normed.sem, 1)

            def ready(self, pe, k):
                pe.wait_ge(normed.sem, self.normed + k + 1)

        ADA_A = 2 * KB
        ada_a_tiles = Tiles(ADA_A // 2, lambda t: cols_of(d["ada_w"][0], 256 * t, 256), KB, 256)

        def act_silu_c(act):
            act.wait_ge(loaded.sem, 16 * SMALL)
            nc.scalar.activation(silu_c[:, :, :].rearrange("p k z -> p (k z)"), vector("c"), ACT.Silu)\
                .then_inc(silu_done.sem, 1)

        ada_row = sb("ada_row", [2, 2, 256])
        ada_turned = sig("ada_turned")

        class Ada:

            def __init__(self, tiles, layer, j0, n):
                self.tiles, self.layer, self.j0, self.n = tiles, layer, j0, n
                self.lin = Linear(evac_act, n // 2, first=6)
                self.turned = ada_turned.take(n // 2)

            def pe_rows(self, pe, t):
                if t == 0:
                    pe.wait_ge(silu_done.sem, 1)
                self.tiles.wait(pe, t)
                self.lin.free(pe, t)
                w = self.tiles.view(t)
                product(pe, self.lin.bank(t)[0:2, 0:256], lambda k: silu_c[:, k, :], lambda k: w[:, k, :], KB)\
                    .then_inc(block_done.sem, UNITS)

            def pe_turn(self, pe, t):
                pe.wait_ge(evac_act.sem, self.lin.base + t + 1)
                for b in range(2):
                    j = self.j0 + 2 * t + b
                    ins = pe.transpose(BADA[:, 2 * j:2 * j + 2], ada_row[:, t % 2, b * P:(b + 1) * P], ident[0:2, 0:2])
                ins.then_inc(ada_turned.sem, 1)

            def pe(self, pe):
                for t in range(self.n // 2 + 1):
                    if t < self.n // 2:
                        self.pe_rows(pe, t)
                    if t >= 1:
                        self.pe_turn(pe, t - 1)

            def act(self, act):
                for t in range(self.n // 2):
                    act.wait_ge(block_done.sem, self.tiles.done(t))
                    if t >= 2:
                        act.wait_ge(ada_turned.sem, self.turned + t - 1)
                    nc.scalar.activation(ada_row[:, t % 2, :], self.lin.bank(t)[0:2, 0:256], ACT.Copy)\
                        .then_inc(evac_act.sem, 1)

            def dve(self, dve):
                dve_ada(dve, self.turned + self.n // 2, self.layer, self.j0, self.n)

        def dve_ada(dve, turned, layer, j0, n):
            dve.wait_ge(ada_turned.sem, turned)
            bias = vector("ada_b").rearrange("p (l j) -> p l j", l=2)[:, layer, j0:j0 + n]
            link(dve, nc.vector.tensor_tensor(
                mod[:, layer, j0:j0 + n, :], BADA[:, 2 * j0:2 * (j0 + n)].rearrange("p (j z) -> p j z", z=2),
                bias.rearrange("p (j o) -> p j o", o=1).broadcast_to((P, n, 2)), ALU.add))
            for which, name in ((0, "norm1_w"), (1, "norm2_w")):
                j = (3 * which + 1) * KB
                if not j0 <= j < j0 + n:
                    continue
                w = vector(name).rearrange("p (l k o) -> p l k o", l=2, o=1)[:, layer].broadcast_to((P, KB, 2))
                nc.vector.scalar_tensor_tensor(out=gain[:, layer, which], in0=mod[:, layer, j:j + KB, :], scalar=1.0,
                                               in1=w, op0=ALU.add, op1=ALU.mult).then_inc(gains_done.sem, 1)

        ada_a = Ada(ada_a_tiles, 0, 0, ADA_A)

        n1 = Modulated(0, 0, T)
        cv = Carve()
        cq, ckv, kpe = cv(QB, T), cv(KVB, T), cv(T)
        gq, gk, gg = cv(GFB, T), cv(GFB, T), cv(GH, T)
        glow = cv(2, T)
        gv = cv(TB, GH * GDV)
        even_at = cv.at
        glow_ones = sig("glow_ones")
        w_even = d["even_w_in"][0]
        even_cols = [(0, 256), (256, 256), (512, 160), (E_GQ, 256), (E_GK, 256), (E_GV, 256), (E_GV + 256, 256),
                     (E_GG, 256), (E_GG + 256, 288)]
        even_tiles = [Tiles(1, lambda t, c0=c0, n=n: cols_of(w_even, c0, n), KB, n) for c0, n in even_cols]
        even_blocks = [(0, 0, P, (cq, 0)), (0, P, P, (cq, 1)), (1, 0, P, (cq, 2)), (1, P, P, (ckv, 0)),
                       (2, 0, P, (ckv, 1)), (2, P, ROPE, (kpe, None)), (3, 0, P, (gq, 0)), (3, P, P, (gq, 1)),
                       (4, 0, P, (gk, 0)), (4, P, P, (gk, 1))]
        even_blocks += [(5 + half, 0, 256, (gv, tb)) for half in range(2) for tb in range(TB)]
        even_blocks += [(7, 0, P, (gg, 0)), (7, P, P, (gg, 1)), (8, 0, P, (gg, 2)), (8, P, P, (gg, 3)),
                        (8, 256, GRANK, (glow, 0)), (8, 256 + GRANK, GRANK, (glow, 1))]
        even_lin = Linear(evac_act, len(even_blocks))

        def even_sync(n):
            t = even_blocks[n][0]
            b = sum(x[0] == t for x in even_blocks[:n])
            return t, b, n + 1 == len(even_blocks) or even_blocks[n + 1][0] != t

        def pe_even_in(pe):
            for n, (t, c0, m, (dst, i)) in enumerate(even_blocks):
                t, b, last_of_tile = even_sync(n)
                w = even_tiles[t].view(0)
                if b == 0:
                    even_tiles[t].wait(pe, 0)
                even_lin.free(pe, n)
                o = even_lin.bank(n)
                before = (lambda k: n1.ready(pe, k)) if n == 0 else None
                if dst is gv:
                    ins = product(pe, o[:, 0:256], lambda k: a[:, k, i * P:(i + 1) * P], lambda k: w[:, k, 0:256], KB)
                else:
                    rows = slice(64, 64 + ROPE) if dst is kpe else slice(0, m)
                    ins = product(pe, o[rows, :], lambda k: w[:, k, c0:c0 + m], lambda k: a[:, k, :], KB, before=before)
                ins.then_inc(block_done.sem, UNITS - b if last_of_tile else 1)

        def act_even_in(act):
            for n, (t, c0, m, (dst, i)) in enumerate(even_blocks):
                t, b, last_of_tile = even_sync(n)
                act.wait_ge(block_done.sem, even_tiles[t].done(0, UNITS - 1 if last_of_tile else b))
                o = even_lin.bank(n)
                func = ACT.Copy
                if dst is gv:
                    half = t - 5
                    o, to = o[:, 0:256], gv[:, i, half * 256:(half + 1) * 256]
                elif dst is kpe:
                    o, to = o[64:64 + ROPE, :], kpe[64:64 + ROPE, :]
                elif dst is glow:
                    if i == 0:
                        act.wait_ge(glow_ones.sem, 1)
                    o, to = o[0:m, :], glow[0:m, i, :]
                else:
                    to = dst[:, i, :]
                    func = ACT.Silu if dst is gg else ACT.Copy
                nc.scalar.activation(to, o if o.shape[0] != P or dst is gv else o[:, :], func).then_inc(evac_act.sem, 1)

        def pool_glow_ones(pool):
            nc.gpsimd.memset(glow[0:GRANK + 1, :, :], 1.0).then_inc(glow_ones.sem, 1)

        copied = sig("kv_copied")
        ranked = sig("ranked")
        cqn, ckvn = mix[:, 0:QB, :], mix[:, QB:QB + KVB, :]
        swing = cv(2 * T)
        norm_q = Norm(lambda k: cq[:, k, :], lambda k: mix[:, QB + KVB + k, :], QB, T, QR)
        norm_kv = Norm(lambda k: ckv[:, k, :], lambda k: swing[:, k * T:(k + 1) * T], KVB, T, KVR)
        uq_tiles = Tiles(1, lambda t: cols_of(d["mla_w_uq"][0], 0, MH * MQK, kb=QB), QB, MH * MQK)
        ukv_tiles = Tiles(1, lambda t: cols_of(d["mla_w_ukv"][0], 0, MH * (NOPE + MV), kb=KVB), KVB, MH * (NOPE + MV))
        qT, kT, vt = cv(MH, T), cv(MH, T), cv(TB, MH * MV)
        mla_end = cv.at
        q_lin = Linear(evac_act, MH)
        kv_lin = Linear(evac_act, MH + TB)
        rope_mm, rope_done, rope_tmp = sig("rope_mm"), sig("rope_done"), sig("rope_tmp")
        rope_cos = table("mla_rope")[64:96, 0:LAT]
        rope_sin = table("mla_rope")[64:96, LAT:2 * LAT]
        rope_rot = table("mla_rope")[64:96, 2 * LAT:2 * LAT + ROPE]

        def dve_ranks(dve):
            r = 0
            for norm, src, dst, nk, name in ((norm_q, cq, cqn, QB, "mla_q_norm"), (norm_kv, ckv, ckvn, KVB, "mla_kv_norm")):
                norm.wait(dve)
                for k in range(nk):
                    nc.vector.scalar_tensor_tensor(out=dst[:, k, :], in0=src[:, k, :], scalar=vector(name)[:, k:k + 1],
                                                   in1=rstd[:, :], op0=ALU.mult, op1=ALU.mult).then_inc(ranked.sem, 1)
                if norm is norm_q:
                    norm_kv.dve_squares(dve)

        def pe_mla_project(pe):
            uq_tiles.wait(pe, 0)
            w = uq_tiles.view(0)
            for n in range(MH):
                if n == 0:
                    pe.wait_ge(ranked.sem, QB)
                q_lin.free(pe, n)
                product(pe, q_lin.bank(n)[0:MQK, :], lambda k: w[:, k, n * MQK:(n + 1) * MQK], lambda k: cqn[:, k, :], QB)\
                    .then_inc(block_done.sem, 1 if n + 1 < MH else UNITS - MH + 1)
            pe.wait_ge(ranked.sem, QB + KVB)
            ukv_tiles.wait(pe, 0)
            w = ukv_tiles.view(0)
            for n in range(MH):
                kv_lin.free(pe, n)
                product(pe, kv_lin.bank(n)[0:NOPE, :], lambda k: w[:, k, n * P:n * P + NOPE], lambda k: ckvn[:, k, :], KVB)\
                    .then_inc(block_done.sem, 1)
            heads = [w[:, k, :].rearrange("p (h c) -> p h c", h=MH)[:, :, NOPE:] for k in range(KVB)]
            for tb in range(TB):
                kv_lin.free(pe, MH + tb)
                product(pe, kv_lin.bank(MH + tb)[:, :], lambda k: ckvn[:, k, tb * P:(tb + 1) * P], lambda k: heads[k], KVB)\
                    .then_inc(block_done.sem, 1)
            for g in range(5):
                if g == 0:
                    pe.wait_ge(evac_act.sem, q_lin.base + MH)
                rhs = qT[64:96, 2 * g:2 * g + 2, 0:LAT] if g < 4 else kpe[64:96, 0:LAT]
                dst = rope_bank(g)
                dst = dst.rearrange("p (h t) -> p h t", h=2) if g < 4 else dst
                pe.matmul(dst, rope_rot, rhs, start=True, stop=True).then_inc(rope_mm.sem, 1)

        def rope_bank(g):
            return bank[(2, 3, 6, 7, 5)[g]][64:96, 0:2 * LAT if g < 4 else LAT]

        def act_mla_project(act):
            for n in range(MH):
                act.wait_ge(block_done.sem, uq_tiles.done(0, n if n + 1 < MH else UNITS - 1))
                nc.scalar.activation(qT[0:MQK, n, :], q_lin.bank(n)[0:MQK, :], ACT.Copy).then_inc(evac_act.sem, 1)
            for n in range(MH + TB):
                act.wait_ge(block_done.sem, ukv_tiles.done(0, n))
                src, dst = (kv_lin.bank(n)[0:NOPE, :], kT[0:NOPE, n, :]) if n < MH else (kv_lin.bank(n)[:, :], vt[:, n - MH, :])
                nc.scalar.activation(dst, src, ACT.Copy).then_inc(evac_act.sem, 1)

        def dve_rope(dve):
            for g in (4, 0, 1, 2, 3):
                dve.wait_ge(rope_mm.sem, g + 1)
                n = 2 if g < 4 else 1
                x = qT[64:96, 2 * g:2 * g + 2, 0:LAT] if g < 4 else kpe[64:96, 0:LAT].rearrange("p (h t) -> p h t", h=1)
                part = rope_bank(g).rearrange("p (h t) -> p h t", h=n)
                s = swing[64:96, 0:n * LAT].rearrange("p (h t) -> p h t", h=n)
                cos = rope_cos.rearrange("p (o t) -> p o t", o=1).broadcast_to((ROPE, n, LAT))
                sin = rope_sin.rearrange("p (o t) -> p o t", o=1).broadcast_to((ROPE, n, LAT))
                nc.vector.tensor_tensor(s, part, sin, ALU.mult)
                link(dve, nc.vector.tensor_tensor(x, x, cos, ALU.mult))
                ins = nc.vector.tensor_tensor(x, x, s, ALU.add)
                ins.then_inc(rope_done.sem, 1)
                dve.wait_ge(rope_done.sem, (1, 2, 3, 4, 5)[(4, 0, 1, 2, 3).index(g)])

        def pool_shared_key(pool):
            pool.wait_ge(rope_done.sem, 1)
            nc.gpsimd.tensor_copy(kT[64:96, :, :], kpe[64:96, :].rearrange("p (o t) -> p o t", o=1)
                                  .broadcast_to((ROPE, MH, T))).then_inc(copied.sem, 1)

        att_scores, att_max, att_exp = sig("att_scores"), sig("att_max"), sig("att_exp")
        att_probs, att_turned, att_probsT = sig("att_probs"), sig("att_turned"), sig("att_probsT")
        att_mixed, att_out = sig("att_mixed"), sig("att_out")
        att_small = sb("att_small", [P, 2, 8])

        class Attention:

            def __init__(self, units, scale, room):
                self.units, self.scale, self.p, self.pt = units, scale, room[0:2], room[2:4]
                n = len(units)
                self.b = {s.sem: s.take(n) for s in (att_scores, att_max, att_exp, att_probs, att_turned, att_probsT,
                                                    att_mixed, att_out)}
                self.masked = room[4:6]
                self.before = Linear.last

            def wait(self, eng, s, u):
                if u >= 0:
                    eng.wait_ge(s.sem, self.b[s.sem] + u + 1)

            def pe(self, pe, ready):
                n = len(self.units)
                for i in range(n + 2):
                    if i < n:
                        u = self.units[i]
                        nk = u["k"].shape[-1]
                        if i == 0:
                            pe.wait_ge(self.before[0].sem, self.before[1])
                        ready(pe, i)
                        self.wait(pe, att_max, i - 2)
                        self.wait(pe, att_exp, i - 2)
                        pe.matmul(bank[2 + i % 2][:, 0:nk], u["q"], u["k"], start=True, stop=True)\
                            .then_inc(att_scores.sem, 1)
                    if 1 <= i <= n:
                        j = i - 1
                        self.wait(pe, att_probs, j)
                        self.wait(pe, att_probsT, j - 2)
                        for b in range(len(self.units[j]["v"])):
                            ins = pe.transpose(bank[6 + j % 2][:, b * P:(b + 1) * P], self.p[j % 2][:, b * P:(b + 1) * P],
                                               ident)
                        ins.then_inc(att_turned.sem, 1)
                    if i >= 2:
                        j = i - 2
                        u = self.units[j]
                        self.wait(pe, att_probsT, j)
                        self.wait(pe, att_out, j - 2)
                        r = u["rows"]
                        product(pe, bank[j % 2][r, 0:P], lambda b: u["v"][b], lambda b: self.pt[j % 2][:, b * P:(b + 1) * P],
                                len(u["v"])).then_inc(att_mixed.sem, 1)

            def dve(self, dve):
                n = len(self.units)
                for i in range(n + 2):
                    if i < n:
                        u = self.units[i]
                        s = att_small[:, i % 2, :]
                        nk = u["k"].shape[-1]
                        src = bank[2 + i % 2][:, 0:nk]
                        self.wait(dve, att_scores, i)
                        self.wait(dve, att_exp, i - 2)
                        if u.get("mask") is not None:
                            m = self.masked[i % 2][:, 0:nk]
                            link(dve, nc.vector.tensor_tensor(m, src, u["mask"], ALU.add))
                            src = m
                        link(dve, nc.vector.reduce_max(s[:, 0:1], src, AX.X))
                        if u.get("sink") is not None:
                            ins = nc.vector.tensor_scalar(s[:, 1:2], s[:, 0:1], -self.scale, u["sink"][1], ALU.mult, ALU.min)
                        else:
                            ins = nc.vector.tensor_scalar(s[:, 1:2], s[:, 0:1], -self.scale, None, ALU.mult)
                        ins.then_inc(att_max.sem, 1)
                    if 1 <= i <= n:
                        j = i - 1
                        s = att_small[:, j % 2, :]
                        nk = self.units[j]["k"].shape[-1]
                        self.wait(dve, att_exp, j)
                        if self.units[j].get("sink") is not None:
                            link(dve, nc.vector.tensor_tensor(s[:, 2:3], s[:, 2:3], s[:, 4:5], ALU.add))
                        link(dve, nc.vector.reciprocal(s[:, 3:4], s[:, 2:3]))
                        p = self.p[j % 2][:, 0:nk]
                        nc.vector.tensor_scalar(p, p, s[:, 3:4], None, ALU.mult).then_inc(att_probs.sem, 1)
                    if i >= 2:
                        j = i - 2
                        self.wait(dve, att_mixed, j)
                        nc.vector.tensor_copy(self.units[j]["out"], bank[j % 2][self.units[j]["rows"], 0:P])\
                            .then_inc(att_out.sem, 1)

            def act(self, act):
                n = len(self.units)
                for i in range(n + 1):
                    if i < n:
                        u = self.units[i]
                        nk = u["k"].shape[-1]
                        s = att_small[:, i % 2, :]
                        self.wait(act, att_max, i)
                        self.wait(act, att_turned, i - 2)
                        src = bank[2 + i % 2][:, 0:nk] if u.get("mask") is None else self.masked[i % 2][:, 0:nk]
                        if u.get("sink") is not None:
                            self.wait(act, att_probs, i - 2)
                            nc.scalar.activation(s[:, 4:5], u["sink"][0], ACT.Exp, bias=s[:, 1:2])
                        nc.scalar.activation(self.p[i % 2][:, 0:nk], src, ACT.Exp, scale=self.scale, bias=s[:, 1:2],
                                             accum_out=s[:, 2:3]).then_inc(att_exp.sem, 1)
                    if i >= 1:
                        j = i - 1
                        nk = self.units[j]["k"].shape[-1]
                        self.wait(act, att_turned, j)
                        self.wait(act, att_mixed, j - 2)
                        nc.scalar.activation(self.pt[j % 2][:, 0:nk], bank[6 + j % 2][:, 0:nk], ACT.Copy)\
                            .then_inc(att_probsT.sem, 1)

        room = [a[:, 2 * i, :] for i in range(4)]
        mla_units = []
        for q0, k0, kn in ((0, 0, T), (LAT, LAT, CTX)):
            for hd in range(MH):
                for q in range(q0, q0 + LAT, P):
                    r = slice((hd % 2) * MV, (hd % 2 + 1) * MV)
                    mla_units.append(dict(q=qT[0:MQK, hd, q:q + P], k=kT[0:MQK, hd, k0:k0 + kn],
                                          v=[vt[:, b, hd * MV:(hd + 1) * MV] for b in range(k0 // P, (k0 + kn) // P)],
                                          rows=r, out=mix[r, hd // 2, q:q + P]))
        mla = Attention(mla_units, MQK ** -0.5, room)

        def pe_mla(pe):
            def ready(pe, i):
                if i == 0:
                    pe.wait_ge(rope_done.sem, 5)
                    pe.wait_ge(copied.sem, 1)
            mla.pe(pe, ready)

        gla_signals = {n: sig("gla_" + n) for n in ("logits", "logs", "gates", "cums", "decays", "decayed", "scores", "masked",
                                                    "turned", "keys", "updates", "states", "outs", "squares", "sums",
                                                    "roots", "merged")}
        cg = Carve()
        cg.at = even_at
        decay = cg(2 * GFB, T)
        qdec, kinv, kend = cg(2 * GFB, T), cg(2 * GFB, T), cg(2 * GFB, T)
        ktok = cg(2 * GFB, TB, P)
        ascore = cg(GH, TB, P)
        states = [arena[:, 0:GFB * NCH * P].rearrange("p (f n v) -> p f n v", f=GFB, n=NCH), cg(GFB, NCH, P)]
        gate = a[:, 0:4, :]
        gate_e = a[:, 4:8, :]
        gout = a[:, 0:4, :]
        gsq, groot = kend, kinv
        ORDER = (list(range(NCH // 2, NCH)) + list(range(NCH // 2)), list(range(NCH - 1, -1, -1)))
        G = {n: s.sem for n, s in gla_signals.items()}
        GBANK = (2, 3, 6, 7)

        def chunk(c):
            return slice(c * C, (c + 1) * C)

        def half(x):
            return slice(x * C, (x + 1) * C)

        def pe_gla(pe):
            for tb in range(TB):
                for z in range(2):
                    ins = pe.matmul(bank[GBANK[tb]][:, z * 256:(z + 1) * 256], glow[0:GRANK + 1, z, tb * P:(tb + 1) * P],
                                    glg[:, z, :], start=True, stop=True)
                ins.then_inc(G["logits"], 1)
            pe.wait_ge(att_out.sem, mla.b[att_out.sem] + len(mla.units))
            for q in range(2 * GFB):
                z = q // GFB
                for tb in range(TB):
                    if q == 0:
                        pe.wait_ge(G["gates"], tb + 1)
                    elif q == 2 and tb == 0:
                        pe.wait_ge(G["gates"], TB)
                    ins = pe.matmul(bank[q][:, tb * P:(tb + 1) * P], gate[:, tb, q * P:(q + 1) * P], upto[:, z, :],
                                    start=True, stop=True)
                ins.then_inc(G["cums"], 1)
            for q in range(2 * GFB):
                pe.wait_ge(G["decayed"], q + 1)
                for hh in range(2):
                    n = 2 * q + hh
                    if n >= 2:
                        pe.wait_ge(G["masked"], n - 1)
                    for tb in range(TB):
                        t = slice(tb * P, (tb + 1) * P)
                        ins = pe.matmul(bank[6 + hh][:, t], kinv[half(hh), q, t], qdec[half(hh), q, t], start=True, stop=True)
                    ins.then_inc(G["scores"], 1)
                if q >= 2:
                    pe.wait_ge(G["keys"], q - 1)
                for tb in range(TB):
                    t = slice(tb * P, (tb + 1) * P)
                    ins = pe.transpose(bank[q % 2][:, t], kend[:, q, t], ident)
                ins.then_inc(G["turned"], 1)
            for q in range(2 * GFB):
                pe.wait_ge(G["keys"], q + 1)
                if q == 1:
                    pe.wait_ge(G["masked"], 4 * GFB)
                    pe.wait_ge(G["decays"], 4 * GFB)
                elif q >= 2:
                    pe.wait_ge(G["states"], q - 1)
                for cp in range(2):
                    if q == 0:
                        pe.wait_ge(G["keys"], 2 * GFB)
                    b = bank[cp + 6 * (q % 2)]
                    for tb in range(TB):
                        for hh in range(2):
                            hd = 2 * (q % GFB) + hh
                            ins = pe.matmul(b[half(hh), tb * P:(tb + 1) * P], ktok[half(cp), q, tb, hh * C:(hh + 1) * C],
                                            gv[half(cp), tb, hd * P:(hd + 1) * P], start=True, stop=True)
                ins.then_inc(G["updates"], 1)
            for hd in range(GH):
                f, hh = hd // 2, hd % 2
                if hd == 0:
                    pe.wait_ge(G["states"], 2 * GFB)
                    pe.wait_ge(G["masked"], 4 * GFB)
                if hd >= 2:
                    pe.wait_ge(G["outs"], hd - 1)
                b = bank[2 + hd % 2]
                for tb in range(TB):
                    t = slice(tb * P, (tb + 1) * P)
                    pe.matmul(b[:, t], gv[:, tb, hd * P:(hd + 1) * P], ascore[:, hd, tb, :], start=tb == 0, stop=False,
                              skip_group_check=True)
                for z in range(2):
                    for n in range(1, NCH):
                        c = ORDER[z][n]
                        ins = pe.matmul(b[:, chunk(c)], states[z][half(hh), f, n, :], qdec[half(hh), GFB * z + f, chunk(c)],
                                        start=False, stop=z == 1 and n == NCH - 1, skip_group_check=True)
                ins.then_inc(G["sums"], 1)
            for hd in range(GH):
                pe.wait_ge(G["squares"], hd + 1)
                pe.matmul(bank[(0, 1, 6, 7)[hd]][:, :], ones, gsq[:, hd, :], start=True, stop=True).then_inc(G["sums"], 1)

        def act_gla(act):
            for tb in range(TB):
                act.wait_ge(G["logits"], tb + 1)
                nc.scalar.activation(gate_e[:, tb, :], bank[GBANK[tb]][:, :], ACT.Abs).then_inc(G["logs"], 1)
            for tb in range(TB):
                act.wait_ge(G["logs"], tb + 1)
                nc.scalar.activation(gate_e[:, tb, :], gate_e[:, tb, :], ACT.Exp, scale=-1.0).then_inc(G["logs"], 1)
            for tb in range(TB):
                act.wait_ge(G["logs"], TB + tb + 1)
                nc.scalar.activation(gate_e[:, tb, :], gate_e[:, tb, :], ACT.Ln, bias=1.0).then_inc(G["logs"], 1)
            for q in range(2 * GFB):
                act.wait_ge(G["cums"], q + 1)
                if q >= 2:
                    act.wait_ge(G["decayed"], q - 1)
                nc.scalar.activation(decay[:, q, :], bank[q][:, :], ACT.Exp, scale=1.0 / 16).then_inc(G["decays"], 1)
                nc.scalar.activation(tmp[:, q % 2, :], bank[q][:, :], ACT.Exp, scale=-1.0 / 16).then_inc(G["decays"], 1)
            for q in range(2 * GFB):
                act.wait_ge(G["turned"], q + 1)
                nc.scalar.activation(ktok[:, q].rearrange("p t f -> p (t f)"), bank[q % 2][:, :], ACT.Copy)\
                    .then_inc(G["keys"], 1)
            for hd in range(GH):
                act.wait_ge(G["sums"], hd + 1)
                act.wait_ge(G["turned"], 2 * GFB)
                nc.scalar.activation(gsq[:, hd, :], bank[2 + hd % 2][:, :], ACT.Square).then_inc(G["squares"], 1)
                nc.scalar.activation(gout[:, hd, :], bank[2 + hd % 2][:, :], ACT.Copy).then_inc(G["outs"], 1)
            for hd in range(GH):
                act.wait_ge(G["sums"], GH + hd + 1)
                nc.scalar.activation(groot[:, hd, :], bank[(0, 1, 6, 7)[hd]][:, :], ACT.Ln, scale=1.0 / GDV, bias=eps_col)\
                    .then_inc(G["roots"], 1)
            for hd in range(GH):
                act.wait_ge(G["roots"], hd + 1)
                nc.scalar.activation(groot[:, hd, :], groot[:, hd, :], ACT.Exp, scale=-0.5).then_inc(G["roots"], 1)

        def dve_gla(dve):
            for tb in range(TB):
                dve.wait_ge(G["logs"], 2 * TB + tb + 1)
                nc.vector.scalar_tensor_tensor(out=gate[:, tb, :], in0=bank[GBANK[tb]][:, :], scalar=0.0,
                                               in1=gate_e[:, tb, :], op0=ALU.min, op1=ALU.subtract).then_inc(G["gates"], 1)
            for q in range(2 * GFB):
                z, f = q // GFB, q % GFB
                dve.wait_ge(G["decays"], 2 * q + 2)
                nc.vector.scalar_tensor_tensor(out=qdec[:, q, :], in0=gq[:, f, :], scalar=GDK ** -0.5, in1=decay[:, q, :],
                                               op0=ALU.mult, op1=ALU.mult)
                link(dve, nc.vector.tensor_tensor(kinv[:, q, :], gk[:, f, :], tmp[:, q % 2, :], ALU.mult))
                last = decay[:, q, :].rearrange("p (n c) -> p n c", c=C)[:, :, (C - 1) * (1 - z):(C - 1) * (1 - z) + 1]
                nc.vector.tensor_tensor(kend[:, q, :].rearrange("p (n c) -> p n c", c=C),
                                        kinv[:, q, :].rearrange("p (n c) -> p n c", c=C),
                                        last.broadcast_to((P, NCH, C)), ALU.mult).then_inc(G["decayed"], 1)
            for q in range(2 * GFB):
                z = q // GFB
                for hh in range(2):
                    n, hd = 2 * q + hh, 2 * (q % GFB) + hh
                    dve.wait_ge(G["scores"], n + 1)
                    mask = upto[:, z:z + 1, :].broadcast_to((P, TB, P))
                    src = bank[6 + hh][:, :].rearrange("p (t i) -> p t i", t=TB)
                    if z == 0:
                        nc.vector.tensor_tensor(ascore[:, hd], src, mask, ALU.mult).then_inc(G["masked"], 1)
                    else:
                        part = tmp[:, hh, :].rearrange("p (t i) -> p t i", t=TB)
                        link(dve, nc.vector.tensor_tensor(part, src, mask, ALU.mult))
                        nc.vector.tensor_tensor(ascore[:, hd], ascore[:, hd], part, ALU.add).then_inc(G["masked"], 1)
            for q in range(2 * GFB):
                z, f = q // GFB, q % GFB
                dve.wait_ge(G["updates"], q + 1)
                for n in range(NCH - 1):
                    c = ORDER[z][n]
                    add = bank[c % 2 + 6 * (q % 2)][:, (c // 2) * P:(c // 2 + 1) * P]
                    to = states[z][:, f, n + 1, :]
                    last = c * C + (C - 1) * (1 - z)
                    if n == 0:
                        ins = nc.vector.tensor_copy(to, add)
                    else:
                        ins = nc.vector.scalar_tensor_tensor(out=to, in0=states[z][:, f, n, :],
                                                             scalar=decay[:, q, last:last + 1], in1=add,
                                                             op0=ALU.mult, op1=ALU.add)
                    if n < NCH - 2:
                        link(dve, ins)
                ins.then_inc(G["states"], 1)
            for hd in range(GH):
                dve.wait_ge(G["roots"], GH + hd + 1)
                link(dve, nc.vector.scalar_tensor_tensor(out=mix[:, 4 + hd, :], in0=gout[:, hd, :],
                                                         scalar=vector("gla_o_norm"), in1=groot[:, hd, :],
                                                         op0=ALU.mult, op1=ALU.mult))
                nc.vector.tensor_tensor(mix[:, 4 + hd, :], mix[:, 4 + hd, :], gg[:, hd, :], ALU.mult).then_inc(G["merged"], 1)

        class Projection:

            def __init__(self, weight, nk, nblocks, width, rhs, evac, split=1, banks=2, source=None):
                self.rhs, self.width, self.split, self.nb = rhs, width, split, nblocks
                self.kt = nk // split
                if split == 1:
                    if source is None:
                        source = lambda t: weight[0:nk * P, bass.ds(256 * t, 256)].rearrange("(k p) c -> p k c", p=P)
                    self.tiles = Tiles(nblocks // 2, source, nk, 256, loop=nblocks // 2 > 2 * SLOTS)
                    self.loop = self.tiles.loop
                else:
                    rows = self.kt * P
                    self.tiles = Tiles(2 * nblocks, lambda t: weight[rows * (t % 2):rows * (t % 2 + 1), bass.ds(P * (t // 2), P)]
                                       .rearrange("(k p) c -> p k c", p=P), self.kt, P)
                    self.tiles.loop = True
                    self.tiles.source_in = lambda i, t: weight[rows * (t % 2):rows * (t % 2 + 1),
                                                               bass.ds(2 * P * i + P * (t // 2), P)]\
                        .rearrange("(k p) c -> p k c", p=P)
                    self.loop = True
                self.per_body = SLOTS * 2 if split == 1 else SLOTS // 2
                self.lin = Linear(evac, nblocks, banks)
                assert not self.loop or self.per_body % banks == 0

            def done(self, n):
                if self.split == 1:
                    return n * (UNITS // 2) + (UNITS * self.tiles.first + UNITS // 2)
                return n * (2 * UNITS) + UNITS * (self.tiles.first + 2)

            def pe_tile(self, pe, t, body=None, ready=None):
                self.tiles.wait(pe, t, 0 if body is None else body)
                w = self.tiles.view(t)
                past = None if body is None else body * self.per_body
                if self.split == 1:
                    for b in range(2):
                        n = 2 * t + b
                        self.lin.free(pe, n, past)
                        product(pe, self.lin.bank(n)[:, 0:self.width], lambda k: w[:, k, b * P:(b + 1) * P], self.rhs, self.kt,
                                before=ready if n == 0 and body is None else None).then_inc(block_done.sem, UNITS // 2)
                else:
                    n, part = t // 2, t % 2
                    if part == 0:
                        self.lin.free(pe, n, past)
                    product(pe, self.lin.bank(n)[:, 0:self.width], lambda k: w[:, k, :], lambda k: self.rhs(self.kt * part + k),
                            self.kt, start=part == 0, stop=part == 1).then_inc(block_done.sem, UNITS)

            def pe(self, pe, ready=None):
                n = self.tiles.n
                bodies = n // SLOTS if self.loop else 0
                for t in range(SLOTS if bodies else n):
                    self.pe_tile(pe, t, ready=ready)
                if bodies:
                    with pe.Fori(1, bodies) as i:
                        for t in range(SLOTS):
                            self.pe_tile(pe, t, body=i)
                    for t in range(SLOTS * bodies, n):
                        self.pe_tile(pe, t)

        class Residual:

            def __init__(self, proj, layer, which):
                self.proj, self.j = proj, (3 * which + 2) * KB
                self.layer = layer

            def step(self, dve, n, u, past):
                dve.wait_ge(block_done.sem, self.proj.done(n))
                for z in range(self.proj.width // LAT):
                    s = slice(z * LAT, (z + 1) * LAT)
                    x = h[:, bass.ds(n, 1), s].rearrange("p o t -> p (o t)")
                    g = mod[:, self.layer, bass.ds(n + self.j, 1), z:z + 1].rearrange("p o t -> p (o t)")
                    ins = nc.vector.scalar_tensor_tensor(out=x, in0=self.proj.lin.bank(u)[:, s], scalar=g, in1=x,
                                                         op0=ALU.mult, op1=ALU.add)
                ins.then_inc(evac_dve.sem, 1)

            def dve(self, dve):
                with dve.Fori(0, KB // 2) as i:
                    for u in range(2):
                        self.step(dve, i * 2 + u, u, i)

        class Mlp:

            def __init__(self, layer, width):
                self.w = width
                self.hidden = arena[:, 0:FB * width].rearrange("p (n t) -> p n t", n=FB)
                self.norm = Modulated(layer, 1, width)
                self.up = Projection(d["mlp_w1"][layer], KB, FB, width, lambda k: a[:, k, 0:width], evac_dve)
                self.down = Projection(d["mlp_w2"][layer], FB, KB, width, lambda k: self.hidden[:, k, :], evac_dve, split=2)
                self.res = Residual(self.down, layer, 1)
                self.relus = relus.take(FB)

            def pe(self, pe):
                self.up.pe(pe, lambda k: self.norm.ready(pe, k))
                pe.wait_ge(evac_dve.sem, self.up.lin.base + FB)
                self.down.pe(pe)

            def act(self, act):
                with act.Fori(0, FB // 2) as i:
                    for u in range(2):
                        n = i * 2 + u
                        act.wait_ge(block_done.sem, self.up.done(n))
                        act.wait_ge(evac_dve.sem, n + (self.up.lin.base - 1))
                        nc.scalar.activation(tmp[:, u, 0:self.w], self.up.lin.bank(u)[:, 0:self.w], ACT.Relu)\
                            .then_inc(relus.sem, 1)

            def dve(self, dve):
                with dve.Fori(0, FB // 2) as i:
                    for u in range(2):
                        n = i * 2 + u
                        dve.wait_ge(relus.sem, n + (self.relus + 1))
                        nc.vector.tensor_tensor(self.hidden[:, bass.ds(n, 1), :].rearrange("p o t -> p (o t)"),
                                                tmp[:, u, 0:self.w], self.up.lin.bank(u)[:, 0:self.w], ALU.mult)\
                            .then_inc(evac_dve.sem, 1)
                self.res.dve(dve)

        relus = sig("relus")
        ada_b = Ada(Tiles((NMOD * KB - ADA_A) // 2, lambda t: cols_of(d["ada_w"][0], P * ADA_A + 256 * t, 256), KB, 256),
                    0, ADA_A, NMOD * KB - ADA_A)
        even_out = Projection(d["even_w_out"][0], KB, KB, T, lambda k: mix[:, k, :], evac_dve)
        even_res = Residual(even_out, 0, 0)
        mlp0 = Mlp(0, T)

        def squares_ready(total):
            def wait(eng, k):
                if k < 2:
                    eng.wait_ge(evac_dve.sem, total)
            return wait

        def pe_rest0(pe):
            pe.wait_ge(G["roots"], GH)
            ada_b.pe(pe)
            pe.wait_ge(G["merged"], GH)
            even_out.pe(pe)
            mlp0.norm.norm.pe_sums(pe)
            mlp0.pe(pe)

        def act_rest0(act):
            ada_b.act(act)
            mlp0.norm.norm.act_squares(act, squares_ready(even_out.lin.base + KB))
            mlp0.norm.norm.act_root(act)
            mlp0.norm.act(act)
            mlp0.act(act)

        def dve_rest0(dve):
            ada_b.dve(dve)
            dve.wait_ge(gains_done.sem, 2)
            even_res.dve(dve)
            mlp0.norm.norm.dve_squares(dve, squares_ready(even_out.lin.base + KB))
            mlp0.norm.dve(dve)
            mlp0.dve(dve)

        n3 = Modulated(1, 0, T)
        ada_c = Ada(Tiles(NMOD * KB // 2, lambda t: cols_of(d["ada_w"][1], 256 * t, 256), KB, 256), 1, 0, NMOD * KB)
        co = Carve()
        qf, kf = co(QKB, LAT), co(QKB, T)
        vtok, ktk = co(TB, NH * NDV), co(TB, NH * NDK)
        sg = co(VB, LAT)
        ab, la, beta = co(TB, 4 * NH), co(TB, 2 * NH), co(TB, 2 * NH)
        gsum, eg, kef, betaw = co(TB, 2 * NH), co(TB, 2 * NH), co(TB, 2 * NH), co(TB, 2 * NH)
        gend = co(NCH, 2, NH // 2)
        gsm = co(TB, 2 * NH)
        vf = co(2, T)
        co.at -= 2 * T
        BT, BX, BXT, BY, BC, BA = (co(2, NH, C) for _ in range(6))
        WT = co(2, 2, NH // 2, C)
        kends, qdc = co(2, NH * NDK), co(2, NH // 2, P)
        S = co(3, 2, NH // 2, NDV)
        U = a[:, 0:4, :].rearrange("p k t -> p (k t)").rearrange("p (z h v) -> p z h v", z=2, h=NH)
        QKT = a[:, 4:8, :].rearrange("p k t -> p (k t)").rearrange("p (z h i) -> p z h i", z=2, h=NH)
        BC2 = tmp[:, :, :].rearrange("p z (h i) -> p z h i", h=NH)
        odd_names = ("gates_in", "scaled", "silu", "turned", "vals", "sq", "sums", "logs", "roots", "normed", "kturn", "ktok",
                     "sp", "gates", "cums", "cumsd", "ge")
        OS = {n: sig("odd_" + n).sem for n in odd_names}
        w_odd = d["gdn_w_in"][0]
        odd_tiles = [Tiles(1, lambda t, j=j: cols_of(w_odd, 256 * j, 256 if j < 11 else 288), KB, 256 if j < 11 else 288)
                     for j in range(12)]
        NB_CONV = 2 * QKB + VB
        odd_mixed = sig("odd_mixed")
        odd_lin = Linear(odd_mixed, NB_CONV)
        OS["mixed"] = odd_mixed.sem
        sg_lin = Linear(evac_act, VB)

        def odd_width(n):
            return LAT if n < QKB or n >= NB_CONV else T

        def odd_dst(n):
            if n < QKB:
                return qf[:, n, :]
            return kf[:, n - QKB, :] if n < 2 * QKB else vf[:, n % 2, :]

        def odd_done(n):
            return odd_tiles[n // 2].done(0, n % 2 if n % 2 == 0 or n // 2 == 11 else UNITS - 1)

        def pe_odd_in(pe):
            def turn(n):
                j = n - 2 * QKB
                pe.wait_ge(OS["silu"], n + 1)
                if j >= 2:
                    pe.wait_ge(OS["vals"], j - 1)
                for tb in range(TB):
                    ins = pe.transpose(bank[2 + j % 2][:, tb * P:(tb + 1) * P], vf[:, n % 2, tb * P:(tb + 1) * P], ident)
                ins.then_inc(OS["turned"], 1)

            for n in range(NB_CONV + VB):
                lin, i = (odd_lin, n) if n < NB_CONV else (sg_lin, n - NB_CONV)
                if n % 2 == 0:
                    odd_tiles[n // 2].wait(pe, 0)
                w, width = odd_tiles[n // 2].view(0), odd_width(n)
                lin.free(pe, i)
                product(pe, lin.bank(i)[:, 0:width], lambda k: w[:, k, (n % 2) * P:(n % 2 + 1) * P],
                        lambda k: a[:, k, 0:width], KB, before=(lambda k: n3.ready(pe, k)) if n == 0 else None)\
                    .then_inc(block_done.sem, 1 if n % 2 == 0 or n // 2 == 11 else UNITS - 1)
                if 2 * QKB < n <= NB_CONV:
                    turn(n - 1)
            w = odd_tiles[11].view(0)
            for tb in range(TB):
                ins = product(pe, bank[6][:, tb * 32:(tb + 1) * 32], lambda k: a[:, k, tb * P:(tb + 1) * P],
                              lambda k: w[:, k, 256:288], KB)
            ins.then_inc(block_done.sem, UNITS - 2)
            for n in range(2 * QKB):
                pe.wait_ge(OS["sq"], n + 1)
                if n == 0:
                    pe.wait_ge(OS["vals"], VB)
                if n >= 4:
                    pe.wait_ge(OS["logs"], n - 3)
                width = odd_width(n)
                pe.matmul(bank[(2, 3, 4, 5)[n % 4]][:, 0:width], ones_half, odd_sq(n), start=True, stop=True)\
                    .then_inc(OS["sums"], 1)
            pe.wait_ge(OS["gates"], 1)
            pe.wait_ge(evac_act.sem, sg_lin.base + VB)
            for tb in range(TB):
                for z in range(2):
                    pe.matmul(bank[7][:, tb * 16 + z * NH:tb * 16 + (z + 1) * NH], upto[:, z, :], la[:, tb, z * NH:(z + 1) * NH],
                              start=True, stop=True)
                pe.matmul(bank[7][:, 64 + tb * 16:64 + (tb + 1) * 16], ones_half, la[:, tb, :], start=True, stop=True)
            for c in range(NCH):
                ins = pe.matmul(bank[c % 2][:, (c // 2) * 16:(c // 2 + 1) * 16], ones[half(c % 2), :], la[half(c % 2), c // 2, :],
                                start=True, stop=True)
            ins.then_inc(OS["cums"], 1)
            for f in range(QKB):
                pe.wait_ge(OS["normed"], QKB + f + 1)
                if f == 0:
                    pe.wait_ge(OS["logs"], 2 * QKB)
                if f >= 2:
                    pe.wait_ge(OS["ktok"], f - 1)
                for tb in range(TB):
                    ins = pe.transpose(bank[2 + f % 2][:, tb * P:(tb + 1) * P], kf[:, f, tb * P:(tb + 1) * P], ident)
                ins.then_inc(OS["kturn"], 1)

        def odd_sq(n):
            return mix[:, n, 0:odd_width(n)]

        def conv_w(tap, n):
            return vector("gdn_conv_w").rearrange("p (t n) -> p t n", t=3)[:, tap, n:n + 1]

        def act_odd_in(act):
            def silu(n):
                act.wait_ge(OS["mixed"], n + 1)
                nc.scalar.activation(odd_dst(n), odd_dst(n), ACT.Silu).then_inc(OS["silu"], 1)

            def vals(j):
                act.wait_ge(OS["turned"], j + 1)
                nc.scalar.activation(vtok[:, :, j * P:(j + 1) * P], bank[2 + j % 2][:, :].rearrange("p (t f) -> p t f", t=TB),
                                     ACT.Copy).then_inc(OS["vals"], 1)

            for n in range(NB_CONV):
                act.wait_ge(block_done.sem, odd_done(n))
                if n >= 2 * QKB + 2:
                    act.wait_ge(OS["turned"], n - 2 * QKB - 1)
                nc.scalar.activation(odd_dst(n), odd_lin.bank(n)[:, 0:odd_width(n)], ACT.Copy, scale=conv_w(1, n))\
                    .then_inc(OS["scaled"], 1)
                if n >= 1:
                    silu(n - 1)
                if n >= 2 * QKB + 2:
                    vals(n - 2 * QKB - 2)
            silu(NB_CONV - 1)
            for i in range(VB):
                act.wait_ge(block_done.sem, odd_done(NB_CONV + i))
                nc.scalar.activation(sg[:, i, :], sg_lin.bank(i)[:, 0:LAT], ACT.Silu).then_inc(evac_act.sem, 1)
                if i < 2:
                    vals(VB - 2 + i)
            act.wait_ge(OS["gates_in"], 1)
            nc.scalar.activation(gsm[:, :, :], ab[:, :, 0:16], ACT.Abs).then_inc(OS["sp"], 1)
            act.wait_ge(OS["sp"], 1)
            nc.scalar.activation(gsm[:, :, :], gsm[:, :, :], ACT.Exp, scale=-1.0).then_inc(OS["sp"], 1)
            nc.scalar.activation(beta[:, :, :], ab[:, :, 16:32], ACT.Exp, scale=-1.0)
            nc.scalar.activation(eg[:, 0, :], vector("gdn_a_log"), ACT.Exp)
            act.wait_ge(OS["sp"], 2)
            nc.scalar.activation(gsm[:, :, :], gsm[:, :, :], ACT.Ln, bias=1.0).then_inc(OS["sp"], 1)
            for n in range(2 * QKB):
                act.wait_ge(OS["sums"], n + 1)
                nc.scalar.activation(odd_sq(n), bank[(2, 3, 4, 5)[n % 4]][:, 0:odd_width(n)], ACT.Ln, bias=eps_col)\
                    .then_inc(OS["logs"], 1)
            for n in range(2 * QKB):
                act.wait_ge(OS["logs"], n + 1)
                nc.scalar.activation(odd_sq(n), odd_sq(n), ACT.Exp, scale=-0.5).then_inc(OS["roots"], 1)
            act.wait_ge(OS["cumsd"], 1)
            nc.scalar.activation(eg[:, :, :], gsum[:, :, :], ACT.Exp).then_inc(OS["ge"], 1)
            nc.scalar.activation(kef[:, :, :], kef[:, :, :], ACT.Exp).then_inc(OS["ge"], 1)
            nc.scalar.activation(gend[:, :, :, :], gend[:, :, :, :], ACT.Exp).then_inc(OS["ge"], 1)
            for f in range(QKB):
                act.wait_ge(OS["kturn"], f + 1)
                nc.scalar.activation(ktk[:, :, f * P:(f + 1) * P], bank[2 + f % 2][:, :].rearrange("p (t f) -> p t f", t=TB),
                                     ACT.Copy).then_inc(OS["ktok"], 1)

        def dve_odd_in(dve):
            for n in range(NB_CONV):
                dve.wait_ge(OS["scaled"], n + 1)
                width = odd_width(n)
                x = odd_lin.bank(n)[:, 0:width].rearrange("p (s t) -> p s t", t=LAT)
                y = odd_dst(n).rearrange("p (s t) -> p s t", t=LAT)
                link(dve, nc.vector.scalar_tensor_tensor(out=y[:, :, 1:], in0=x[:, :, 0:LAT - 1], scalar=conv_w(0, n),
                                                         in1=y[:, :, 1:], op0=ALU.mult, op1=ALU.add))
                nc.vector.scalar_tensor_tensor(out=y[:, :, 0:LAT - 1], in0=x[:, :, 1:], scalar=conv_w(2, n),
                                               in1=y[:, :, 0:LAT - 1], op0=ALU.mult, op1=ALU.add).then_inc(OS["mixed"], 1)
            for n in range(2 * QKB):
                dve.wait_ge(OS["silu"], n + 1)
                nc.vector.tensor_tensor(odd_sq(n), odd_dst(n), odd_dst(n), ALU.mult).then_inc(OS["sq"], 1)
            dve.wait_ge(block_done.sem, odd_tiles[11].done(0))
            link(dve, nc.vector.tensor_copy(ab[:, :, :], bank[6][:, 0:128].rearrange("p (t c) -> p t c", t=TB)))
            bias = vector("gdn_dt_bias").rearrange("p (o c) -> p o c", o=1).broadcast_to((P, TB, 16))
            nc.vector.tensor_tensor(ab[:, :, 0:16], ab[:, :, 0:16], bias, ALU.add).then_inc(OS["gates_in"], 1)
            dve.wait_ge(OS["gates_in"], 1)
            link(dve, nc.vector.tensor_scalar(la[:, :, :], ab[:, :, 0:16], 0.0, None, ALU.max))
            dve.wait_ge(OS["sp"], 3)
            link(dve, nc.vector.tensor_tensor(la[:, :, :], la[:, :, :], gsm[:, :, :], ALU.add))
            link(dve, nc.vector.tensor_tensor(la[:, :, :], la[:, :, :], eg[:, 0:1, :].broadcast_to((P, TB, 16)), ALU.mult))
            nc.vector.tensor_scalar(la[:, :, :], la[:, :, :], -1.0, None, ALU.mult).then_inc(OS["gates"], 1)
            link(dve, nc.vector.tensor_scalar(beta[:, :, :], beta[:, :, :], 1.0, None, ALU.add))
            link(dve, nc.vector.reciprocal(beta[:, :, :], beta[:, :, :]))
            for n in range(2 * QKB):
                dve.wait_ge(OS["roots"], n + 1)
                nc.vector.scalar_tensor_tensor(out=odd_dst(n), in0=odd_dst(n), scalar=NDK ** -0.5 if n < QKB else 1.0,
                                               in1=odd_sq(n), op0=ALU.mult, op1=ALU.mult).then_inc(OS["normed"], 1)
            dve.wait_ge(OS["cums"], 1)
            link(dve, nc.vector.tensor_copy(gsum[:, :, :].rearrange("p t c -> p (t c)"), bank[7][:, 0:64]))
            nc.vector.tensor_tensor(kef[:, :, :].rearrange("p t c -> p (t c)"), bank[7][:, 64:128],
                                    gsum[:, :, :].rearrange("p t c -> p (t c)"), ALU.subtract)
            for cp in range(2):
                for par in range(2):
                    src = bank[cp][half(par), 0:64].rearrange("p (c x) -> p c x", c=TB)
                    src = src.rearrange("p c (z h r) -> p c z h r", z=2, r=2)[:, :, :, :, par]
                    dst = gend[half(par), :, :, :].rearrange("p (c r) z h -> p c r z h", r=2)[:, :, cp]
                    ins = nc.vector.tensor_copy(dst, src)
            ins.then_inc(OS["cumsd"], 1)
            dve.wait_ge(OS["ge"], 1)
            nc.vector.tensor_tensor(betaw[:, :, :], beta[:, :, :], eg[:, :, :], ALU.mult).then_inc(OS["cumsd"], 1)

        pair_names = ("g", "d", "qe", "clamp", "e", "em", "kk", "aa", "xb", "at", "atc", "xtb", "qk", "qkt", "ct", "y", "yc", "zx",
                      "zt", "xs", "xts", "tts", "u", "uc", "wt", "wtc", "kend", "ws", "vn", "su", "ss", "o", "oc", "qdec", "clear", "eb")
        N = {n: sig("gdn_" + n).sem for n in pair_names}
        TBS = ((2, 3), (3, 2), (0, 1), (1, 0))
        LEVELS = 5
        levels = table("levels").rearrange("p (z l c) -> p z l c", z=2, l=LEVELS)
        pairs = table("pairs").rearrange("p (z c) -> p z c", z=2)
        strict = table("strict").rearrange("p (z c) -> p z c", z=2)
        upto64 = table("upto64").rearrange("p (z c) -> p z c", z=2)
        eye64 = table("eye64")

        def heads(m):
            return m.rearrange("p (o c) -> p o c", o=1).broadcast_to((P, NH, C))

        def per_head(m, n=C):
            return m.rearrange("p (h o) -> p h o", o=1).broadcast_to((P, NH, n))

        def zb(z, i):
            return bank[4 * z + i]

        def gview(z, hq):
            return zb(z, hq)[:, :].rearrange("p (h i) -> p h i", h=4)

        def hb(b, n=C):
            return b[:, 0:4 * n].rearrange("p (h i) -> p h i", h=4)

        def pe_pair(pe, p):
            lat = p >= 2
            us = [(z, 2 * p + z) for z in range(2)]
            if p == 0:
                pe.wait_ge(OS["cumsd"], 2)
                pe.wait_ge(OS["ktok"], QKB)
            for z, u in us:
                if p >= 1:
                    pe.wait_ge(N["vn"], 4 * p)
                    if p == 3:
                        pe.wait_ge(N["oc"], 4)
                for hd in range(NH):
                    col = la[:, TBS[p][z], z * NH + hd:z * NH + hd + 1].broadcast_to((P, P))
                    ins = pe.matmul(zb(z, hd // 4)[:, (hd % 4) * P:(hd % 4 + 1) * P], col, upto[:, z, :], start=True, stop=True)
                ins.then_inc(N["g"], 1)
            for z, u in us:
                if p >= 1:
                    pe.wait_ge(N["ss"], 4 * p)
                for par in range(2):
                    for c in range(2):
                        t = slice(TBS[p][z] * P + c * C, TBS[p][z] * P + (c + 1) * C)
                        for hp in range(4):
                            ins = pe.matmul(hb(zb(z, 2 + par))[half(c), hp, :], kf[half(par), hp, t], kf[half(par), hp, t],
                                            start=True, stop=True)
                ins.then_inc(N["kk"], 1)
            for z, u in us:
                pe.wait_ge(N["aa"], u + 1)
                if lat:
                    pe.wait_ge(N["qe"], u - 3)
                for c in range(2):
                    for hd in range(NH):
                        ins = pe.matmul(zb(z, 0)[half(c), hd * C:(hd + 1) * C], BA[half(c), z, hd, :], eye64[half(c), :],
                                        start=True, stop=True)
                ins.then_inc(N["at"], 1)
                if lat:
                    for par in range(2):
                        for c in range(2):
                            t = slice(TBS[p][z] * P + c * C, TBS[p][z] * P + (c + 1) * C)
                            for hp in range(4):
                                ins = pe.matmul(hb(zb(z, 2 + par))[half(c), hp, :], kf[half(par), hp, t],
                                                qf[half(par), hp, t], start=True, stop=True)
                    ins.then_inc(N["qk"], 1)
            for lv in range(LEVELS):
                for z, u in us:
                    pe.wait_ge(N["ct"], LEVELS * 2 * p + 2 * lv + z + 1)
                    if lv == 0:
                        pe.wait_ge(N["xb"], u + 1)
                        pe.wait_ge(N["atc"], u + 1)
                    else:
                        pe.wait_ge(N["xs"], (LEVELS - 1) * 2 * p + 2 * (lv - 1) + z + 1)
                    for c in range(2):
                        for hd in range(NH):
                            ins = pe.matmul(zb(z, 1)[half(c), hd * C:(hd + 1) * C], ctv(lv)[half(c), z, hd, :],
                                            BX[half(c), z, hd, :], start=True, stop=True)
                    ins.then_inc(N["y"], 1)
                for z, u in us:
                    v = LEVELS * 2 * p + 2 * lv + z
                    pe.wait_ge(N["yc"], v + 1)
                    if lv == 0:
                        pe.wait_ge(N["xtb"], u + 1)
                        if lat:
                            pe.wait_ge(N["qkt"], u - 3)
                    else:
                        pe.wait_ge(N["xts"], v - 1)
                    if lv < LEVELS - 1:
                        for c in range(2):
                            for hd in range(NH):
                                ins = pe.matmul(zb(z, 2)[half(c), hd * C:(hd + 1) * C], BXT[half(c), z, hd, :],
                                                BY[half(c), z, hd, :], start=True, stop=True)
                        ins.then_inc(N["zx"], 1)
                    for c in range(2):
                        for hd in range(NH):
                            ins = pe.matmul(zb(z, 3)[half(c), hd * C:(hd + 1) * C], BY[half(c), z, hd, :],
                                            BXT[half(c), z, hd, :], start=True, stop=True)
                    ins.then_inc(N["zt"], 1)
            for z, u in us:
                pe.wait_ge(N["tts"], u + 1)
                pe.wait_ge(N["yc"], LEVELS * 2 * (p + 1))
                pe.wait_ge(N["xts"], LEVELS * 2 * (p + 1))
                tb = TBS[p][z]
                for c in range(2):
                    for hd in range(NH):
                        ins = pe.matmul(gview(z, hd // 4)[half(c), hd % 4, :], BY[half(c), z, hd, :],
                                        vtok[half(c), tb, hd * P:(hd + 1) * P], start=True, stop=True)
                ins.then_inc(N["u"], 1)
                for c in range(2):
                    for hd in range(NH):
                        ins = pe.matmul(hb(zb(z, 2 + c))[half(hd % 2), hd // 2, :], ktk[half(c), tb, hd * C:(hd + 1) * C],
                                        BX[half(c), z, hd, :], start=True, stop=True)
                ins.then_inc(N["wt"], 1)
            for st in range(2):
                for z, u in us:
                    c = st if z == 0 else 1 - st
                    s = 4 * p + 2 * st + z
                    if st == 0:
                        pe.wait_ge(N["uc"], u + 1)
                        pe.wait_ge(N["wtc"], u + 1)
                    if s >= 2:
                        pe.wait_ge(N["ss"], s - 1)
                        for par in range(2):
                            for hp in range(4):
                                ins = pe.matmul(gview(z, par)[half(c), hp, :], WT[half(par), z, c, hp, :],
                                                S[half(par), (2 * p + st) % 3, z, hp, :], start=True, stop=True)
                        ins.then_inc(N["ws"], 1)
                for z, u in us:
                    c = st if z == 0 else 1 - st
                    s = 4 * p + 2 * st + z
                    if not (p == 3 and st == 1):
                        pe.wait_ge(N["vn"], s + 1)
                        pe.wait_ge(N["kend"], u + 1)
                        for hd in range(NH):
                            ins = pe.matmul(zb(z, 2)[half(hd % 2), (hd // 2) * P:(hd // 2 + 1) * P],
                                            kends[half(c), z, hd * C:(hd + 1) * C], U[half(c), z, hd, :], start=True, stop=True)
                        ins.then_inc(N["su"], 1)
            if lat:
                pe.wait_ge(N["vn"], 4 * (p + 1))
                pe.wait_ge(N["qdec"], 2 * (p - 1))
                pe.wait_ge(N["qkt"], 2 * (p - 1))
                for b in range(4):
                    par, h2 = b // 2, b % 2
                    o = obank(b)
                    for i in range(2):
                        hd = 2 * (2 * h2 + i) + par
                        for z in range(2):
                            pe.matmul(o[:, (2 * i + z) * P:(2 * i + z + 1) * P], U[:, z, hd, :], QKT[:, z, hd, :],
                                      start=i == 0 and z == 0, stop=False, skip_group_check=True)
                    for i in range(2):
                        hp = 2 * h2 + i
                        for z in range(2):
                            for st in range(2):
                                c = st if z == 0 else 1 - st
                                at = (2 * i + z) * P + c * C
                                ins = pe.matmul(o[:, at:at + C], S[half(par), (2 * p + st) % 3, z, hp, :],
                                                qdc[half(par), z, hp, c * C:(c + 1) * C], start=False,
                                                stop=i == 1 and z == 1 and st == 1, skip_group_check=True)
                    ins.then_inc(N["o"], 1)

        def obank(b):
            return bank[(0, 1, 4, 5)[b]]

        def ctv(lv):
            return BC if lv % 2 == 0 else BC2

        def act_pair(act, p):
            lat = p >= 2
            us = [(z, 2 * p + z) for z in range(2)]
            for z, u in us:
                if lat:
                    act.wait_ge(N["d"], u + 1)
                    if p == 3:
                        act.wait_ge(N["o"], 4)
                    for par in range(2):
                        for hq in range(2):
                            src = gview(z, hq).rearrange("p (h r) i -> p h r i", r=2)[half(par), :, par, :]
                            ins = nc.scalar.activation(qdc[half(par), z, 2 * hq:2 * hq + 2, :], src, ACT.Exp)
                    ins.then_inc(N["qe"], 1)
            for z, u in us:
                act.wait_ge(N["clamp"], u + 1)
                nc.scalar.activation(BA[:, z], BA[:, z], ACT.Exp, scale=-1.0).then_inc(N["e"], 1)
                if lat:
                    nc.scalar.activation(BT[:, z], BT[:, z], ACT.Exp).then_inc(N["e"], 1)
            for z, u in us:
                act.wait_ge(N["at"], u + 1)
                if lat:
                    act.wait_ge(N["qkt"], u - 3)
                nc.scalar.activation(BT[:, z].rearrange("p h c -> p (h c)"), zb(z, 0)[:, :], ACT.Copy).then_inc(N["atc"], 1)
            for lv in range(LEVELS):
                for z, u in us:
                    v = LEVELS * 2 * p + 2 * lv + z
                    act.wait_ge(N["y"], v + 1)
                    if lv >= 1:
                        act.wait_ge(N["zt"], v - 1)
                    nc.scalar.activation(BY[:, z].rearrange("p h c -> p (h c)"), zb(z, 1)[:, :], ACT.Copy)\
                        .then_inc(N["yc"], 1)
            for z, u in us:
                act.wait_ge(N["u"], u + 1)
                for hq in range(2):
                    ins = nc.scalar.activation(U[:, z, 4 * hq:4 * hq + 4, :], gview(z, hq), ACT.Copy)
                ins.then_inc(N["uc"], 1)
                act.wait_ge(N["wt"], u + 1)
                for c in range(2):
                    ins = nc.scalar.activation(WT[:, z, c], hb(zb(z, 2 + c)), ACT.Copy)
                ins.then_inc(N["wtc"], 1)

        def dve_pair(dve, p):
            lat = p >= 2
            us = [(z, 2 * p + z) for z in range(2)]
            for z, u in us:
                dve.wait_ge(N["g"], u + 1)
                if p >= 1:
                    dve.wait_ge(N["at"], 2 * p)
                for c in range(2):
                    for hq in range(2):
                        col = gsum[half(c), TBS[p][z], z * NH + 4 * hq:z * NH + 4 * hq + 4]\
                            .rearrange("p (h o) -> p h o", o=1).broadcast_to((C, 4, C))
                        ins = nc.vector.tensor_tensor(BA[half(c), z, 4 * hq:4 * hq + 4, :],
                                                      gview(z, hq)[half(c), :, c * C:(c + 1) * C], col, ALU.subtract)
                ins.then_inc(N["d"], 1)
            for z, u in us:
                dve.wait_ge(N["em"], u + 1)
                dve.wait_ge(N["kk"], u + 1)
                for par in range(2):
                    e = BA[:, z].rearrange("p (h r) c -> p h r c", r=2)[:, :, par, :]
                    ins = nc.vector.tensor_tensor(e, hb(zb(z, 2 + par)), e, ALU.mult)
                ins.then_inc(N["aa"], 1)
                if lat:
                    dve.wait_ge(N["aa"], u + 1)
                link_x(dve, BX, BA, z, pairs[:, z, :], N["xb"], N["aa"], u)
                if lat:
                    dve.wait_ge(N["qk"], u - 3)
                    dve.wait_ge(N["clear"], 1)
                    if p == 3:
                        dve.wait_ge(N["o"], 4)
                    for par in range(2):
                        for c in range(2):
                            e = BT[half(c), z].rearrange("p (h r) c -> p h r c", r=2)[:, :, par, :]
                            dst = QKT[half(c), z].rearrange("p (h r) i -> p h r i", r=2)[:, :, par, c * C:(c + 1) * C]
                            ins = nc.vector.tensor_tensor(dst, hb(zb(z, 2 + par))[half(c)], e, ALU.mult)
                    ins.then_inc(N["qkt"], 1)
            for z, u in us:
                link_x(dve, BXT, BT, z, pairs[:, 1 - z, :], N["xtb"], N["atc"], u)
            for lv in range(LEVELS):
                for z, u in us:
                    v = LEVELS * 2 * p + 2 * lv + z
                    if lv < LEVELS - 1:
                        w = (LEVELS - 1) * 2 * p + 2 * lv + z
                        dve.wait_ge(N["zx"], w + 1)
                        x = BX[:, z].rearrange("p h c -> p (h c)")
                        nc.vector.tensor_tensor(x, x, zb(z, 2)[:, :], ALU.subtract).then_inc(N["xs"], 1)
                    dve.wait_ge(N["zt"], v + 1)
                    x = BXT[:, z].rearrange("p h c -> p (h c)")
                    nc.vector.tensor_tensor(x, x, zb(z, 3)[:, :], ALU.subtract).then_inc(N["xts"], 1)
            for z, u in us:
                tb = TBS[p][z]
                dve.wait_ge(N["xts"], LEVELS * 2 * (p + 1) - 1 + z)
                dve.wait_ge(N["zt"], LEVELS * 2 * (p + 1))
                nc.vector.tensor_tensor(BY[:, z], BXT[:, z], per_head(beta[:, tb, z * NH:(z + 1) * NH]), ALU.mult)
                nc.vector.tensor_tensor(BX[:, z], BXT[:, z], per_head(betaw[:, tb, z * NH:(z + 1) * NH]), ALU.mult)\
                    .then_inc(N["tts"], 1)
            for st in range(2):
                for z, u in us:
                    c = st if z == 0 else 1 - st
                    s = 4 * p + 2 * st + z
                    dve.wait_ge(N["uc"], u + 1)
                    if s >= 2:
                        dve.wait_ge(N["ws"], s - 1)
                        for par in range(2):
                            x = U[half(c), z].rearrange("p (h r) v -> p h r v", r=2)[:, :, par, :]
                            ins = nc.vector.tensor_tensor(x, x, gview(z, par)[half(c)], ALU.subtract)
                        ins.then_inc(N["vn"], 1)
                    else:
                        dve.sem_inc(N["vn"], 1)
                for z, u in us:
                    c = st if z == 0 else 1 - st
                    s = 4 * p + 2 * st + z
                    if p == 3 and st == 1:
                        continue
                    dve.wait_ge(N["su"], s + 1)
                    if p == 3:
                        dve.wait_ge(N["o"], 4)
                    old, new = S[:, (2 * p + st) % 3, z], S[:, (2 * p + st + 1) % 3, z]
                    if s >= 2:
                        dve.wait_ge(N["ss"], s - 1)
                    for hp in range(4):
                        add = zb(z, 2)[:, hp * P:(hp + 1) * P]
                        if s < 2:
                            ins = nc.vector.tensor_copy(new[:, hp, :], add)
                        else:
                            g = gend[:, 2 * TBS[p][z] + c, z, hp:hp + 1]
                            ins = nc.vector.scalar_tensor_tensor(out=new[:, hp, :], in0=old[:, hp, :], scalar=g, in1=add,
                                                                 op0=ALU.mult, op1=ALU.add)
                    ins.then_inc(N["ss"], 1)
            if lat:
                for b in range(4):
                    par, h2 = b // 2, b % 2
                    dve.wait_ge(N["o"], 4 * (p - 2) + b + 1)
                    for z in range(2):
                        t = slice(TBS[p][z] * P, (TBS[p][z] + 1) * P)
                        dst = mix[:, :, t].rearrange("p (h r) t -> p h r t", r=2)[:, 2 * h2:2 * h2 + 2, par, :]
                        src = obank(b)[:, :].rearrange("p (h z t) -> p h z t", h=2, z=2)[:, :, z, :]
                        if p == 2:
                            ins = nc.vector.tensor_copy(dst, src)
                        else:
                            ins = nc.vector.tensor_tensor(dst, dst, src, ALU.add)
                    ins.then_inc(N["oc"], 1)

        def link_x(dve, dst, src, z, mask, signal, source, u):
            dve.wait_ge(source, u + 1)
            link(dve, nc.vector.tensor_tensor(dst[:, z], src[:, z], heads(mask), ALU.mult))
            nc.vector.tensor_tensor(dst[:, z], heads(eye64), dst[:, z], ALU.subtract).then_inc(signal, 1)

        def pool_pair(pool, p):
            lat = p >= 2
            us = [(z, 2 * p + z) for z in range(2)]
            if p == 0:
                pool.wait_ge(evac_act.sem, sg_lin.base + VB)
                pool.wait_ge(OS["cums"], 1)
                pool.wait_ge(OS["cumsd"], 2)
                nc.gpsimd.memset(QKT, 0.0).then_inc(N["clear"], 1)
            for z, u in us:
                pool.wait_ge(N["d"], u + 1)
                if lat:
                    nc.gpsimd.tensor_scalar(BT[:, z], BA[:, z], 0.0, None, ALU.min)
                nc.gpsimd.tensor_scalar(BA[:, z], BA[:, z], 0.0, None, ALU.max).then_inc(N["clamp"], 1)
            for z, u in us:
                tb = TBS[p][z]
                pool.wait_ge(N["e"], 2 * u - 2 if lat else u + 1)
                nc.gpsimd.tensor_tensor(BA[:, z], BA[:, z], per_head(beta[:, tb, z * NH:(z + 1) * NH]), ALU.mult)\
                    .then_inc(N["eb"], 1)
                if lat:
                    nc.gpsimd.tensor_tensor(BT[:, z], BT[:, z], heads(upto64[:, z, :]), ALU.mult)
                pool.wait_ge(N["eb"], u + 1)
                nc.gpsimd.tensor_tensor(BA[:, z], BA[:, z], heads(strict[:, z, :]), ALU.mult).then_inc(N["em"], 1)
            for z, u in us:
                tb = TBS[p][z]
                if p >= 1:
                    pool.wait_ge(N["su"], 4 * p)
                pool.wait_ge(OS["ge"], 3)
                nc.gpsimd.tensor_tensor(kends[:, z].rearrange("p (h c) -> p h c", h=NH),
                                        ktk[:, tb, :].rearrange("p (h c) -> p h c", h=NH),
                                        per_head(kef[:, tb, z * NH:(z + 1) * NH]), ALU.mult).then_inc(N["kend"], 1)
                if lat:
                    pool.wait_ge(N["qe"], u - 3)
                    nc.gpsimd.tensor_tensor(qdc[:, z], qdc[:, z], qf[:, :, tb * P:(tb + 1) * P], ALU.mult)\
                        .then_inc(N["qdec"], 1)
            for lv in range(LEVELS):
                for z, u in us:
                    v = LEVELS * 2 * p + 2 * lv + z
                    if lv == 0:
                        pool.wait_ge(N["atc"], u + 1)
                    if lv >= 2:
                        pool.wait_ge(N["y"], v - 3)
                    nc.gpsimd.tensor_tensor(ctv(lv)[:, z], BT[:, z], heads(levels[:, z, lv, :]), ALU.mult)\
                        .then_inc(N["ct"], 1)

        OT = {n: sig("odd_out_" + n).sem for n in ("squares", "sums", "roots", "merged")}
        osq, oroot = (BT, BX, BXT, BY), (BC, BA, BT, BX)

        def obuf(x, i):
            return x[i].rearrange("p z h c -> p (z h c)")[:, 0:2 * LAT]

        def two_heads(i):
            return mix[:, 2 * i:2 * i + 2, 0:LAT]

        def as_heads(x):
            return x.rearrange("p (h t) -> p h t", h=2)

        def pe_odd_out(pe):
            for i in range(4):
                pe.wait_ge(OT["squares"], i + 1)
                pe.matmul(bank[i][:, :], ones, obuf(osq, i), start=True, stop=True).then_inc(OT["sums"], 1)

        def act_odd_out(act):
            act.wait_ge(N["oc"], 8)
            for i in range(4):
                nc.scalar.activation(as_heads(obuf(osq, i)), two_heads(i), ACT.Square).then_inc(OT["squares"], 1)
            for i in range(4):
                act.wait_ge(OT["sums"], 4 if i >= 2 else i + 1)
                nc.scalar.activation(obuf(oroot, i), bank[i][:, :], ACT.Ln, scale=1.0 / NDV, bias=eps_col)\
                    .then_inc(OT["roots"], 1)
            for i in range(4):
                act.wait_ge(OT["roots"], i + 1)
                nc.scalar.activation(obuf(oroot, i), obuf(oroot, i), ACT.Exp, scale=-0.5).then_inc(OT["roots"], 1)

        def dve_odd_out(dve):
            for i in range(4):
                dve.wait_ge(OT["roots"], 4 + i + 1)
                link(dve, nc.vector.scalar_tensor_tensor(out=two_heads(i), in0=two_heads(i), scalar=vector("gdn_o_norm"),
                                                         in1=as_heads(obuf(oroot, i)), op0=ALU.mult, op1=ALU.mult))
                nc.vector.tensor_tensor(two_heads(i), two_heads(i), sg[:, 2 * i:2 * i + 2, :], ALU.mult)\
                    .then_inc(OT["merged"], 1)

        odd_out = Projection(d["gdn_w_out"][0], KB, KB, LAT, lambda k: mix[:, k, 0:LAT], evac_dve)
        odd_res = Residual(odd_out, 1, 0)
        mlp1 = Mlp(1, LAT)
        final = Norm(lambda k: h[:, k, 0:LAT], lambda k: a[:, k, 0:LAT], KB, LAT, D)

        def pe_layer1(pe):
            ada_c.pe(pe)
            n3.norm.pe_sums(pe)
            pe_odd_in(pe)
            for p in range(4):
                pe_pair(pe, p)
            pe_odd_out(pe)
            pe.wait_ge(OT["merged"], 4)
            odd_out.pe(pe)
            mlp1.norm.norm.pe_sums(pe)
            mlp1.pe(pe)
            final.pe_sums(pe)

        def act_layer1(act):
            ada_c.act(act)
            n3.norm.act_squares(act, squares_ready(mlp0.down.lin.base + KB))
            n3.norm.act_root(act)
            n3.act(act)
            act_odd_in(act)
            for p in range(4):
                act_pair(act, p)
            act_odd_out(act)
            mlp1.norm.norm.act_squares(act, squares_ready(odd_out.lin.base + KB))
            mlp1.norm.norm.act_root(act)
            mlp1.norm.act(act)
            mlp1.act(act)
            final.act_squares(act, squares_ready(mlp1.down.lin.base + KB))
            final.act_root(act)

        def dve_layer1(dve):
            ada_c.dve(dve)
            n3.norm.dve_squares(dve, squares_ready(mlp0.down.lin.base + KB))
            n3.dve(dve)
            dve_odd_in(dve)
            for p in range(4):
                dve_pair(dve, p)
            dve_odd_out(dve)
            odd_res.dve(dve)
            mlp1.norm.norm.dve_squares(dve, squares_ready(odd_out.lin.base + KB))
            mlp1.norm.dve(dve)
            mlp1.dve(dve)
            final.dve_squares(dve, squares_ready(mlp1.down.lin.base + KB))
            final.wait(dve)
            for k in range(KB):
                nc.vector.scalar_tensor_tensor(out=h[:, k, 0:LAT], in0=h[:, k, 0:LAT], scalar=vector("final_norm")[:, k:k + 1],
                                               in1=rstd[:, 0:LAT], op0=ALU.mult, op1=ALU.mult).then_inc(entered.sem, 1)

        def pool_layer1(pool):
            for p in range(4):
                pool_pair(pool, p)

        entered = sig("entered")

        ca = Carve()
        hid2 = ca(F2B, LAT)
        att_room = [ca(T) for _ in range(6)]
        mk, mv = ca(2, 2, NMEM), ca(2, NMEM // P, MEMH * HD)
        shk, shv = ca(4, LAT), ca(2, SKH * HD)
        mq = ca(2, LAT)
        xc, gr, gi, ga, gm, gelu = (ca(LB, LAT) for _ in range(6))
        qs, qswing = xc, gr
        lam8 = ca(3, LB)
        nsink = ca(SQH)
        b2_names = ("mem", "memn", "pre", "post", "scaled", "lr_c", "lr_g", "lr_a", "lr_m", "lr_s", "rot", "roped", "small", "ffn", "kvn")
        B = {n: sig("b2_" + n) for n in b2_names}
        mem = [h[:, k, LAT:T] for k in range(KB)]
        memn = [a[:, k, LAT:T] for k in range(KB)]
        mem_norm = Norm(lambda k: mem[k], lambda k: memn[k], KB, NMEM, D)

        class Weighted:

            def __init__(self, w):
                self.w = w
                self.norm = Norm(lambda k: h[:, k, 0:LAT], lambda k: a[:, k, 0:LAT], KB, LAT, D)
                self.base = B["pre"].take(KB)

            def dve(self, dve):
                self.norm.wait(dve)
                for k in range(KB):
                    nc.vector.scalar_tensor_tensor(out=a[:, k, 0:LAT], in0=h[:, k, 0:LAT], scalar=self.w[:, k:k + 1],
                                                   in1=rstd[:, 0:LAT], op0=ALU.mult, op1=ALU.mult).then_inc(B["pre"].sem, 1)

            def ready(self, pe, k):
                pe.wait_ge(B["pre"].sem, self.base + k + 1)

        class Post:

            def __init__(self, proj, w):
                self.proj, self.w = proj, w
                self.norm = Norm(lambda k: a[:, k, 0:LAT], lambda k: mix[:, k, LAT:T], KB, LAT, D)
                self.base = B["post"].take(KB)

            def act_copies(self, act):
                with act.Fori(0, KB // 2) as i:
                    for u in range(2):
                        n = i * 2 + u
                        act.wait_ge(block_done.sem, self.proj.done(n))
                        nc.scalar.activation(a[:, bass.ds(n, 1), 0:LAT].rearrange("p o t -> p (o t)"),
                                             self.proj.lin.bank(u)[:, 0:LAT], ACT.Copy).then_inc(evac_act.sem, 1)

            def copied(self, eng, k):
                if k < 2:
                    eng.wait_ge(evac_act.sem, self.proj.lin.base + KB)

            def act(self, act):
                self.act_copies(act)
                self.norm.act_squares(act, self.copied)
                self.norm.act_root(act)

            def dve(self, dve):
                self.norm.dve_squares(dve, self.copied)
                self.norm.wait(dve)
                for k in range(KB):
                    link(dve, nc.vector.scalar_tensor_tensor(out=a[:, k, 0:LAT], in0=a[:, k, 0:LAT], scalar=self.w[:, k:k + 1],
                                                             in1=rstd[:, 0:LAT], op0=ALU.mult, op1=ALU.mult))
                    nc.vector.tensor_tensor(h[:, k, 0:LAT], h[:, k, 0:LAT], a[:, k, 0:LAT], ALU.add)\
                        .then_inc(B["post"].sem, 1)

            def ready(self, eng, k):
                eng.wait_ge(B["post"].sem, self.base + k + 1)

        class Blocks:

            def __init__(self, weight, tile_cols, blocks, rhs):
                self.tiles = [Tiles(1, lambda t, c0=c0, n=n: cols_of(weight, c0, n), KB, n) for c0, n in tile_cols]
                self.blocks, self.rhs = blocks, rhs
                self.lin = Linear(evac_act, len(blocks))

            def sync(self, n):
                t = self.blocks[n][0]
                b = sum(x[0] == t for x in self.blocks[:n])
                return t, b, n + 1 == len(self.blocks) or self.blocks[n + 1][0] != t

            def pe(self, pe, ready=None):
                for n, (t, c0, m, dst, _) in enumerate(self.blocks):
                    t, b, last = self.sync(n)
                    if b == 0:
                        self.tiles[t].wait(pe, 0)
                    w = self.tiles[t].view(0)
                    self.lin.free(pe, n)
                    o = self.lin.bank(n)
                    before = (lambda k: ready(pe, k)) if n == 0 and ready else None
                    if m is None:
                        ins = product(pe, o[:, 0:256], lambda k: self.rhs(k)[:, c0 * P:(c0 + 1) * P], lambda k: w[:, k, 0:256],
                                      KB, before=before)
                    elif m == P:
                        ins = product(pe, o[:, 0:LAT], lambda k: w[:, k, c0:c0 + P], self.rhs, KB, before=before)
                    else:
                        for x in range(2):
                            c = c0 + (1 - x) * HD
                            ins = product(pe, o[half(x), 0:LAT], lambda k: w[:, k, c:c + HD], self.rhs, KB, before=before)
                    ins.then_inc(block_done.sem, UNITS - b if last else 1)

            def done(self, n):
                t, b, last = self.sync(n)
                return self.tiles[t].done(0, UNITS - 1 if last else b)

            def act(self, act, n, **how):
                act.wait_ge(block_done.sem, self.done(n))
                nc.scalar.activation(self.blocks[n][3], self.lin.bank(n)[:, 0:LAT], self.blocks[n][4], **how)\
                    .then_inc(evac_act.sem, 1)

        mem_blocks = [Blocks(d["w_mem_kv_2"][l], [(0, 256), (256, 256)],
                             [(0, 0, P, mk[:, l, 0, :], ACT.Copy), (0, P, P, mk[:, l, 1, :], ACT.Copy),
                              (1, 0, None, mv[:, l, 0, :], ACT.Copy), (1, 1, None, mv[:, l, 1, :], ACT.Copy)],
                             lambda k: memn[k]) for l in range(2)]
        pre_a = Weighted(vector("norm_mix_pre_2")[:, 0:KB])
        xa = lambda k: a[:, k, 0:LAT]
        in_a = Blocks(d["w_in_a_2"][0], [(256 * j, 256) for j in range(7)],
                      [(n // 2, (n % 2) * P, P, dst, f) for n, (dst, f) in enumerate(
                          [(xc[:, i, :], ACT.Identity) for i in range(LB)] + [(gelu[:, i, :], ACT.Gelu_apprx_tanh) for i in range(LB)]
                          + [(mq[:, i, :], ACT.Copy) for i in range(2)])], xa)
        gate_tiles = [Tiles(1, lambda t, w=w: d[w][0].rearrange("h i j -> i h j"), LB, P) for w in ("w_gate_r_2", "w_gate_i_2")]
        gate_lin = Linear(evac_act, 2 * LB)

        def memory_units(l):
            return [dict(q=mq[half(hd % 2), hd // 2, q:q + P], k=mk[half(hd % 2), l, hd // 2, :],
                         v=[mv[:, l, b, hd * HD:(hd + 1) * HD] for b in range(2)], rows=half(hd % 2),
                         out=mix[half(hd % 2), 6 + hd // 2, q:q + P]) for hd in range(MEMH) for q in (0, P)]

        mem_att_a = Attention(memory_units(0), HD ** -0.5, att_room)

        class Ffn:

            def __init__(self, l):
                self.pre = Weighted(vector("norm_ffn_pre_2")[:, l * KB:(l + 1) * KB])
                w = d["w_ffn_in_2"][l].rearrange("(k p) c -> p k c", p=P)
                self.up = Projection(None, KB, 2 * F2B, LAT, xa, evac_dve, banks=4,
                                     source=lambda t: w[:, :, bass.ds(256 * (t // 2) + FF2 * (t % 2), 256)])
                self.up.tiles.source_in = lambda i, t: w[:, :, bass.ds(512 * i + 256 * (t // 2) + FF2 * (t % 2), 256)]
                self.down = Projection(d["w_ffn_out_2"][l], F2B, KB, LAT, lambda k: hid2[:, k, :], evac_act, split=2)
                self.post = Post(self.down, vector("norm_ffn_post_2")[:, l * KB:(l + 1) * KB])
                self.silus = B["ffn"].take(F2B)

            def pe(self, pe):
                self.pre.norm.pe_sums(pe)
                self.up.pe(pe, lambda k: self.pre.ready(pe, k))
                pe.wait_ge(evac_dve.sem, self.up.lin.base + 2 * F2B)
                self.down.pe(pe)
                self.post.norm.pe_sums(pe)

            def act(self, act, ready):
                self.pre.norm.act_squares(act, ready)
                self.pre.norm.act_root(act)
                with act.Fori(0, F2B // 2) as i:
                    for u in range(2):
                        act.wait_ge(block_done.sem, self.up.done(i * 4 + u))
                        act.wait_ge(evac_dve.sem, i * 4 + (self.up.lin.base - 3 + 3 * u))
                        nc.scalar.activation(tmp[:, u, 0:LAT], bank[u][:, 0:LAT], ACT.Silu).then_inc(B["ffn"].sem, 1)
                self.post.act(act)

            def dve(self, dve, ready):
                self.pre.norm.dve_squares(dve, ready)
                self.pre.dve(dve)
                with dve.Fori(0, F2B // 2) as i:
                    for u in range(2):
                        n = i * 2 + u
                        dve.wait_ge(B["ffn"].sem, n + (self.silus + 1))
                        dve.wait_ge(block_done.sem, self.up.done(i * 4 + (2 + u)))
                        nc.vector.tensor_tensor(hid2[:, bass.ds(n, 1), :].rearrange("p o t -> p (o t)"), tmp[:, u, 0:LAT],
                                                bank[2 + u][:, 0:LAT], ALU.mult).then_inc(evac_dve.sem, 1 + 2 * u)
                self.post.dve(dve)

        out_a = Projection(d["w_out_2"][0], KB, KB, LAT, lambda k: mix[:, k, 0:LAT], evac_act)
        post_a = Post(out_a, vector("norm_mix_post_2")[:, 0:KB])
        ffn_a = Ffn(0)
        pre_kv = Weighted(vector("norm_kv_2"))
        kv_sh = Blocks(d["w_kv_shared_2"], [(0, 256), (256, 256)],
                       [(0, 0, P, shk[:, 0, :], ACT.Copy), (0, P, P, shk[:, 1, :], ACT.Copy),
                        (0, 0, HD, shk[:, 2, :], ACT.Copy), (0, P, HD, shk[:, 3, :], ACT.Copy),
                        (1, 0, None, shv[:, 0, :], ACT.Copy), (1, 1, None, shv[:, 1, :], ACT.Copy)], xa)
        pre_b = Weighted(vector("norm_mix_pre_2")[:, KB:2 * KB])
        in_b = Blocks(d["w_in_b_2"][0], [(256 * j, 256) for j in range(4)],
                      [(n // 2, (n % 2) * P, P, dst, ACT.Copy) for n, dst in enumerate(
                          [qs[:, i, :] for i in range(6)] + [mq[:, i, :] for i in range(2)])], xa)
        window = table("window")
        sinks = vector("sinks_2")
        swa_units = []
        for hd in range(SQH):
            kv, par = hd // (SQH // SKH), hd % 2
            kx = kv // 2 + (0 if kv % 2 == par else 2)
            for qb in range(2):
                nk = (qb + 1) * P
                swa_units.append(dict(q=qs[half(par), hd // 2, qb * P:(qb + 1) * P], k=shk[half(par), kx, 0:nk],
                                      v=[shv[:, b, kv * HD:(kv + 1) * HD] for b in range(qb + 1)], rows=half(par),
                                      out=mix[half(par), hd // 2, qb * P:(qb + 1) * P], mask=window[:, 2 * P - nk:2 * P],
                                      sink=(sinks[:, hd:hd + 1], nsink[:, hd:hd + 1])))
        att_b = Attention(swa_units + memory_units(1), HD ** -0.5, att_room)
        out_b = Projection(d["w_out_2"][1], KB, KB, LAT, lambda k: mix[:, k, 0:LAT], evac_act)
        post_b = Post(out_b, vector("norm_mix_post_2")[:, KB:2 * KB])
        ffn_b = Ffn(1)
        scos, ssin = table("swa_rope")[:, 0:LAT], table("swa_rope")[:, LAT:2 * LAT]
        srot = table("swa_rope")[:, 2 * LAT:2 * LAT + P]

        def pe_rotate(pe, x, groups, base, evac_total):
            pe.wait_ge(evac_act.sem, evac_total)
            for g in range(groups):
                pe.matmul(bank[2 + g][:, :], srot, x[:, 2 * g:2 * g + 2, :], start=True, stop=True).then_inc(B["rot"].sem, 1)

        def dve_rotate(dve, x, groups, base):
            cos = scos.rearrange("p (o t) -> p o t", o=1).broadcast_to((P, 2, LAT))
            sin = ssin.rearrange("p (o t) -> p o t", o=1).broadcast_to((P, 2, LAT))
            for g in range(groups):
                y = x[:, 2 * g:2 * g + 2, :]
                s = tmp[:, g % 2, :].rearrange("p (h t) -> p h t", h=2)
                dve.wait_ge(B["rot"].sem, base + g + 1)
                nc.vector.tensor_tensor(s, bank[2 + g][:, :].rearrange("p (h t) -> p h t", h=2), sin, ALU.mult)
                link(dve, nc.vector.tensor_tensor(y, y, cos, ALU.mult))
                ins = nc.vector.tensor_tensor(y, y, s, ALU.add)
                ins.then_inc(B["roped"].sem, 1)
                dve.wait_ge(B["roped"].sem, base + g + 1)

        def entered_ready(eng, k):
            eng.wait_ge(entered.sem, k + 1)

        def pe_second(pe):
            mem_norm.pe_sums(pe)
            pe.wait_ge(B["memn"].sem, KB)
            for m in mem_blocks:
                m.pe(pe)
            pre_a.norm.pe_sums(pe)
            in_a.pe(pe, pre_a.ready)
            for j in range(2):
                gate_tiles[j].wait(pe, 0)
                for n in range(LB):
                    if j == 0:
                        pe.wait_ge(B["lr_c"].sem, n + 1)
                    gate_lin.free(pe, LB * j + n)
                    pe.matmul(gate_lin.bank(LB * j + n)[:, 0:LAT], gate_tiles[j].view(0)[:, n, :], xc[:, n, :],
                              start=True, stop=True).then_inc(block_done.sem, 1 if n + 1 < LB else UNITS - LB + 1)
            mem_att_a.pe(pe, lambda pe, i: None)
            pe.wait_ge(B["lr_s"].sem, 1)
            pe.wait_ge(att_out.sem, mem_att_a.b[att_out.sem] + 8)
            out_a.pe(pe)
            post_a.norm.pe_sums(pe)
            ffn_a.pe(pe)
            pre_kv.norm.pe_sums(pe)
            kv_sh.pe(pe, pre_kv.ready)
            pe_rotate(pe, shk, 2, 0, kv_sh.lin.base + 6)
            pre_b.norm.pe_sums(pe)
            in_b.pe(pe, pre_b.ready)
            pe_rotate(pe, qs, 3, 2, in_b.lin.base + 8)
            att_b.pe(pe, lambda pe, i: pe.wait_ge(B["roped"].sem, 5) if i == 0 else None)
            pe.wait_ge(att_out.sem, att_b.b[att_out.sem] + len(att_b.units))
            out_b.pe(pe)
            post_b.norm.pe_sums(pe)
            ffn_b.pe(pe)

        def act_second(act):
            mem_norm.act_squares(act, lambda e, k: e.wait_ge(B["mem"].sem, 16))
            mem_norm.act_root(act)
            for m in mem_blocks:
                for n in range(4):
                    m.act(act, n)
            pre_a.norm.act_squares(act, entered_ready)
            pre_a.norm.act_root(act)
            cw = vector("conv_w_2").rearrange("p (t n) -> p t n", t=4)
            for n in range(LB):
                act.wait_ge(block_done.sem, in_a.done(n))
                nc.scalar.activation(xc[:, n, :], in_a.lin.bank(n)[:, 0:LAT], ACT.Identity, scale=cw[:, 3, n:n + 1],
                                     bias=vector("conv_b_2")[:, n:n + 1]).then_inc(B["scaled"].sem, 1)
                act.wait_ge(B["lr_c"].sem, n + 1)
                act.sem_inc(evac_act.sem, 1)
            for n in range(LB, 2 * LB + 2):
                in_a.act(act, n)
            nc.scalar.activation(lam8[:, 0, :], vector("lru_lambda_2"), ACT.Abs).then_inc(B["small"].sem, 1)
            act.wait_ge(B["small"].sem, 1)
            nc.scalar.activation(lam8[:, 0, :], lam8[:, 0, :], ACT.Exp, scale=-1.0).then_inc(B["small"].sem, 1)
            act.wait_ge(B["small"].sem, 2)
            nc.scalar.activation(lam8[:, 0, :], lam8[:, 0, :], ACT.Ln, bias=1.0).then_inc(B["small"].sem, 1)
            for j, (dst, name) in enumerate(((gr, "b_gate_r_2"), (gi, "b_gate_i_2"))):
                for n in range(LB):
                    act.wait_ge(block_done.sem, gate_tiles[j].done(0, n if n + 1 < LB else UNITS - 1))
                    nc.scalar.activation(dst[:, n, :], gate_lin.bank(LB * j + n)[:, 0:LAT], ACT.Sigmoid,
                                         bias=vector(name)[:, n:n + 1]).then_inc(evac_act.sem, 1)
            act.wait_ge(B["small"].sem, 4)
            act.wait_ge(evac_act.sem, gate_lin.base + 2 * LB)
            for n in range(LB):
                nc.scalar.activation(ga[:, n, :], gr[:, n, :], ACT.Exp, scale=lam8[:, 1, n:n + 1])
                nc.scalar.activation(gm[:, n, :], gr[:, n, :], ACT.Exp, scale=lam8[:, 2, n:n + 1]).then_inc(B["lr_a"].sem, 1)
            act.wait_ge(B["lr_m"].sem, 1)
            nc.scalar.activation(gm[:, :, :], gm[:, :, :], ACT.Sqrt).then_inc(B["lr_g"].sem, 1)
            mem_att_a.act(act)
            post_a.act(act)
            ffn_a.act(act, post_a.ready)
            pre_kv.norm.act_squares(act, ffn_a.post.ready)
            pre_kv.norm.act_root(act)
            for n in range(6):
                kv_sh.act(act, n)
            pre_b.norm.act_squares(act)
            pre_b.norm.act_root(act)
            for n in range(8):
                in_b.act(act, n)
            att_b.act(act)
            post_b.act(act)
            ffn_b.act(act, post_b.ready)

        def dve_second(dve):
            mem_norm.dve_squares(dve, lambda e, k: e.wait_ge(B["mem"].sem, 16))
            mem_norm.wait(dve)
            for k in range(KB):
                nc.vector.scalar_tensor_tensor(out=memn[k], in0=mem[k], scalar=vector("mem_norm_2")[:, k:k + 1],
                                               in1=rstd[:, 0:LAT], op0=ALU.mult, op1=ALU.mult).then_inc(B["memn"].sem, 1)
            pre_a.norm.dve_squares(dve, entered_ready)
            pre_a.dve(dve)
            cw = vector("conv_w_2").rearrange("p (t n) -> p t n", t=4)
            for n in range(LB):
                dve.wait_ge(B["scaled"].sem, n + 1)
                x = in_a.lin.bank(n)[:, 0:LAT]
                for s in (1, 2, 3):
                    ins = nc.vector.scalar_tensor_tensor(out=xc[:, n, s:], in0=x[:, 0:LAT - s], scalar=cw[:, 3 - s, n:n + 1],
                                                         in1=xc[:, n, s:], op0=ALU.mult, op1=ALU.add)
                    if s < 3:
                        link(dve, ins)
                ins.then_inc(B["lr_c"].sem, 1)
            dve.wait_ge(B["small"].sem, 3)
            link(dve, nc.vector.tensor_scalar(lam8[:, 2, :], vector("lru_lambda_2"), 0.0, None, ALU.min))
            link(dve, nc.vector.tensor_tensor(lam8[:, 2, :], lam8[:, 2, :], lam8[:, 0, :], ALU.subtract))
            nc.vector.tensor_scalar(lam8[:, 1, :], lam8[:, 2, :], 8.0, None, ALU.mult)
            link(dve, nc.vector.tensor_scalar(lam8[:, 2, :], lam8[:, 2, :], 16.0, None, ALU.mult))
            nc.vector.tensor_scalar(nsink, sinks, -1.0, None, ALU.mult).then_inc(B["small"].sem, 1)
            dve.wait_ge(evac_act.sem, gate_lin.base + 2 * LB)
            link(dve, nc.vector.tensor_tensor(gi[:, :, :], gi[:, :, :], xc[:, :, :], ALU.mult))
            dve.wait_ge(B["lr_a"].sem, LB)
            link(dve, nc.vector.tensor_scalar(gm[:, :, :], gm[:, :, :], -1.0, 1.0, ALU.mult, ALU.add))
            nc.vector.tensor_scalar(gm[:, :, :], gm[:, :, :], 0.0, None, ALU.max).then_inc(B["lr_m"].sem, 1)
            dve.wait_ge(B["lr_g"].sem, 1)
            link(dve, nc.vector.memset(gm[:, :, 0:1], 1.0))
            link(dve, nc.vector.tensor_tensor(gi[:, :, :], gi[:, :, :], gm[:, :, :], ALU.mult))
            for n in range(LB):
                ins = nc.vector.tensor_tensor_scan(gr[:, n, :], ga[:, n, :], gi[:, n, :], 0.0, ALU.mult, ALU.add)
            link(dve, ins)
            nc.vector.tensor_tensor(mix[:, 0:LB, 0:LAT], gr[:, :, :], gelu[:, :, :], ALU.mult).then_inc(B["lr_s"].sem, 1)
            mem_att_a.dve(dve)
            post_a.dve(dve)
            ffn_a.dve(dve, post_a.ready)
            pre_kv.norm.dve_squares(dve, ffn_a.post.ready)
            pre_kv.dve(dve)
            dve_rotate(dve, shk, 2, 0)
            pre_b.norm.dve_squares(dve)
            pre_b.dve(dve)
            dve_rotate(dve, qs, 3, 2)
            att_b.dve(dve)
            post_b.dve(dve)
            ffn_b.dve(dve, post_b.ready)

        def sp_end(sp):
            for k in range(0, KB, 4):
                sp.wait_ge(B["post"].sem, ffn_b.post.base + k + 4)
                sp.dma_start(out[:, k:k + 4, :], h[:, k:k + 4, 0:LAT]).then_inc(stored.sem, 16)
            sp.wait_ge(stored.sem, 32)

        stored = sig("stored")


        def sp_tiles(sp, g):
            def load(t, body=0, src=None):
                at = g.first + t
                if at >= SLOTS:
                    sp.wait_ge(block_done.sem, UNITS * (at - SLOTS + 1) + UNITS * SLOTS * body)
                sp.dma_start(g.view(t), g.source(t) if src is None else src).then_inc(here[at % SLOTS].sem, 16)

            bodies = g.n // SLOTS if g.loop else 0
            if bodies:
                with sp.Fori(0, bodies) as i:
                    for t in range(SLOTS):
                        load(t, i, g.source_in(i, t))
            for t in range(SLOTS * bodies, g.n):
                load(t)

        block = ctx.enter_context(nc.Block())

        @block.sync
        def _(sp):
            sp.dma_start(vec[:, :], d["vec"]).then_inc(loaded.sem, 16)
            sp.dma_start(h[:, :, :], d["xt"]).then_inc(loaded.sem, 16)
            sp.dma_start(tab[:, :], d["tab"]).then_inc(loaded.sem, 16)
            sp.dma_start(glg[:, :, :], d["glg"]).then_inc(loaded.sem, 16)
            for group in Tiles.every:
                if group is mem_blocks[0].tiles[0]:
                    sp.wait_ge(normed.sem, n3.normed + KB)
                    sp.wait_ge(scaled.sem, n3.scaled + KB)
                    sp.dma_start(h[:, :, LAT:T], d["memt"]).then_inc(B["mem"].sem, 16)
                sp_tiles(sp, group)
            sp_end(sp)


        @block.gpsimd
        def _(pool):
            pool_glow_ones(pool)
            pool_shared_key(pool)
            pool_layer1(pool)

        @block.scalar
        def _(act):
            act_silu_c(act)
            n1.norm.act_squares(act)
            ada_a.act(act)
            n1.norm.act_root(act)
            n1.act(act)
            act_even_in(act)
            norm_q.act_squares(act)
            norm_q.act_root(act)
            norm_kv.act_squares(act)
            norm_kv.act_root(act)
            act_mla_project(act)
            mla.act(act)
            act_gla(act)
            act_rest0(act)
            act_layer1(act)
            act_second(act)

        @block.vector
        def _(dve):
            dve.wait_ge(loaded.sem, 16 * SMALL)
            n1.norm.dve_squares(dve)
            ada_a.dve(dve)
            n1.dve(dve)
            norm_q.dve_squares(dve, lambda e, k: e.wait_ge(evac_act.sem, even_lin.base + 5))
            dve_ranks(dve)
            dve_rope(dve)
            mla.dve(dve)
            dve_gla(dve)
            dve_rest0(dve)
            dve_layer1(dve)
            dve_second(dve)

        @block.tensor
        def _(pe):
            pe.wait_ge(loaded.sem, 16 * SMALL)
            n1.norm.pe_sums(pe)
            ada_a.pe(pe)
            pe_even_in(pe)
            norm_q.pe_sums(pe)
            norm_kv.pe_sums(pe)
            pe_mla_project(pe)
            pe_mla(pe)
            pe_gla(pe)
            pe_rest0(pe)
            pe_layer1(pe)
            pe_second(pe)


SMALL = 4
WEIGHTS = ["ada_w", "mlp_w1", "mlp_w2", "even_w_in", "mla_w_uq", "mla_w_ukv", "even_w_out", "gdn_w_in", "gdn_w_out",
           "w_mem_kv_2", "w_in_a_2", "w_gate_r_2", "w_gate_i_2", "w_kv_shared_2", "w_in_b_2", "w_out_2",
           "w_ffn_in_2", "w_ffn_out_2"]


def feature_major(v):
    v = np.asarray(v)
    v = v.reshape(-1, v.shape[-1] // P, P) if v.shape[-1] % P == 0 else v.reshape(-1, 1, P)
    return np.ascontiguousarray(v.transpose(2, 0, 1).reshape(P, -1))


def laid_out(inputs):
    cols = []
    for name, n in VECTORS:
        if name == "c":
            v = np.stack([np.asarray(inputs["c"])[0], np.asarray(inputs["c_ctx"])])
            v = feature_major(v).reshape(P, 2, KB).transpose(0, 2, 1).reshape(P, -1)
        elif name in ("gdn_a_log", "gdn_dt_bias", "sinks_2"):
            v = np.repeat(np.asarray(inputs[name]).reshape(1, -1), P, 0)
        elif name == "eps":
            v = np.full((P, 1), EPS, np.float32)
        elif name in ("c_ctx",):
            continue
        else:
            v = feature_major(inputs[name])
        assert v.shape == (P, n), (name, v.shape, n)
        cols.append(v)
    maps = {"vec": np.ascontiguousarray(np.concatenate(cols, 1))}
    tokens = np.concatenate([np.asarray(inputs["x"])[0], np.asarray(inputs["ctx"])[0]], 0)
    maps["xt"] = np.ascontiguousarray(tokens.T.reshape(KB, P, T).transpose(1, 0, 2))
    maps["memt"] = np.ascontiguousarray(np.asarray(inputs["mem_2"])[0].T.reshape(KB, P, NMEM).transpose(1, 0, 2))
    maps["tab"] = np.ascontiguousarray(np.concatenate([TABLES[n] for n in TABLES], 1))
    up, bias = np.asarray(inputs["gla_gate_up"])[0], np.asarray(inputs["gla_gate_bias"])[0]
    maps["glg"] = np.ascontiguousarray(np.concatenate([up, bias[:, None, :]], 1).transpose(1, 0, 2))
    for name in WEIGHTS:
        maps[name] = np.ascontiguousarray(inputs[name])
    return maps


def kernel(**inputs):
    import concourse.bacc as bacc
    from concourse.bass_utils import run_bass_kernel_spmd

    nc = bacc.Bacc("TRN2", target_bir_lowering=False, num_devices=1)
    arrays = laid_out(inputs)
    d = {n: nc.dram_tensor(n, v.shape, mybir.dt.from_np(v.dtype), kind="ExternalInput").ap() for n, v in arrays.items()}
    out = nc.dram_tensor("out_t", (P, KB, LAT), F32, kind="ExternalOutput").ap()
    two_block_kernel(nc, d, out)
    r = run_bass_kernel_spmd(nc, [arrays], core_ids=[0])
    got = r.results[0]["out_t"]
    return np.ascontiguousarray(got.transpose(2, 1, 0).reshape(1, LAT, D))
```

```python
import numpy as np
import concourse.bass as bass
from concourse import mybir
from contextlib import ExitStack

F32 = mybir.dt.float32
F32R = mybir.dt.float32r
ALU = mybir.AluOpType
ACT = mybir.ActivationFunctionType
AX = mybir.AxisListType

P = 128
D = 1024
KB = D // P
LAT = 256
CTX = 256
T = LAT + CTX
TB = T // P
NMOD = 6
FF = 4 * D
FB = FF // P
EPS = 1e-6

MH, NOPE, ROPE, MV = 8, 64, 32, 64
MQK = NOPE + ROPE
QR, KVR = 3 * D // 8, D // 4
QB, KVB = QR // P, KVR // P
GH, GDK, GDV, GRANK = 4, 64, 128, 16
GFB = GH * GDK // P
C = 64
NCH = T // C
E_KV, E_KPE = QR, QR + KVR
E_GQ = E_KPE + ROPE
E_GK = E_GQ + GH * GDK
E_GV = E_GK + GH * GDK
E_GG = E_GV + GH * GDV
E_GLOW = E_GG + GH * GDV
EVEN_IN = E_GLOW + 2 * GRANK

NH, NDK, NDV = 8, 64, 128
QKB = NH * NDK // P
VB = NH * NDV // P
O_G = 2 * NH * NDK + NH * NDV
O_AB = O_G + NH * NDV
ODD_IN = O_AB + 4 * NH
NPAIR = 2

HD = 64
LW = 768
LB = LW // P
MEMH = 4
NMEM = 256
SQH, SKH = 12, 4
FF2 = 2816
F2B = FF2 // P
A_IN = 2 * LW + MEMH * HD
B_IN = SQH * HD + MEMH * HD

RAW = 4
AHEAD = 4
TILE = KB * P
UNITS = 12
HIDDEN = 8192
ARENA = 2 * HIDDEN + 2 * KB * T


class Signal:

    def __init__(self, nc, ctx, name):
        self.sem = ctx.enter_context(nc.semaphore(name))
        self.total = 0

    def take(self, n=1):
        base = self.total
        self.total += n
        return base



def constant_tables():
    t = {}
    i = np.arange(P)
    t["ident"] = np.eye(P)
    t["ones"] = np.ones((P, P))
    same = (i[:, None] // C) == (i[None, :] // C)
    t["ones_half"] = same.astype(float)
    t["upto"] = np.stack([same & (i[:, None] <= i[None, :]), same & (i[:, None] >= i[None, :])], 1).reshape(P, -1)
    r, c = (i % C)[:, None], np.arange(C)[None, :]
    t["strict"] = np.stack([c < r, c > r], 1).reshape(P, -1)
    lev = []
    for s in (2, 4, 8, 16, 32):
        pair, jh, ih = (r // (2 * s)) == (c // (2 * s)), (r // s) % 2, (c // s) % 2
        lev.append(np.stack([pair & (jh == 0) & (ih == 1), pair & (jh == 1) & (ih == 0)], 1))
    t["levels"] = np.stack(lev, 2).reshape(P, -1)
    pair = (r // 2) == (c // 2)
    t["pairs"] = np.stack([pair & (c < r), pair & (c > r)], 1).reshape(P, -1)
    t["fold"] = np.concatenate([np.eye(2), np.eye(2), np.zeros((P - 4, 2))], 0)
    t["eye64"] = (r == c).astype(float)
    t["upto64"] = np.stack([r <= c, r >= c], 1).reshape(P, -1)
    nf = ROPE // 4
    inv = 10000.0 ** (-np.arange(0, ROPE // 2, 2, dtype=np.float32) / np.float32(ROPE // 2))
    tok = np.arange(LAT)
    ang = np.stack([(tok // 64).astype(np.float32)[None, :] * inv[:, None],
                    (tok % 64).astype(np.float32)[None, :] * inv[:, None]], 0)
    cos = np.broadcast_to(np.cos(ang)[:, None], (2, 2, nf, LAT)).reshape(ROPE, LAT)
    sin = np.broadcast_to(np.sin(ang)[:, None], (2, 2, nf, LAT)).reshape(ROPE, LAT)
    rot = np.zeros((ROPE, ROPE))
    for a in range(2):
        for f in range(nf):
            x1, x2 = a * 2 * nf + f, a * 2 * nf + nf + f
            rot[x2, x1], rot[x1, x2] = -1.0, 1.0
    m = np.zeros((P, 2 * LAT + ROPE))
    m[64:96] = np.concatenate([cos, sin, rot], 1)
    t["mla_rope"] = m
    half = HD // 8
    inv = (1.0 / (np.float32(500000.0) ** (np.arange(0, 2 * half, 2, dtype=np.float32) / np.float32(2 * half)))).astype(np.float32)
    ang = tok.astype(np.float32)[None, :] * inv[:, None]
    cos, sin, rot = np.ones((P, LAT)), np.zeros((P, LAT)), np.zeros((P, P))
    for h in (0, HD):
        for b in (0, half):
            cos[h + b:h + b + half], sin[h + b:h + b + half] = np.cos(ang), np.sin(ang)
        for f in range(half):
            rot[h + half + f, h + f], rot[h + f, h + half + f] = -1.0, 1.0
    t["swa_rope"] = np.concatenate([cos, sin, rot], 1)
    q, k = i[:, None], i[None, :]
    t["window"] = np.concatenate([np.where(k > q, 0.0, -1e30), np.where(k <= q, 0.0, -1e30)], 1)
    return {n: np.ascontiguousarray(a, dtype=np.float32) for n, a in t.items()}


TABLES = constant_tables()

VECTORS = [("c", 2 * KB), ("ada_b", 2 * NMOD * KB), ("norm1_w", 2 * KB), ("norm2_w", 2 * KB), ("final_norm", KB),
           ("mla_q_norm", QB), ("mla_kv_norm", KVB), ("gla_o_norm", 1), ("gdn_conv_w", 3 * 16), ("gdn_o_norm", 1),
           ("norm_mix_pre_2", 2 * KB), ("norm_mix_post_2", 2 * KB), ("norm_ffn_pre_2", 2 * KB),
           ("norm_ffn_post_2", 2 * KB), ("mem_norm_2", KB), ("conv_w_2", 4 * LB), ("conv_b_2", LB),
           ("b_gate_r_2", LB), ("b_gate_i_2", LB), ("lru_lambda_2", LB), ("norm_kv_2", KB),
           ("gdn_a_log", 16), ("gdn_dt_bias", 16), ("sinks_2", SQH), ("eps", 1)]


def columns(sizes):
    at, out = 0, {}
    for name, n in sizes:
        out[name] = (at, n)
        at += n
    return out, at


VCOL, NVEC = columns(VECTORS)
TURNS = (("mla_rope",), ("strict", "levels", "pairs", "eye64", "upto64"), ("swa_rope", "window"))
LASTING = tuple(n for n in TABLES if not any(n in turn for turn in TURNS))
TCOL, TURN_AT = columns([(n, TABLES[n].shape[1]) for n in LASTING])
TURN_SIZES = []
for turn in TURNS:
    _cols, _n = columns([(n, TABLES[n].shape[1]) for n in turn])
    TCOL.update({n: (at + TURN_AT, size) for n, (at, size) in _cols.items()})
    TURN_SIZES.append(_n)
NTAB = TURN_AT + max(TURN_SIZES)


def two_block_kernel(nc, d, out):
    ctx = ExitStack()
    with ctx:
        def sb(name, shape, dtype=F32):
            return ctx.enter_context(nc.sbuf_tensor(name, shape, dtype))

        def sig(name):
            return Signal(nc, ctx, name)

        tab = sb("tables", [P, NTAB])
        vec = sb("vectors", [P, NVEC])
        ring = sb("ring", [P, RAW, TILE])
        w_hi = sb("weights_hi", [P, AHEAD, TILE], F32R)
        w_lo = sb("weights_lo", [P, AHEAD, TILE], F32R)
        h = sb("h", [P, KB, T])
        a = sb("a", [P, KB, T])
        mix = sb("mix", [P, KB, T])
        mod = sb("mod", [P, 2, NMOD * KB, 2])
        gain = sb("gain", [P, 2, 2, KB, 2])
        silu_c = sb("silu_c", [P, KB, 2])
        rstd = sb("rstd", [P, T])
        tmp = sb("tmp", [P, 2, T])
        with nc.sbuf_tensor("arena", [P, ARENA], F32) as arena:
            pass
        hid_hi = sb("hidden_hi", [P, HIDDEN], F32R)
        hid_lo = sb("hidden_lo", [P, HIDDEN], F32R)
        x_hi = sb("x_hi", [P, KB, T], F32R)
        x_lo = sb("x_lo", [P, KB, T], F32R)
        c_split = hid_lo[:, HIDDEN - KB * 4 - P:HIDDEN]
        ada_at = 2 * HIDDEN - KB * 4 - P - 512
        ada_row = arena[0:4, ada_at:ada_at + 512].rearrange("p (b c) -> p b c", b=2)
        bank = [ctx.enter_context(nc.psum_tensor(f"bank{i}", [P, 512], F32)) for i in range(8)]
        BSUM, BADA = bank[4], bank[5]

        def table(name):
            at, n = TCOL[name]
            return tab[:, at:at + n]

        def vector(name):
            at, n = VCOL[name]
            return vec[:, at:at + n]

        ident, ones, ones_half = table("ident"), table("ones"), table("ones_half")
        upto = table("upto").rearrange("p (z i) -> p z i", z=2)

        class Carve:

            def __init__(self):
                self.at = 0

            def __call__(self, *shape):
                n = int(np.prod(shape))
                v = arena[:, self.at:self.at + n]
                self.at += n
                assert self.at <= ARENA, self.at
                if len(shape) == 1:
                    return v
                names = "abcdef"[:len(shape)]
                return v.rearrange(f"p ({' '.join(names)}) -> p {' '.join(names)}",
                                   **{x: s for x, s in zip(names[1:], shape[1:])})

        loaded = sig("loaded")
        here = [sig(f"weights_here{s}") for s in range(RAW)]
        hi_done = [sig(f"weights_hi{s}") for s in range(AHEAD)]
        lo_done = [sig(f"weights_lo{s}") for s in range(AHEAD)]
        xh_done, xl_done = sig("x_hi_done"), sig("x_lo_done")
        block_done = sig("block_done")
        evac_act, evac_dve = sig("evac_act"), sig("evac_dve")
        sq_act, sq_dve = sig("squares_act"), sig("squares_dve")
        sums_done, root_done, rstd_done = sig("sums_done"), sig("root_done"), sig("rstd_done")
        gains_done, silu_done = sig("gains_done"), sig("silu_done")
        chain = sig("dve_chain")

        def link(eng, ins):
            chain.total += 1
            ins.then_inc(chain.sem, 1)
            eng.wait_ge(chain.sem, chain.total)

        class Tiles:
            count = 0
            every = []

            def __init__(self, n, source, kb=KB, cols=P):
                self.n, self.source, self.kb, self.cols, self.body = n, source, kb, cols, None
                self.first = Tiles.count
                Tiles.count += n
                Tiles.every.append(self)

            def landing(self, t):
                return ring[:, (self.first + t) % RAW, 0:self.kb * self.cols].rearrange("p (k c) -> p k c", k=self.kb)

            def parts(self, t):
                s, c = (self.first + t) % AHEAD, self.cols
                return tuple((lambda k, x=x: x[:, s, k * c:(k + 1) * c]) for x in (w_hi, w_lo))

            def stationary(self, t):
                s, c = (self.first + t) % AHEAD, self.cols
                return tuple((lambda k, x=x: x[:, s, k * c:k * c + P]) for x in (w_hi, w_lo))

            def two(self, t):
                s = (self.first + t) % AHEAD
                assert s % 2 == 0
                return tuple((lambda k, x=x: x[:, s:s + 2, k * P:(k + 1) * P]) for x in (w_hi, w_lo))

            def wait(self, pe, t, body=None):
                g = self.first + t
                pe.wait_ge(lo_done[g % AHEAD].sem, after(g // AHEAD + 1, body, 1 / AHEAD))

            def done(self, t, block=UNITS - 1):
                return UNITS * (self.first + t) + block + 1

        def after(count, body, each):
            if body is None:
                return count
            step = body[1] * each
            assert step == int(step)
            return body[0] * int(step) + count

        def split_hi(act, g, body=None):
            if body is None and g >= Tiles.count:
                return
            act.wait_ge(here[g % RAW].sem, after(16 * (g // RAW + 1), body, 16 / RAW))
            if g >= AHEAD:
                act.wait_ge(block_done.sem, after(UNITS * (g - AHEAD + 1), body, UNITS))
            nc.scalar.activation(w_hi[:, g % AHEAD, :], ring[:, g % RAW, :], ACT.Copy).then_inc(hi_done[g % AHEAD].sem, 1)

        def split_lo(dve, g, body=None):
            if body is None and g >= Tiles.count:
                return
            dve.wait_ge(hi_done[g % AHEAD].sem, after(g // AHEAD + 1, body, 1 / AHEAD))
            nc.vector.tensor_tensor(w_lo[:, g % AHEAD, :], ring[:, g % RAW, :], w_hi[:, g % AHEAD, :].bitcast(F32),
                                    ALU.subtract).then_inc(lo_done[g % AHEAD].sem, 1)

        def follow(eng, split, tiles):
            for t in range(tiles.n):
                split(eng, tiles.first + t + AHEAD)

        def cols_of(w, c0, n, kb=KB):
            return w[0:kb * P, c0:c0 + n].rearrange("(k p) c -> p k c", p=P)

        def dyn(w, c0, r0=0, kb=KB):
            return w[r0:r0 + kb * P, bass.ds(c0, P)].rearrange("(k p) c -> p k c", p=P)

        class Linear:
            last = None

            def __init__(self, evac, n, banks=2, first=0):
                self.before, self.evac, self.base, self.banks, self.first = Linear.last, evac, evac.take(n), banks, first
                Linear.last = (evac, evac.total)

            def bank(self, n):
                return bank[self.first + n % self.banks]

            def free(self, pe, n, past=None):
                if n == 0 and past is None and self.before is not None:
                    pe.wait_ge(self.before[0].sem, self.before[1])
                if past is not None:
                    pe.wait_ge(self.evac.sem, self.base + n - self.banks + 1 + past)
                elif n >= self.banks:
                    pe.wait_ge(self.evac.sem, self.base + n - self.banks + 1)

        def product(pe, dst, lhs, rhs, nk, start=True, stop=True, before=None):
            for k in range(nk):
                if before is not None:
                    before(k)
                last = pe.matmul(dst, lhs(k), rhs(k), start=start and k == 0, stop=stop and k == nk - 1)
            return last

        def split_product(pe, dst, lhs, rhs, nk, start=True, stop=True, before=None):
            for k in range(nk):
                if before is not None:
                    before(k)
                pe.matmul(dst, lhs[0](k), rhs[0](k), start=start and k == 0, stop=False)
                pe.matmul(dst, lhs[0](k), rhs[1](k), start=False, stop=False)
                last = pe.matmul(dst, lhs[1](k), rhs[0](k), start=False, stop=stop and k == nk - 1)
            return last

        def split_products(pe, dsts, lhss, rhs, nk, ready):
            for k in range(nk):
                ready(k)
                last = [split_product(pe, dst, tuple((lambda _, x=x: x(k)) for x in lhs), tuple((lambda _, x=x: x(k)) for x in rhs),
                                      1, start=k == 0, stop=k == nk - 1) for dst, lhs in zip(dsts, lhss)]
            return last

        class Operand:

            def __init__(self, source, nk, s):
                self.source, self.nk, self.s = source, nk, s
                self.base, self.base_lo = xh_done.take(nk), xl_done.take(nk)

            def view(self, x, k):
                return x[:, k, self.s]

            def act(self, act, k):
                nc.scalar.activation(self.view(x_hi, k), self.source(k), ACT.Copy).then_inc(xh_done.sem, 1)

            def dve(self, dve, k):
                dve.wait_ge(xh_done.sem, self.base + k + 1)
                nc.vector.tensor_tensor(self.view(x_lo, k), self.source(k), self.view(x_hi, k).bitcast(F32), ALU.subtract)\
                    .then_inc(xl_done.sem, 1)

            def ready(self, pe, k):
                pe.wait_ge(xl_done.sem, self.base_lo + k + 1)

        def split_x(width, start=0):
            return tuple((lambda k, x=x: x[:, k, start:start + width]) for x in (x_hi, x_lo))

        class Norm:

            def __init__(self, src, sq, nk, width, features):
                self.src, self.sq, self.nk, self.w, self.n = src, sq, nk, width, features
                self.sa, self.sd = sq_act.take((nk + 1) // 2), sq_dve.take(nk // 2)
                self.sum, self.root, self.rstd = sums_done.take(), root_done.take(), rstd_done.take()

            def act_squares(self, act, ready=None):
                for k in range(0, self.nk, 2):
                    if ready is not None:
                        ready(act, k)
                    nc.scalar.activation(self.sq(k), self.src(k), ACT.Square).then_inc(sq_act.sem, 1)

            def dve_squares(self, dve, ready=None):
                for k in range(1, self.nk, 2):
                    if ready is not None:
                        ready(dve, k)
                    nc.vector.tensor_tensor(self.sq(k), self.src(k), self.src(k), ALU.mult).then_inc(sq_dve.sem, 1)

            def pe_sums(self, pe):
                for k in range(self.nk):
                    if k % 2 == 0:
                        pe.wait_ge(sq_act.sem, self.sa + k // 2 + 1)
                    else:
                        pe.wait_ge(sq_dve.sem, self.sd + k // 2 + 1)
                    last = pe.matmul(BSUM[:, 0:self.w], ones, self.sq(k), start=k == 0, stop=k == self.nk - 1)
                last.then_inc(sums_done.sem, 1)

            def act_root(self, act):
                act.wait_ge(sums_done.sem, self.sum + 1)
                nc.scalar.activation(rstd[:, 0:self.w], BSUM[:, 0:self.w], ACT.Ln, scale=1.0 / self.n,
                                     bias=eps_col).then_inc(root_done.sem, 1)
                act.wait_ge(root_done.sem, self.root + 1)
                nc.scalar.activation(rstd[:, 0:self.w], rstd[:, 0:self.w], ACT.Exp, scale=-0.5)\
                    .then_inc(rstd_done.sem, 1)

            def wait(self, eng):
                eng.wait_ge(rstd_done.sem, self.rstd + 1)

        scaled = sig("scaled")
        eps_col = vec[:, NVEC - 1:NVEC]

        class Modulated:

            def __init__(self, layer, which, width):
                self.l, self.which, self.w = layer, which, width
                self.parts = 2 if width == T else 1
                self.norm = Norm(lambda k: h[:, k, 0:width], lambda k: a[:, k, 0:width], KB, width, D)
                self.scaled, self.hi, self.lo = scaled.take(KB), xh_done.take(KB), xl_done.take(KB)

            def halves(self, k):
                for z in range(self.parts):
                    yield slice(z * LAT, (z + 1) * LAT), z, mod[:, self.l, 3 * self.which * KB + k, z:z + 1]

            def dve(self, dve):
                dve.wait_ge(gains_done.sem, 2 * self.l + self.which + 1)
                self.norm.wait(dve)
                for k in range(KB + 1):
                    if k < KB:
                        for s, z, shift in self.halves(k):
                            ins = nc.vector.scalar_tensor_tensor(
                                out=a[:, k, s], in0=h[:, k, s], scalar=gain[:, self.l, self.which, k, z:z + 1],
                                in1=rstd[:, s], op0=ALU.mult, op1=ALU.mult)
                        ins.then_inc(scaled.sem, 1)
                    if k >= 1:
                        dve.wait_ge(xh_done.sem, self.hi + k)
                        for s, z, shift in self.halves(k - 1):
                            ins = nc.vector.scalar_tensor_tensor(
                                out=x_lo[:, k - 1, s], in0=a[:, k - 1, s], scalar=shift,
                                in1=x_hi[:, k - 1, s].bitcast(F32), op0=ALU.add, op1=ALU.subtract)
                        ins.then_inc(xl_done.sem, 1)

            def act(self, act):
                for k in range(KB):
                    act.wait_ge(scaled.sem, self.scaled + k + 1)
                    for s, z, shift in self.halves(k):
                        ins = nc.scalar.activation(x_hi[:, k, s], a[:, k, s], ACT.Identity, bias=shift)
                    ins.then_inc(xh_done.sem, 1)

            def ready(self, pe, k):
                pe.wait_ge(xl_done.sem, self.lo + k + 1)

        ADA_A = 2 * KB
        ada_a_tiles = Tiles(ADA_A, lambda t: cols_of(d["ada_w"][0], P * t, P))
        c_parts, vec_here = sig("c_parts"), sig("vectors_here")

        def act_silu_c(act):
            act.wait_ge(vec_here.sem, 16)
            nc.scalar.activation(silu_c[:, :, :].rearrange("p k z -> p (k z)"), vector("c"), ACT.Silu)\
                .then_inc(silu_done.sem, 1)
            nc.scalar.activation(c_split[:, :], vec[:, 0:KB * 4 + P], ACT.Copy).then_inc(c_parts.sem, 1)
            act.wait_ge(silu_done.sem, 1)
            act.wait_ge(c_parts.sem, 1)
            nc.scalar.activation(c_view[:, :, 0:2], silu_c[:, :, :], ACT.Copy).then_inc(c_parts.sem, 1)

        def dve_silu_c(dve):
            dve.wait_ge(c_parts.sem, 2)
            nc.vector.tensor_tensor(c_view[:, :, 2:4], silu_c[:, :, :], c_view[:, :, 0:2].bitcast(F32), ALU.subtract)\
                .then_inc(silu_done.sem, 1)

        c_view = c_split[:, 0:KB * 4].rearrange("p (k z) -> p k z", z=4)
        ada_turned = sig("ada_turned")
        fold = table("fold")

        class Ada:

            def __init__(self, tiles, layer, j0, n):
                self.tiles, self.layer, self.j0, self.n = tiles, layer, j0, n
                self.lin = Linear(evac_act, n // 2, 2 if layer == 0 and j0 == 0 else 1, 6 if layer == 0 and j0 == 0 else 4)
                self.turned = ada_turned.take(n // 2)

            def pe_rows(self, pe, t):
                if t == 0:
                    pe.wait_ge(silu_done.sem, 2)
                self.tiles.wait(pe, 2 * t)
                self.tiles.wait(pe, 2 * t + 1)
                self.lin.free(pe, t)
                hi, lo = self.tiles.two(2 * t)
                o = self.lin.bank(t)[:, 0:256].rearrange("p (b c) -> p b c", b=2)
                for k in range(KB):
                    c = c_split[:, 4 * k:4 * k + P]
                    pe.matmul(o, c, hi(k), start=k == 0, stop=False)
                    ins = pe.matmul(o, c, lo(k), start=False, stop=k == KB - 1)
                ins.then_inc(block_done.sem, 2 * UNITS)

            def pe_turn(self, pe, t):
                pe.wait_ge(evac_act.sem, self.lin.base + t + 1)
                for b in range(2):
                    j = self.j0 + 2 * t + b
                    ins = pe.matmul(ada_columns(self.layer, j, 1), ada_row[:, t % 2, b * P:(b + 1) * P], fold[0:4, :],
                                    start=True, stop=True)
                ins.then_inc(ada_turned.sem, 1)

            def pe(self, pe, late):
                for t in range(self.n // 2 + 1):
                    if t == self.n // 2 - 3:
                        late()
                    if t < self.n // 2:
                        self.pe_rows(pe, t)
                    if t == 1:
                        pe.wait_ge(loaded.sem, 16 * SMALL)
                    if t >= 1:
                        self.pe_turn(pe, t - 1)

            def act_row(self, act, t):
                act.wait_ge(block_done.sem, self.tiles.done(2 * t + 1))
                if t >= 2:
                    act.wait_ge(ada_turned.sem, self.turned + t - 1)
                nc.scalar.activation(ada_row[:, t % 2, :], self.lin.bank(t)[0:4, 0:256], ACT.Copy)\
                    .then_inc(evac_act.sem, 1)

            def act(self, act, middle, late):
                for t in range(self.n // 2):
                    if t == 2:
                        middle()
                    if t == self.n // 2 - 1:
                        late()
                    self.act_row(act, t)
                    for b in range(2):
                        split_hi(act, self.tiles.first + 2 * t + b + AHEAD)

            def dve(self, dve, middle):
                for t in range(self.n):
                    if t == 4:
                        middle()
                    split_lo(dve, self.tiles.first + t + AHEAD)
                dve_ada(dve, self.turned + self.n // 2, self.layer, self.j0, self.n)

        def ada_columns(layer, j, n):
            at = 2 * NMOD * KB * layer + 2 * j
            return BADA[:, at:at + 2 * n]

        class Background:

            def __init__(self, adas):
                self.pairs = [(x, t) for x in adas for t in range(x.n // 2)]

            def at(self, s):
                return s // 2 + min((s + 1) // 2, self.extra) if s % 2 == 0 or s // 2 < self.extra else None

            def begin(self, steps):
                self.extra = len(self.pairs) - steps

            def pe(self, pe, s):
                if self.at(s) is not None:
                    self.pe_step(pe, self.at(s))

            def act_empty(self, act, s):
                if self.at(s):
                    self.act_row(act, self.at(s))

            def act_split(self, act, s):
                if self.at(s):
                    self.act_hi(act, self.at(s))

            def dve(self, dve, s):
                if self.at(s):
                    self.dve_lo(dve, self.at(s))

            def pe_step(self, pe, p):
                if p >= 2:
                    x, t = self.pairs[p - 2]
                    x.pe_turn(pe, t)
                if p < len(self.pairs):
                    x, t = self.pairs[p]
                    x.pe_rows(pe, t)

            def act_row(self, act, p):
                x, t = self.pairs[p - 1]
                x.act_row(act, t)

            def act_hi(self, act, p):
                x, t = self.pairs[p - 1]
                for b in range(2):
                    split_hi(act, x.tiles.first + 2 * t + b + AHEAD)

            def dve_lo(self, dve, p):
                x, t = self.pairs[p - 1]
                for b in range(2):
                    split_lo(dve, x.tiles.first + 2 * t + b + AHEAD)

        def dve_ada(dve, turned, layer, j0, n):
            dve.wait_ge(ada_turned.sem, turned)
            bias = vector("ada_b").rearrange("p (l j) -> p l j", l=2)[:, layer, j0:j0 + n]
            link(dve, nc.vector.tensor_tensor(
                mod[:, layer, j0:j0 + n, :], ada_columns(layer, j0, n).rearrange("p (j z) -> p j z", z=2),
                bias.rearrange("p (j o) -> p j o", o=1).broadcast_to((P, n, 2)), ALU.add))
            for which, name in ((0, "norm1_w"), (1, "norm2_w")):
                j = (3 * which + 1) * KB
                if not j0 <= j < j0 + n:
                    continue
                w = vector(name).rearrange("p (l k o) -> p l k o", l=2, o=1)[:, layer].broadcast_to((P, KB, 2))
                nc.vector.scalar_tensor_tensor(out=gain[:, layer, which], in0=mod[:, layer, j:j + KB, :], scalar=1.0,
                                               in1=w, op0=ALU.add, op1=ALU.mult).then_inc(gains_done.sem, 1)

        ada_a = Ada(ada_a_tiles, 0, 0, ADA_A)

        n1 = Modulated(0, 0, T)
        cv = Carve()
        cq, ckv, kpe = cv(QB, T), cv(KVB, T), cv(T)
        gq, gk, gg = cv(GFB, T), cv(GFB, T), cv(GH, T)
        glow = cv(2, T)
        gv = cv(TB, GH * GDV)
        even_at = cv.at
        glow_ones = sig("glow_ones")
        w_even = d["even_w_in"][0]
        even_cols = [P * i for i in range(5)] + [E_KPE - 64] + [E_GQ + P * i for i in range(12)]
        even_tiles = Tiles(18, lambda t: cols_of(w_even, even_cols[t], P))
        glow_tiles = Tiles(2, lambda t: cols_of(w_even, E_GLOW + t * GRANK, GRANK), KB, GRANK)
        even_blocks = [(i, 0, P, (cq, i) if i < QB else (ckv, i - QB)) for i in range(5)] + [(5, 64, ROPE, (kpe, None))]
        even_blocks += [(6, 0, P, (gq, 0)), (7, 0, P, (gq, 1)), (8, 0, P, (gk, 0)), (9, 0, P, (gk, 1))]
        even_blocks += [(10 + 2 * half, 0, 256, (gv, tb)) for half in range(2) for tb in range(TB)]
        even_blocks += [(14 + i, 0, P, (gg, i)) for i in range(4)] + [(18, 0, GRANK, (glow, 0)), (19, 0, GRANK, (glow, 1))]
        even_lin = Linear(evac_act, len(even_blocks))

        def even_sync(n):
            t = even_blocks[n][0]
            b = sum(x[0] == t for x in even_blocks[:n])
            last = n + 1 == len(even_blocks) or even_blocks[n + 1][0] != t
            units = UNITS * (2 if even_blocks[n][3][0] is gv else 1)
            return t, even_tiles.done(t, units - 1 if last else b), units - b if last else 1, last

        def pe_even_in(pe):
            for n in range(2):
                even_tiles.wait(pe, n)
                even_lin.free(pe, n)
            for ins in split_products(pe, [even_lin.bank(n)[:, :] for n in range(2)], [even_tiles.parts(n) for n in range(2)],
                                      split_x(T), KB, lambda k: n1.ready(pe, k)):
                ins.then_inc(block_done.sem, UNITS)
            for n, (t, c0, m, (dst, i)) in enumerate(even_blocks):
                if n < 2:
                    continue
                t, done, inc, last = even_sync(n)
                if even_blocks[n - 1][0] != t:
                    even_tiles.wait(pe, t)
                    if dst is gv:
                        even_tiles.wait(pe, t + 1)
                even_lin.free(pe, n)
                o = even_lin.bank(n)
                if dst is gv:
                    ins = split_product(pe, o[:, 0:256].rearrange("p (b c) -> p b c", b=2), split_x(P, i * P),
                                        even_tiles.two(t), KB)
                else:
                    w = glow_tiles.stationary(i) if dst is glow else even_tiles.parts(t)
                    ins = split_product(pe, o[:, :], w, split_x(T), KB)
                ins.then_inc(block_done.sem, inc)

        def act_even_in(act):
            for n, (t, c0, m, (dst, i)) in enumerate(even_blocks):
                t, done, inc, last = even_sync(n)
                act.wait_ge(block_done.sem, done)
                o = even_lin.bank(n)
                func = ACT.Copy
                if dst is gv:
                    part = (t - 10) // 2
                    o, to = o[:, 0:256], gv[:, i, part * 256:(part + 1) * 256]
                elif dst is kpe:
                    o, to = o[64:64 + ROPE, :], kpe[64:64 + ROPE, :]
                elif dst is glow:
                    if i == 0:
                        act.wait_ge(glow_ones.sem, 1)
                    o, to = o[0:m, :], glow[0:m, i, :]
                else:
                    o, to = o[:, :], dst[:, i, :]
                    func = ACT.Silu if dst is gg else ACT.Copy
                nc.scalar.activation(to, o, func).then_inc(evac_act.sem, 1)
                if last:
                    for b in range(2 if dst is gv else 1):
                        split_hi(act, even_tiles.first + t + b + AHEAD)

        def dve_even_in(dve):
            follow(dve, split_lo, even_tiles)
            follow(dve, split_lo, glow_tiles)

        def pool_glow_ones(pool):
            nc.gpsimd.memset(glow[0:GRANK + 1, :, :], 1.0).then_inc(glow_ones.sem, 1)

        copied = sig("kv_copied")
        ranked = sig("ranked")
        cqn, ckvn = mix[:, 0:QB, :], mix[:, QB:QB + KVB, :]
        swing = cv(2 * T)
        norm_q = Norm(lambda k: cq[:, k, :], lambda k: mix[:, QB + KVB + k, :], QB, T, QR)
        norm_kv = Norm(lambda k: ckv[:, k, :], lambda k: swing[:, k * T:(k + 1) * T], KVB, T, KVR)
        w_uq, w_ukv = cv(QB, MH * MQK), cv(KVB, MH * (NOPE + MV))
        mla_here, mla_mm = sig("mla_weights_here"), sig("mla_mm")
        assert cv.at <= 2 * HIDDEN
        cv.at = 2 * HIDDEN
        qT, kT = cv(MH, T), cv(MH, T)
        vt = arena[:, 0:TB * MH * MV].rearrange("p (b f) -> p b f", b=TB)
        mla_end = cv.at
        q_lin = Linear(evac_act, MH)
        kv_lin = Linear(evac_act, MH + TB)
        rope_mm, rope_done = sig("rope_mm"), sig("rope_done")
        rope_cos = table("mla_rope")[64:96, 0:LAT]
        rope_sin = table("mla_rope")[64:96, LAT:2 * LAT]
        rope_rot = table("mla_rope")[64:96, 2 * LAT:2 * LAT + ROPE]

        def dve_ranks(dve):
            r = 0
            for norm, src, dst, nk, name in ((norm_q, cq, cqn, QB, "mla_q_norm"), (norm_kv, ckv, ckvn, KVB, "mla_kv_norm")):
                norm.wait(dve)
                for k in range(nk):
                    nc.vector.scalar_tensor_tensor(out=dst[:, k, :], in0=src[:, k, :], scalar=vector(name)[:, k:k + 1],
                                                   in1=rstd[:, :], op0=ALU.mult, op1=ALU.mult).then_inc(ranked.sem, 1)
                if norm is norm_q:
                    norm_kv.dve_squares(dve)

        def pe_mla_project(pe):
            pe.wait_ge(mla_here.sem, 32)
            for n in range(MH):
                if n == 0:
                    pe.wait_ge(ranked.sem, QB)
                q_lin.free(pe, n)
                product(pe, q_lin.bank(n)[0:MQK, :], lambda k: w_uq[:, k, n * MQK:(n + 1) * MQK], lambda k: cqn[:, k, :], QB)\
                    .then_inc(mla_mm.sem, 1)
            pe.wait_ge(ranked.sem, QB + KVB)
            for n in range(MH):
                kv_lin.free(pe, n)
                product(pe, kv_lin.bank(n)[0:NOPE, :], lambda k: w_ukv[:, k, n * P:n * P + NOPE], lambda k: ckvn[:, k, :], KVB)\
                    .then_inc(mla_mm.sem, 1)
            heads = [w_ukv[:, k, :].rearrange("p (h c) -> p h c", h=MH)[:, :, NOPE:] for k in range(KVB)]
            for tb in range(TB):
                kv_lin.free(pe, MH + tb)
                product(pe, kv_lin.bank(MH + tb)[:, :], lambda k: ckvn[:, k, tb * P:(tb + 1) * P], lambda k: heads[k], KVB)\
                    .then_inc(mla_mm.sem, 1)
            for g in range(5):
                if g == 0:
                    pe.wait_ge(evac_act.sem, q_lin.base + MH)
                rhs = qT[64:96, 2 * g:2 * g + 2, 0:LAT] if g < 4 else kpe[64:96, 0:LAT]
                dst = rope_bank(g)
                dst = dst.rearrange("p (h t) -> p h t", h=2) if g < 4 else dst
                pe.matmul(dst, rope_rot, rhs, start=True, stop=True).then_inc(rope_mm.sem, 1)

        def rope_bank(g):
            return bank[(2, 3, 6, 7, 5)[g]][64:96, 0:2 * LAT if g < 4 else LAT]

        def act_mla_project(act):
            for n in range(MH):
                act.wait_ge(mla_mm.sem, n + 1)
                nc.scalar.activation(qT[0:MQK, n, :], q_lin.bank(n)[0:MQK, :], ACT.Copy).then_inc(evac_act.sem, 1)
            for n in range(MH + TB):
                act.wait_ge(mla_mm.sem, MH + n + 1)
                src, dst = (kv_lin.bank(n)[0:NOPE, :], kT[0:NOPE, n, :]) if n < MH else (kv_lin.bank(n)[:, :], vt[:, n - MH, :])
                nc.scalar.activation(dst, src, ACT.Copy).then_inc(evac_act.sem, 1)

        def dve_rope(dve):
            for g in (4, 0, 1, 2, 3):
                dve.wait_ge(rope_mm.sem, g + 1)
                n = 2 if g < 4 else 1
                x = qT[64:96, 2 * g:2 * g + 2, 0:LAT] if g < 4 else kpe[64:96, 0:LAT].rearrange("p (h t) -> p h t", h=1)
                part = rope_bank(g).rearrange("p (h t) -> p h t", h=n)
                s = swing[64:96, 0:n * LAT].rearrange("p (h t) -> p h t", h=n)
                cos = rope_cos.rearrange("p (o t) -> p o t", o=1).broadcast_to((ROPE, n, LAT))
                sin = rope_sin.rearrange("p (o t) -> p o t", o=1).broadcast_to((ROPE, n, LAT))
                nc.vector.tensor_tensor(s, part, sin, ALU.mult)
                link(dve, nc.vector.tensor_tensor(x, x, cos, ALU.mult))
                ins = nc.vector.tensor_tensor(x, x, s, ALU.add)
                ins.then_inc(rope_done.sem, 1)
                dve.wait_ge(rope_done.sem, (1, 2, 3, 4, 5)[(4, 0, 1, 2, 3).index(g)])

        def pool_shared_key(pool):
            pool.wait_ge(rope_done.sem, 1)
            for hd in range(MH):
                nc.gpsimd.tensor_copy(kT[64:96, hd, :], kpe[64:96, :]).then_inc(copied.sem, 1)

        att_scores, att_max, att_exp = sig("att_scores"), sig("att_max"), sig("att_exp")
        att_probs, att_turned, att_probsT = sig("att_probs"), sig("att_turned"), sig("att_probsT")
        att_mixed, att_out = sig("att_mixed"), sig("att_out")
        att_small = sb("att_small", [P, 2, 8])

        class Attention:

            def __init__(self, units, scale, room):
                self.units, self.scale, self.p, self.pt = units, scale, room[0:2], room[2:4]
                n = len(units)
                self.b = {s.sem: s.take(n) for s in (att_scores, att_max, att_exp, att_probs, att_turned, att_probsT,
                                                    att_mixed, att_out)}
                self.masked = room[4:6]
                self.before = Linear.last

            def wait(self, eng, s, u):
                if u >= 0:
                    eng.wait_ge(s.sem, self.b[s.sem] + u + 1)

            def pe(self, pe, ready, side=None):
                n = len(self.units)
                for i in range(n + 2):
                    if i < n:
                        u = self.units[i]
                        nk = u["k"].shape[-1]
                        if i == 0:
                            pe.wait_ge(self.before[0].sem, self.before[1])
                        ready(pe, i)
                        self.wait(pe, att_max, i - 2)
                        self.wait(pe, att_exp, i - 2)
                        pe.matmul(bank[2 + i % 2][:, 0:nk], u["q"], u["k"], start=True, stop=True)\
                            .then_inc(att_scores.sem, 1)
                    if side is not None:
                        side.pe(pe, 2 * i)
                    if 1 <= i <= n:
                        j = i - 1
                        self.wait(pe, att_probs, j)
                        self.wait(pe, att_probsT, j - 2)
                        for b in range(len(self.units[j]["v"])):
                            ins = pe.transpose(bank[6 + j % 2][:, b * P:(b + 1) * P], self.p[j % 2][:, b * P:(b + 1) * P],
                                               ident)
                        ins.then_inc(att_turned.sem, 1)
                    if side is not None:
                        side.pe(pe, 2 * i + 1)
                    if i >= 2:
                        j = i - 2
                        u = self.units[j]
                        self.wait(pe, att_probsT, j)
                        self.wait(pe, att_out, j - 2)
                        r = u["rows"]
                        product(pe, bank[j % 2][r, 0:P], lambda b: u["v"][b], lambda b: self.pt[j % 2][:, b * P:(b + 1) * P],
                                len(u["v"])).then_inc(att_mixed.sem, 1)

            def dve(self, dve, side=None):
                n = len(self.units)
                for i in range(n + 2):
                    if 1 <= i <= n:
                        j = i - 1
                        s = att_small[:, j % 2, :]
                        nk = self.units[j]["k"].shape[-1]
                        self.wait(dve, att_exp, j)
                        if self.units[j].get("sink") is not None:
                            link(dve, nc.vector.tensor_tensor(s[:, 2:3], s[:, 2:3], s[:, 4:5], ALU.add))
                        link(dve, nc.vector.reciprocal(s[:, 3:4], s[:, 2:3]))
                        p = self.p[j % 2][:, 0:nk]
                        nc.vector.tensor_scalar(p, p, s[:, 3:4], None, ALU.mult).then_inc(att_probs.sem, 1)
                    if i < n:
                        u = self.units[i]
                        s = att_small[:, i % 2, :]
                        nk = u["k"].shape[-1]
                        src = bank[2 + i % 2][:, 0:nk]
                        self.wait(dve, att_scores, i)
                        self.wait(dve, att_exp, i - 2)
                        if u.get("mask") is not None:
                            m = self.masked[i % 2][:, 0:nk]
                            link(dve, nc.vector.tensor_tensor(m, src, u["mask"], ALU.add))
                            src = m
                        link(dve, nc.vector.reduce_max(s[:, 0:1], src, AX.X))
                        if u.get("sink") is not None:
                            ins = nc.vector.tensor_scalar(s[:, 1:2], s[:, 0:1], -self.scale, u["sink"][1], ALU.mult, ALU.min)
                        else:
                            ins = nc.vector.tensor_scalar(s[:, 1:2], s[:, 0:1], -self.scale, None, ALU.mult)
                        ins.then_inc(att_max.sem, 1)
                    if side is not None:
                        side.dve(dve, 2 * i)
                    if i >= 2:
                        j = i - 2
                        self.wait(dve, att_mixed, j)
                        nc.vector.tensor_copy(self.units[j]["out"], bank[j % 2][self.units[j]["rows"], 0:P])\
                            .then_inc(att_out.sem, 1)
                    if side is not None:
                        side.dve(dve, 2 * i + 1)

            def act(self, act, side=None):
                n = len(self.units)
                for i in range(n + 2):
                    if side is not None:
                        side.act_empty(act, 2 * i)
                    if i < n:
                        u = self.units[i]
                        nk = u["k"].shape[-1]
                        s = att_small[:, i % 2, :]
                        self.wait(act, att_max, i)
                        self.wait(act, att_turned, i - 2)
                        src = bank[2 + i % 2][:, 0:nk] if u.get("mask") is None else self.masked[i % 2][:, 0:nk]
                        if u.get("sink") is not None:
                            self.wait(act, att_probs, i - 2)
                            nc.scalar.activation(s[:, 4:5], u["sink"][0], ACT.Exp, bias=s[:, 1:2])
                        nc.scalar.activation(self.p[i % 2][:, 0:nk], src, ACT.Exp, scale=self.scale, bias=s[:, 1:2],
                                             accum_out=s[:, 2:3]).then_inc(att_exp.sem, 1)
                    if side is not None:
                        side.act_split(act, 2 * i)
                    if 1 <= i <= n:
                        j = i - 1
                        nk = self.units[j]["k"].shape[-1]
                        self.wait(act, att_turned, j)
                        self.wait(act, att_mixed, j - 2)
                        nc.scalar.activation(self.pt[j % 2][:, 0:nk], bank[6 + j % 2][:, 0:nk], ACT.Copy)\
                            .then_inc(att_probsT.sem, 1)
                    if side is not None:
                        side.act_empty(act, 2 * i + 1)
                        side.act_split(act, 2 * i + 1)

        room = [a[:, 2 * i, :] for i in range(4)]
        mla_units = []
        for q0, k0, kn in ((0, 0, T), (LAT, LAT, CTX)):
            for hd in range(MH):
                for q in range(q0, q0 + LAT, P):
                    r = slice((hd % 2) * MV, (hd % 2 + 1) * MV)
                    mla_units.append(dict(q=qT[0:MQK, hd, q:q + P], k=kT[0:MQK, hd, k0:k0 + kn],
                                          v=[vt[:, b, hd * MV:(hd + 1) * MV] for b in range(k0 // P, (k0 + kn) // P)],
                                          rows=r, out=mix[r, hd // 2, q:q + P]))
        mla = Attention(mla_units, MQK ** -0.5, room)

        def pe_mla(pe):
            def ready(pe, i):
                hd = i * P // LAT
                if i % (LAT // P) == 0 and hd < MH:
                    pe.wait_ge(rope_done.sem, 2 + hd // 2)
                    pe.wait_ge(copied.sem, hd + 1)
                if i == 0:
                    pe.wait_ge(evac_act.sem, kv_lin.base + MH + TB)
                if i == 1:
                    pe.wait_ge(rope_done.sem, 3)
            mla.pe(pe, ready, back)
            for p in (0, 1):
                back.pe_step(pe, len(back.pairs) + p)

        def act_mla(act):
            mla.act(act, back)
            back.act_row(act, len(back.pairs))
            back.act_hi(act, len(back.pairs))

        def dve_mla(dve):
            mla.dve(dve, back)
            back.dve_lo(dve, len(back.pairs))
            for x in (ada_b, ada_c):
                dve_ada(dve, ada_c.turned + ada_c.n // 2, x.layer, x.j0, x.n)

        ada_b = Ada(Tiles(NMOD * KB - ADA_A, lambda t: cols_of(d["ada_w"][0], P * (ADA_A + t), P)), 0, ADA_A, NMOD * KB - ADA_A)
        ada_c = Ada(Tiles(NMOD * KB, lambda t: cols_of(d["ada_w"][1], P * t, P)), 1, 0, NMOD * KB)
        back = Background((ada_b, ada_c))
        back.begin(len(mla.units) + 2)

        gla_signals = {n: sig("gla_" + n) for n in ("logits", "logs", "gates", "cums", "decays", "decayed", "scores", "masked",
                                                    "turned", "keys", "updates", "states", "outs", "squares", "sums",
                                                    "roots", "merged")}
        cg = Carve()
        cg.at = even_at
        decay = cg(2 * GFB, T)
        qdec, kinv, kend = cg(2 * GFB, T), cg(2 * GFB, T), cg(2 * GFB, T)
        ktok = cg(2 * GFB, TB, P)
        ascore = cg(GH, TB, P)
        states = [arena[:, 0:GFB * NCH * P].rearrange("p (f n v) -> p f n v", f=GFB, n=NCH), cg(GFB, NCH, P)]
        glg = table("mla_rope")[0:GRANK + 1, 0:2 * GH * GDK].rearrange("r (z f) -> r z f", z=2)
        gate = a[:, 0:4, :]
        gate_e = a[:, 4:8, :]
        gout = a[:, 0:4, :]
        gsq, groot = kend, kinv
        ORDER = (list(range(NCH // 2, NCH)) + list(range(NCH // 2)), list(range(NCH - 1, -1, -1)))
        G = {n: s.sem for n, s in gla_signals.items()}
        GBANK = (2, 3, 6, 7)

        def chunk(c):
            return slice(c * C, (c + 1) * C)

        def half(x):
            return slice(x * C, (x + 1) * C)

        def pe_gla(pe):
            for tb in range(TB):
                for z in range(2):
                    ins = pe.matmul(bank[GBANK[tb]][:, z * 256:(z + 1) * 256], glow[0:GRANK + 1, z, tb * P:(tb + 1) * P],
                                    glg[:, z, :], start=True, stop=True)
                ins.then_inc(G["logits"], 1)
            pe.wait_ge(att_out.sem, mla.b[att_out.sem] + len(mla.units))
            for q in range(2 * GFB):
                z = q // GFB
                for tb in range(TB):
                    if q == 0:
                        pe.wait_ge(G["gates"], tb + 1)
                    elif q == 2 and tb == 0:
                        pe.wait_ge(G["gates"], TB)
                    ins = pe.matmul(bank[q][:, tb * P:(tb + 1) * P], gate[:, tb, q * P:(q + 1) * P], upto[:, z, :],
                                    start=True, stop=True)
                ins.then_inc(G["cums"], 1)
            for q in range(2 * GFB):
                pe.wait_ge(G["decayed"], q + 1)
                for hh in range(2):
                    n = 2 * q + hh
                    if n >= 2:
                        pe.wait_ge(G["masked"], n - 1)
                    for tb in range(TB):
                        t = slice(tb * P, (tb + 1) * P)
                        ins = pe.matmul(bank[6 + hh][:, t], kinv[half(hh), q, t], qdec[half(hh), q, t], start=True, stop=True)
                    ins.then_inc(G["scores"], 1)
                if q >= 2:
                    pe.wait_ge(G["keys"], q - 1)
                for tb in range(TB):
                    t = slice(tb * P, (tb + 1) * P)
                    ins = pe.transpose(bank[q % 2][:, t], kend[:, q, t], ident)
                ins.then_inc(G["turned"], 1)
            for q in range(2 * GFB):
                pe.wait_ge(G["keys"], q + 1)
                if q == 1:
                    pe.wait_ge(G["masked"], 4 * GFB)
                    pe.wait_ge(G["decays"], 4 * GFB)
                elif q >= 2:
                    pe.wait_ge(G["states"], q - 1)
                for cp in range(2):
                    if q == 0:
                        pe.wait_ge(G["keys"], 2 * GFB)
                    b = bank[cp + 6 * (q % 2)]
                    for tb in range(TB):
                        for hh in range(2):
                            hd = 2 * (q % GFB) + hh
                            ins = pe.matmul(b[half(hh), tb * P:(tb + 1) * P], ktok[half(cp), q, tb, hh * C:(hh + 1) * C],
                                            gv[half(cp), tb, hd * P:(hd + 1) * P], start=True, stop=True)
                ins.then_inc(G["updates"], 1)
            for hd in range(GH):
                f, hh = hd // 2, hd % 2
                if hd == 0:
                    pe.wait_ge(G["states"], 2 * GFB)
                    pe.wait_ge(G["masked"], 4 * GFB)
                if hd >= 2:
                    pe.wait_ge(G["outs"], hd - 1)
                b = bank[2 + hd % 2]
                for tb in range(TB):
                    t = slice(tb * P, (tb + 1) * P)
                    pe.matmul(b[:, t], gv[:, tb, hd * P:(hd + 1) * P], ascore[:, hd, tb, :], start=tb == 0, stop=False,
                              skip_group_check=True)
                for z in range(2):
                    for n in range(1, NCH):
                        c = ORDER[z][n]
                        ins = pe.matmul(b[:, chunk(c)], states[z][half(hh), f, n, :], qdec[half(hh), GFB * z + f, chunk(c)],
                                        start=False, stop=z == 1 and n == NCH - 1, skip_group_check=True)
                ins.then_inc(G["sums"], 1)
            for hd in range(GH):
                pe.wait_ge(G["squares"], hd + 1)
                pe.matmul(bank[(0, 1, 6, 7)[hd]][:, :], ones, gsq[:, hd, :], start=True, stop=True).then_inc(G["sums"], 1)

        def act_gla(act):
            for tb in range(TB):
                act.wait_ge(G["logits"], tb + 1)
                nc.scalar.activation(gate_e[:, tb, :], bank[GBANK[tb]][:, :], ACT.Abs).then_inc(G["logs"], 1)
            for tb in range(TB):
                act.wait_ge(G["logs"], tb + 1)
                nc.scalar.activation(gate_e[:, tb, :], gate_e[:, tb, :], ACT.Exp, scale=-1.0).then_inc(G["logs"], 1)
            for tb in range(TB):
                act.wait_ge(G["logs"], TB + tb + 1)
                nc.scalar.activation(gate_e[:, tb, :], gate_e[:, tb, :], ACT.Ln, bias=1.0).then_inc(G["logs"], 1)
            for q in range(2 * GFB):
                act.wait_ge(G["cums"], q + 1)
                if q >= 2:
                    act.wait_ge(G["decayed"], q - 1)
                nc.scalar.activation(decay[:, q, :], bank[q][:, :], ACT.Exp, scale=1.0 / 16).then_inc(G["decays"], 1)
                nc.scalar.activation(tmp[:, q % 2, :], bank[q][:, :], ACT.Exp, scale=-1.0 / 16).then_inc(G["decays"], 1)
            for q in range(2 * GFB):
                act.wait_ge(G["turned"], q + 1)
                nc.scalar.activation(ktok[:, q].rearrange("p t f -> p (t f)"), bank[q % 2][:, :], ACT.Copy)\
                    .then_inc(G["keys"], 1)
            for hd in range(GH):
                act.wait_ge(G["sums"], hd + 1)
                act.wait_ge(G["turned"], 2 * GFB)
                nc.scalar.activation(gsq[:, hd, :], bank[2 + hd % 2][:, :], ACT.Square).then_inc(G["squares"], 1)
                nc.scalar.activation(gout[:, hd, :], bank[2 + hd % 2][:, :], ACT.Copy).then_inc(G["outs"], 1)
            for hd in range(GH):
                act.wait_ge(G["sums"], GH + hd + 1)
                nc.scalar.activation(groot[:, hd, :], bank[(0, 1, 6, 7)[hd]][:, :], ACT.Ln, scale=1.0 / GDV, bias=eps_col)\
                    .then_inc(G["roots"], 1)
            for hd in range(GH):
                act.wait_ge(G["roots"], hd + 1)
                nc.scalar.activation(groot[:, hd, :], groot[:, hd, :], ACT.Exp, scale=-0.5).then_inc(G["roots"], 1)

        def dve_gla(dve):
            for tb in range(TB):
                dve.wait_ge(G["logs"], 2 * TB + tb + 1)
                nc.vector.scalar_tensor_tensor(out=gate[:, tb, :], in0=bank[GBANK[tb]][:, :], scalar=0.0,
                                               in1=gate_e[:, tb, :], op0=ALU.min, op1=ALU.subtract).then_inc(G["gates"], 1)
            for q in range(2 * GFB):
                z, f = q // GFB, q % GFB
                dve.wait_ge(G["decays"], 2 * q + 2)
                nc.vector.scalar_tensor_tensor(out=qdec[:, q, :], in0=gq[:, f, :], scalar=GDK ** -0.5, in1=decay[:, q, :],
                                               op0=ALU.mult, op1=ALU.mult)
                link(dve, nc.vector.tensor_tensor(kinv[:, q, :], gk[:, f, :], tmp[:, q % 2, :], ALU.mult))
                last = decay[:, q, :].rearrange("p (n c) -> p n c", c=C)[:, :, (C - 1) * (1 - z):(C - 1) * (1 - z) + 1]
                nc.vector.tensor_tensor(kend[:, q, :].rearrange("p (n c) -> p n c", c=C),
                                        kinv[:, q, :].rearrange("p (n c) -> p n c", c=C),
                                        last.broadcast_to((P, NCH, C)), ALU.mult).then_inc(G["decayed"], 1)
            for q in range(2 * GFB):
                z = q // GFB
                for hh in range(2):
                    n, hd = 2 * q + hh, 2 * (q % GFB) + hh
                    dve.wait_ge(G["scores"], n + 1)
                    mask = upto[:, z:z + 1, :].broadcast_to((P, TB, P))
                    src = bank[6 + hh][:, :].rearrange("p (t i) -> p t i", t=TB)
                    if z == 0:
                        nc.vector.tensor_tensor(ascore[:, hd], src, mask, ALU.mult).then_inc(G["masked"], 1)
                    else:
                        part = tmp[:, hh, :].rearrange("p (t i) -> p t i", t=TB)
                        link(dve, nc.vector.tensor_tensor(part, src, mask, ALU.mult))
                        nc.vector.tensor_tensor(ascore[:, hd], ascore[:, hd], part, ALU.add).then_inc(G["masked"], 1)
            for q in range(2 * GFB):
                z, f = q // GFB, q % GFB
                dve.wait_ge(G["updates"], q + 1)
                for n in range(NCH - 1):
                    c = ORDER[z][n]
                    add = bank[c % 2 + 6 * (q % 2)][:, (c // 2) * P:(c // 2 + 1) * P]
                    to = states[z][:, f, n + 1, :]
                    last = c * C + (C - 1) * (1 - z)
                    if n == 0:
                        ins = nc.vector.tensor_copy(to, add)
                    else:
                        ins = nc.vector.scalar_tensor_tensor(out=to, in0=states[z][:, f, n, :],
                                                             scalar=decay[:, q, last:last + 1], in1=add,
                                                             op0=ALU.mult, op1=ALU.add)
                    if n < NCH - 2:
                        link(dve, ins)
                ins.then_inc(G["states"], 1)
            for hd in range(GH):
                dve.wait_ge(G["roots"], GH + hd + 1)
                link(dve, nc.vector.scalar_tensor_tensor(out=mix[:, 4 + hd, :], in0=gout[:, hd, :],
                                                         scalar=vector("gla_o_norm"), in1=groot[:, hd, :],
                                                         op0=ALU.mult, op1=ALU.mult))
                nc.vector.tensor_tensor(mix[:, 4 + hd, :], mix[:, 4 + hd, :], gg[:, hd, :], ALU.mult).then_inc(G["merged"], 1)

        class Projection:

            def __init__(self, source, rows, nblocks, width, x, evac, body=AHEAD, banks=2):
                self.rows, self.per, self.nb, self.width, self.x, self.body = rows, len(rows), nblocks, width, x, body
                n = nblocks * self.per
                self.tiles = Tiles(n, source)
                self.tiles.body, self.tiles.rows = body, rows
                self.tiles.place = lambda i, t: source(i * self.blocks + t // self.per, rows[t % self.per])
                self.bodies = n // body
                self.blocks = body // self.per
                self.lin = Linear(evac, nblocks, banks)
                assert n % body == 0 and body % AHEAD == 0 and self.blocks % banks == 0

            def done(self, n):
                return n * (UNITS * self.per) + UNITS * (self.tiles.first + self.per)

            def pe_tile(self, pe, t, body=None):
                n, part = t // self.per, t % self.per
                k0, nk = self.rows[part]
                self.tiles.wait(pe, t, None if body is None else (body, self.body))
                if part == 0:
                    self.lin.free(pe, n, None if body is None else body * self.blocks)
                split_product(pe, self.lin.bank(n)[:, 0:self.width], self.tiles.parts(t),
                              tuple((lambda k, x=x: x(k0 + k)) for x in self.x), nk, start=part == 0, stop=part + 1 == self.per)\
                    .then_inc(block_done.sem, UNITS)

            def pe(self, pe, ready=None):
                pair = 2 if ready is not None else 0
                for t in range(pair):
                    self.tiles.wait(pe, t)
                    self.lin.free(pe, t)
                if pair:
                    assert self.per == 1
                    for ins in split_products(pe, [self.lin.bank(n)[:, 0:self.width] for n in range(2)],
                                              [self.tiles.parts(n) for n in range(2)], self.x, self.rows[0][1], ready):
                        ins.then_inc(block_done.sem, UNITS)
                for t in range(pair, self.body):
                    self.pe_tile(pe, t)
                if self.bodies > 1:
                    with pe.Fori(1, self.bodies) as i:
                        for t in range(self.body):
                            self.pe_tile(pe, t, body=i)

            def walk(self, eng, split, empty=None):
                final = self.tiles.first + self.tiles.n == Tiles.count
                bodies = self.bodies - final

                def body(i, at, g, loop):
                    for t in range(self.body):
                        if empty is not None and t % self.per == self.per - 1:
                            b = t // self.per
                            empty(i, at + b, b)
                        split(eng, g + t + AHEAD, loop)

                if bodies:
                    with eng.Fori(0, bodies) as i:
                        body(i, i * self.blocks, self.tiles.first, (i, self.body))
                if final:
                    body(bodies, bodies * self.blocks, self.tiles.first + bodies * self.body, None)

        def whole(kb=KB):
            return [(k, min(KB, kb - k)) for k in range(0, kb, KB)]

        class Residual:

            def __init__(self, proj, layer, which):
                self.proj, self.j = proj, (3 * which + 2) * KB
                self.layer = layer

            def step(self, dve, n, u):
                dve.wait_ge(block_done.sem, self.proj.done(n))
                for z in range(self.proj.width // LAT):
                    s = slice(z * LAT, (z + 1) * LAT)
                    x = h[:, bass.ds(n, 1), s].rearrange("p o t -> p (o t)")
                    g = mod[:, self.layer, bass.ds(n + self.j, 1), z:z + 1].rearrange("p o t -> p (o t)")
                    ins = nc.vector.scalar_tensor_tensor(out=x, in0=self.proj.lin.bank(u)[:, s], scalar=g, in1=x,
                                                         op0=ALU.mult, op1=ALU.add)
                ins.then_inc(evac_dve.sem, 1)

            def dve(self, dve):
                self.proj.walk(dve, split_lo, lambda i, n, b: self.step(dve, n, b % 2))

        class Mlp:

            def __init__(self, layer, width):
                self.w = width
                self.blocks = HIDDEN // width
                view = lambda x: x.rearrange("p (n t) -> p n t", t=width)
                self.hi, self.lo = view(hid_hi), view(hid_lo)
                self.norm = Modulated(layer, 1, width)
                self.parts = []
                for part in range(FB // self.blocks):
                    b0 = part * self.blocks
                    up = Projection(lambda n, r, b0=b0: dyn(d["mlp_w1"][layer], n * P + b0 * P), whole(), self.blocks, width,
                                    split_x(width), evac_dve)
                    down = Projection(lambda n, r, b0=b0: dyn(d["mlp_w2"][layer], n * P, (b0 + r[0]) * P, r[1]),
                                      whole(self.blocks), KB, width,
                                      tuple((lambda k, x=x: x[:, k, :]) for x in (self.hi, self.lo)), evac_dve,
                                      body=2 * self.blocks // KB)
                    self.parts.append((up, down, Residual(down, layer, 1), relus.take(2 * self.blocks)))

            def last(self):
                return self.parts[-1][1].lin.base + KB

            def pe(self, pe):
                for up, down, res, base in self.parts:
                    up.pe(pe, (lambda k: self.norm.ready(pe, k)) if up is self.parts[0][0] else None)
                    pe.wait_ge(evac_dve.sem, up.lin.base + self.blocks)
                    down.pe(pe)

            def act(self, act):
                for up, down, res, base in self.parts:
                    def empty(i, n, b):
                        u = b % 2
                        act.wait_ge(block_done.sem, up.done(n))
                        act.wait_ge(evac_dve.sem, n + (up.lin.base - 1))
                        nc.scalar.activation(tmp[:, u, 0:self.w], up.lin.bank(u)[:, 0:self.w], ACT.Relu).then_inc(relus.sem, 1)
                        act.wait_ge(relus.sem, n * 2 + (base + 1))
                        nc.scalar.activation(self.hi[:, bass.ds(n, 1), :].rearrange("p o t -> p (o t)"), tmp[:, u, 0:self.w],
                                             ACT.Square).then_inc(relus.sem, 1)
                    up.walk(act, split_hi, empty)
                    down.walk(act, split_hi)

            def dve(self, dve):
                for up, down, res, base in self.parts:
                    def empty(i, n, b):
                        u = b % 2
                        dve.wait_ge(relus.sem, n * 2 + (base + 1))
                        nc.vector.tensor_tensor(a[:, u, 0:self.w], tmp[:, u, 0:self.w], tmp[:, u, 0:self.w], ALU.mult)\
                            .then_inc(squared.sem, 1)
                        dve.wait_ge(squared.sem, n + (base // 2 + 1))
                        dve.wait_ge(relus.sem, n * 2 + (base + 2))
                        at = bass.ds(n, 1)
                        nc.vector.tensor_tensor(self.lo[:, at, :].rearrange("p o t -> p (o t)"), a[:, u, 0:self.w],
                                                self.hi[:, at, :].rearrange("p o t -> p (o t)").bitcast(F32), ALU.subtract)\
                            .then_inc(evac_dve.sem, 1)
                    up.walk(dve, split_lo, empty)
                    res.dve(dve)

        relus, squared = sig("relus"), sig("squared")
        even_x = Operand(lambda k: mix[:, k, :], KB, slice(0, T))
        even_out = Projection(lambda n, r: dyn(d["even_w_out"][0], n * P), whole(), KB, T, split_x(T), evac_dve)
        even_res = Residual(even_out, 0, 0)
        mlp0 = Mlp(0, T)

        def squares_ready(total):
            def wait(eng, k):
                if k < 2:
                    eng.wait_ge(evac_dve.sem, total)
            return wait

        def pe_rest0(pe):
            pe.wait_ge(G["roots"], GH)
            even_out.pe(pe, lambda k: even_x.ready(pe, k))
            mlp0.norm.norm.pe_sums(pe)
            mlp0.pe(pe)

        def act_rest0(act):
            for k in range(KB):
                if k == 0:
                    act.wait_ge(att_out.sem, mla.b[att_out.sem] + len(mla.units))
                if k >= KB - GH:
                    act.wait_ge(G["merged"], k - (KB - GH) + 1)
                even_x.act(act, k)
            even_out.walk(act, split_hi)
            mlp0.norm.norm.act_squares(act, squares_ready(even_out.lin.base + KB))
            mlp0.norm.norm.act_root(act)
            mlp0.norm.act(act)
            mlp0.act(act)

        def dve_rest0(dve):
            for k in range(KB):
                even_x.dve(dve, k)
            dve.wait_ge(gains_done.sem, 2)
            even_res.dve(dve)
            mlp0.norm.norm.dve_squares(dve, squares_ready(even_out.lin.base + KB))
            mlp0.norm.dve(dve)
            mlp0.dve(dve)

        n3 = Modulated(1, 0, T)
        co = Carve()
        qf, kf = co(QKB, LAT), co(QKB, T)
        vtok, ktk = co(TB, NH * NDV), co(TB, NH * NDK)
        sg = co(VB, LAT)
        ab, la, beta = co(TB, 4 * NH), co(TB, 2 * NH), co(TB, 2 * NH)
        gsum, eg, kef, betaw = co(TB, 2 * NH), co(TB, 2 * NH), co(TB, 2 * NH), co(TB, 2 * NH)
        gend = co(NCH, 2, NH // 2)
        gsm = co(TB, 2 * NH)
        vf = co(2, T)
        co.at -= 2 * T
        BT, BA = co(2, NH, C), co(2, NH, C)
        qdc = co(2, NH // 2, P)
        first_state = co(2, NH // 2, NDV)
        BX, BXT, BY, BC = (co(2, NH, P) for _ in range(4))
        kends = BA

        def state(i, z, hp, rows=slice(0, P)):
            if i % 3 == 0:
                return first_state[rows, z, hp, :]
            if i % 3 == 1:
                return tmp[rows, z, hp * P:(hp + 1) * P]
            return mix[rows, 2 * z + hp // 2, LAT + (hp % 2) * P:LAT + (hp % 2 + 1) * P]

        def WT(z, c):
            return mix[:, 4 + 2 * z + c, LAT:T].rearrange("p (h i) -> p h i", h=NH // 2)

        U = a[:, 0:4, :].rearrange("p k t -> p (k t)").rearrange("p (z h v) -> p z h v", z=2, h=NH)
        QKT = a[:, 4:8, :].rearrange("p k t -> p (k t)").rearrange("p (z h i) -> p z h i", z=2, h=NH)
        odd_names = ("gates_in", "scaled", "silu", "turned", "vals", "sq", "sums", "logs", "roots", "normed", "kturn", "ktok",
                     "sp", "gates", "cums", "cumsd", "ge")
        OS = {n: sig("odd_" + n).sem for n in odd_names}
        w_odd = d["gdn_w_in"][0]
        odd_tiles = Tiles(O_AB // P, lambda t: cols_of(w_odd, P * t, P))
        ab_tiles = Tiles(2, lambda t: cols_of(w_odd, O_AB + 2 * NH * t, 2 * NH), KB, 2 * NH)
        NB_CONV = 2 * QKB + VB
        odd_mixed = sig("odd_mixed")
        odd_lin = Linear(odd_mixed, NB_CONV)
        OS["mixed"] = odd_mixed.sem
        sg_lin = Linear(evac_act, VB)

        def odd_width(n):
            return LAT if n < QKB or n >= NB_CONV else T

        def odd_dst(n):
            if n < QKB:
                return qf[:, n, :]
            return kf[:, n - QKB, :] if n < 2 * QKB else vf[:, n % 2, :]

        def odd_done(n):
            return odd_tiles.done(n)

        def pe_odd_in(pe):
            def turn(n):
                j = n - 2 * QKB
                pe.wait_ge(OS["silu"], n + 1)
                if j >= 2:
                    pe.wait_ge(OS["vals"], j - 1)
                for tb in range(TB):
                    ins = pe.transpose(bank[2 + j % 2][:, tb * P:(tb + 1) * P], vf[:, n % 2, tb * P:(tb + 1) * P], ident)
                ins.then_inc(OS["turned"], 1)

            for n in range(2):
                odd_tiles.wait(pe, n)
                odd_lin.free(pe, n)
            for ins in split_products(pe, [odd_lin.bank(n)[:, 0:odd_width(n)] for n in range(2)],
                                      [odd_tiles.parts(n) for n in range(2)], split_x(LAT), KB, lambda k: n3.ready(pe, k)):
                ins.then_inc(block_done.sem, UNITS)
            for n in range(2, NB_CONV + VB):
                lin, i = (odd_lin, n) if n < NB_CONV else (sg_lin, n - NB_CONV)
                odd_tiles.wait(pe, n)
                width = odd_width(n)
                lin.free(pe, i)
                split_product(pe, lin.bank(i)[:, 0:width], odd_tiles.parts(n), split_x(width), KB)\
                    .then_inc(block_done.sem, UNITS)
                if 2 * QKB < n <= NB_CONV:
                    turn(n - 1)
            for z in range(2):
                ab_tiles.wait(pe, z)
                for tb in range(TB):
                    ins = split_product(pe, bank[6][:, tb * 32 + z * 16:tb * 32 + (z + 1) * 16], split_x(P, tb * P),
                                        ab_tiles.parts(z), KB)
                ins.then_inc(block_done.sem, UNITS)
            for n in range(2 * QKB):
                pe.wait_ge(OS["sq"], n + 1)
                if n == 0:
                    pe.wait_ge(OS["vals"], VB)
                if n >= 4:
                    pe.wait_ge(OS["logs"], n - 3)
                width = odd_width(n)
                pe.matmul(bank[(2, 3, 4, 5)[n % 4]][:, 0:width], ones_half, odd_sq(n), start=True, stop=True)\
                    .then_inc(OS["sums"], 1)
            pe.wait_ge(OS["gates"], 1)
            pe.wait_ge(evac_act.sem, sg_lin.base + VB)
            for tb in range(TB):
                for z in range(2):
                    pe.matmul(bank[7][:, tb * 16 + z * NH:tb * 16 + (z + 1) * NH], upto[:, z, :], la[:, tb, z * NH:(z + 1) * NH],
                              start=True, stop=True)
                pe.matmul(bank[7][:, 64 + tb * 16:64 + (tb + 1) * 16], ones_half, la[:, tb, :], start=True, stop=True)
            for c in range(NCH):
                ins = pe.matmul(bank[c % 2][:, (c // 2) * 16:(c // 2 + 1) * 16], ones[half(c % 2), :], la[half(c % 2), c // 2, :],
                                start=True, stop=True)
            ins.then_inc(OS["cums"], 1)
            for f in range(QKB):
                pe.wait_ge(OS["normed"], QKB + f + 1)
                if f == 0:
                    pe.wait_ge(OS["logs"], 2 * QKB)
                if f >= 2:
                    pe.wait_ge(OS["ktok"], f - 1)
                for tb in range(TB):
                    ins = pe.transpose(bank[2 + f % 2][:, tb * P:(tb + 1) * P], kf[:, f, tb * P:(tb + 1) * P], ident)
                ins.then_inc(OS["kturn"], 1)

        def odd_sq(n):
            return mix[:, n, 0:odd_width(n)]

        def conv_w(tap, n):
            return vector("gdn_conv_w").rearrange("p (t n) -> p t n", t=3)[:, tap, n:n + 1]

        def act_odd_in(act):
            def silu(n):
                act.wait_ge(OS["mixed"], n + 1)
                nc.scalar.activation(odd_dst(n), odd_dst(n), ACT.Silu).then_inc(OS["silu"], 1)

            def vals(j):
                act.wait_ge(OS["turned"], j + 1)
                nc.scalar.activation(vtok[:, :, j * P:(j + 1) * P], bank[2 + j % 2][:, :].rearrange("p (t f) -> p t f", t=TB),
                                     ACT.Copy).then_inc(OS["vals"], 1)

            for n in range(NB_CONV):
                if n >= 1:
                    silu(n - 1)
                if n >= 2 * QKB + 2:
                    vals(n - 2 * QKB - 2)
                act.wait_ge(block_done.sem, odd_done(n))
                if n >= 2 * QKB + 2:
                    act.wait_ge(OS["turned"], n - 2 * QKB - 1)
                nc.scalar.activation(odd_dst(n), odd_lin.bank(n)[:, 0:odd_width(n)], ACT.Copy, scale=conv_w(1, n))\
                    .then_inc(OS["scaled"], 1)
                split_hi(act, odd_tiles.first + n + AHEAD)
            silu(NB_CONV - 1)
            for i in range(VB):
                act.wait_ge(block_done.sem, odd_done(NB_CONV + i))
                nc.scalar.activation(sg[:, i, :], sg_lin.bank(i)[:, 0:LAT], ACT.Silu).then_inc(evac_act.sem, 1)
                split_hi(act, odd_tiles.first + NB_CONV + i + AHEAD)
                if i < 2:
                    vals(VB - 2 + i)
            for z in range(2):
                split_hi(act, ab_tiles.first + z + AHEAD)
            act.wait_ge(OS["gates_in"], 1)
            nc.scalar.activation(gsm[:, :, :], ab[:, :, 0:16], ACT.Abs).then_inc(OS["sp"], 1)
            act.wait_ge(OS["sp"], 1)
            nc.scalar.activation(gsm[:, :, :], gsm[:, :, :], ACT.Exp, scale=-1.0).then_inc(OS["sp"], 1)
            nc.scalar.activation(beta[:, :, :], ab[:, :, 16:32], ACT.Exp, scale=-1.0)
            nc.scalar.activation(eg[:, 0, :], vector("gdn_a_log"), ACT.Exp)
            act.wait_ge(OS["sp"], 2)
            nc.scalar.activation(gsm[:, :, :], gsm[:, :, :], ACT.Ln, bias=1.0).then_inc(OS["sp"], 1)
            for n in range(2 * QKB):
                act.wait_ge(OS["sums"], n + 1)
                nc.scalar.activation(odd_sq(n), bank[(2, 3, 4, 5)[n % 4]][:, 0:odd_width(n)], ACT.Ln, bias=eps_col)\
                    .then_inc(OS["logs"], 1)
            for n in range(2 * QKB):
                act.wait_ge(OS["logs"], n + 1)
                nc.scalar.activation(odd_sq(n), odd_sq(n), ACT.Exp, scale=-0.5).then_inc(OS["roots"], 1)
            act.wait_ge(OS["cumsd"], 1)
            nc.scalar.activation(eg[:, :, :], gsum[:, :, :], ACT.Exp).then_inc(OS["ge"], 1)
            nc.scalar.activation(kef[:, :, :], kef[:, :, :], ACT.Exp).then_inc(OS["ge"], 1)
            nc.scalar.activation(gend[:, :, :, :], gend[:, :, :, :], ACT.Exp).then_inc(OS["ge"], 1)
            for f in range(QKB):
                act.wait_ge(OS["kturn"], f + 1)
                nc.scalar.activation(ktk[:, :, f * P:(f + 1) * P], bank[2 + f % 2][:, :].rearrange("p (t f) -> p t f", t=TB),
                                     ACT.Copy).then_inc(OS["ktok"], 1)

        def dve_odd_in(dve):
            for n in range(NB_CONV):
                dve.wait_ge(OS["scaled"], n + 1)
                width = odd_width(n)
                x = odd_lin.bank(n)[:, 0:width].rearrange("p (s t) -> p s t", t=LAT)
                y = odd_dst(n).rearrange("p (s t) -> p s t", t=LAT)
                link(dve, nc.vector.scalar_tensor_tensor(out=y[:, :, 1:], in0=x[:, :, 0:LAT - 1], scalar=conv_w(0, n),
                                                         in1=y[:, :, 1:], op0=ALU.mult, op1=ALU.add))
                nc.vector.scalar_tensor_tensor(out=y[:, :, 0:LAT - 1], in0=x[:, :, 1:], scalar=conv_w(2, n),
                                               in1=y[:, :, 0:LAT - 1], op0=ALU.mult, op1=ALU.add).then_inc(OS["mixed"], 1)
                split_lo(dve, odd_tiles.first + n + AHEAD)
            for i in range(VB + 2):
                split_lo(dve, odd_tiles.first + NB_CONV + i + AHEAD)
            for n in range(2 * QKB):
                dve.wait_ge(OS["silu"], n + 1)
                nc.vector.tensor_tensor(odd_sq(n), odd_dst(n), odd_dst(n), ALU.mult).then_inc(OS["sq"], 1)
            dve.wait_ge(block_done.sem, ab_tiles.done(1))
            link(dve, nc.vector.tensor_copy(ab[:, :, :], bank[6][:, 0:128].rearrange("p (t c) -> p t c", t=TB)))
            bias = vector("gdn_dt_bias").rearrange("p (o c) -> p o c", o=1).broadcast_to((P, TB, 16))
            nc.vector.tensor_tensor(ab[:, :, 0:16], ab[:, :, 0:16], bias, ALU.add).then_inc(OS["gates_in"], 1)
            dve.wait_ge(OS["gates_in"], 1)
            link(dve, nc.vector.tensor_scalar(la[:, :, :], ab[:, :, 0:16], 0.0, None, ALU.max))
            dve.wait_ge(OS["sp"], 3)
            link(dve, nc.vector.tensor_tensor(la[:, :, :], la[:, :, :], gsm[:, :, :], ALU.add))
            link(dve, nc.vector.tensor_tensor(la[:, :, :], la[:, :, :], eg[:, 0:1, :].broadcast_to((P, TB, 16)), ALU.mult))
            nc.vector.tensor_scalar(la[:, :, :], la[:, :, :], -1.0, None, ALU.mult).then_inc(OS["gates"], 1)
            link(dve, nc.vector.tensor_scalar(beta[:, :, :], beta[:, :, :], 1.0, None, ALU.add))
            link(dve, nc.vector.reciprocal(beta[:, :, :], beta[:, :, :]))
            for n in range(2 * QKB):
                dve.wait_ge(OS["roots"], n + 1)
                nc.vector.scalar_tensor_tensor(out=odd_dst(n), in0=odd_dst(n), scalar=NDK ** -0.5 if n < QKB else 1.0,
                                               in1=odd_sq(n), op0=ALU.mult, op1=ALU.mult).then_inc(OS["normed"], 1)
            dve.wait_ge(OS["cums"], 1)
            link(dve, nc.vector.tensor_copy(gsum[:, :, :].rearrange("p t c -> p (t c)"), bank[7][:, 0:64]))
            nc.vector.tensor_tensor(kef[:, :, :].rearrange("p t c -> p (t c)"), bank[7][:, 64:128],
                                    gsum[:, :, :].rearrange("p t c -> p (t c)"), ALU.subtract)
            for cp in range(2):
                for par in range(2):
                    src = bank[cp][half(par), 0:64].rearrange("p (c x) -> p c x", c=TB)
                    src = src.rearrange("p c (z h r) -> p c z h r", z=2, r=2)[:, :, :, :, par]
                    dst = gend[half(par), :, :, :].rearrange("p (c r) z h -> p c r z h", r=2)[:, :, cp]
                    ins = nc.vector.tensor_copy(dst, src)
            ins.then_inc(OS["cumsd"], 1)
            dve.wait_ge(OS["ge"], 1)
            nc.vector.tensor_tensor(betaw[:, :, :], beta[:, :, :], eg[:, :, :], ALU.mult).then_inc(OS["cumsd"], 1)

        pair_names = ("g", "d", "qe", "clamp", "e", "em", "kk", "aa", "xb", "at", "atc", "xtb", "qk", "qkt", "ct", "y", "yc", "zx",
                      "zt", "xs", "xts", "tts", "u", "uc", "wt", "wtc", "kend", "ws", "vn", "su", "ss", "o", "oc", "qdec", "clear", "eb")
        N = {n: sig("gdn_" + n).sem for n in pair_names}
        TBS = ((2, 3), (3, 2), (0, 1), (1, 0))
        LEVELS = 5
        levels = table("levels").rearrange("p (z l c) -> p z l c", z=2, l=LEVELS)
        pairs = table("pairs").rearrange("p (z c) -> p z c", z=2)
        strict = table("strict").rearrange("p (z c) -> p z c", z=2)
        upto64 = table("upto64").rearrange("p (z c) -> p z c", z=2)
        eye64 = table("eye64")

        def heads(m):
            return m.rearrange("p (o c) -> p o c", o=1).broadcast_to((P, NH, C))

        def per_head(m, n=C):
            return m.rearrange("p (h o) -> p h o", o=1).broadcast_to((P, NH, n))

        def zb(z, i):
            return bank[4 * z + i]

        def gview(z, hq):
            return zb(z, hq)[:, :].rearrange("p (h i) -> p h i", h=4)

        def hb(b, n=C):
            return b[:, 0:4 * n].rearrange("p (h i) -> p h i", h=4)

        gdn_tables = sig("gdn_tables")

        def pe_pair(pe, p):
            lat = p >= 2
            us = [(z, 2 * p + z) for z in range(2)]
            if p == 0:
                pe.wait_ge(gdn_tables.sem, 16)
                pe.wait_ge(OS["cumsd"], 2)
                pe.wait_ge(OS["ktok"], QKB)
            for z, u in us:
                if p >= 1:
                    pe.wait_ge(N["vn"], 4 * p)
                    if p == 3:
                        pe.wait_ge(N["oc"], 4)
                for hd in range(NH):
                    col = la[:, TBS[p][z], z * NH + hd:z * NH + hd + 1].broadcast_to((P, P))
                    ins = pe.matmul(zb(z, hd // 4)[:, (hd % 4) * P:(hd % 4 + 1) * P], col, upto[:, z, :], start=True, stop=True)
                ins.then_inc(N["g"], 1)
            for z, u in us:
                if p >= 1:
                    pe.wait_ge(N["ss"], 4 * p)
                for par in range(2):
                    for c in range(2):
                        t = slice(TBS[p][z] * P + c * C, TBS[p][z] * P + (c + 1) * C)
                        for hp in range(4):
                            ins = pe.matmul(hb(zb(z, 2 + par))[half(c), hp, :], kf[half(par), hp, t], kf[half(par), hp, t],
                                            start=True, stop=True)
                ins.then_inc(N["kk"], 1)
            for z, u in us:
                pe.wait_ge(N["aa"], u + 1)
                if lat:
                    pe.wait_ge(N["qe"], u - 3)
                for c in range(2):
                    for hd in range(NH):
                        ins = pe.matmul(zb(z, 0)[half(c), hd * C:(hd + 1) * C], BA[half(c), z, hd, :], eye64[half(c), :],
                                        start=True, stop=True)
                ins.then_inc(N["at"], 1)
                if lat:
                    for par in range(2):
                        for c in range(2):
                            t = slice(TBS[p][z] * P + c * C, TBS[p][z] * P + (c + 1) * C)
                            for hp in range(4):
                                ins = pe.matmul(hb(zb(z, 2 + par))[half(c), hp, :], kf[half(par), hp, t],
                                                qf[half(par), hp, t], start=True, stop=True)
                    ins.then_inc(N["qk"], 1)
            for lv in range(LEVELS):
                for z, u in us:
                    v = LEVELS * 2 * p + 2 * lv + z
                    pe.wait_ge(N["ct"], v + 1)
                    if lv == 0:
                        pe.wait_ge(N["xb"], u + 1)
                        pe.wait_ge(N["atc"], u + 1)
                    else:
                        pe.wait_ge(N["xs"], (LEVELS - 1) * 2 * p + 2 * (lv - 1) + z + 1)
                        pe.wait_ge(N["xts"], v - 1)
                    for hd in range(NH):
                        ins = pe.matmul(gview(z, hd // 4)[:, hd % 4, :], BC[:, z, hd, :], BX[:, z, hd, :], start=True, stop=True)
                    ins.then_inc(N["y"], 1)
                for z, u in us:
                    v = LEVELS * 2 * p + 2 * lv + z
                    pe.wait_ge(N["yc"], v + 1)
                    if lv == 0:
                        pe.wait_ge(N["xtb"], u + 1)
                        if lat:
                            pe.wait_ge(N["qkt"], u - 3)
                    else:
                        pe.wait_ge(N["xts"], v - 1)
                    if lv < LEVELS - 1:
                        for hd in range(NH):
                            ins = pe.matmul(gview(z, 2 + hd // 4)[:, hd % 4, :], BXT[:, z, hd, :], BY[:, z, hd, :],
                                            start=True, stop=True)
                        ins.then_inc(N["zx"], 1)
                    for hd in range(NH):
                        ins = pe.matmul(gview(z, hd // 4)[:, hd % 4, :], BY[:, z, hd, :], BXT[:, z, hd, :],
                                        start=True, stop=True)
                    ins.then_inc(N["zt"], 1)
            for z, u in us:
                pe.wait_ge(N["tts"], 2 * u + 1)
                tb = TBS[p][z]
                for hd in range(NH):
                    ins = pe.matmul(gview(z, hd // 4)[:, hd % 4, :], BY[:, z, hd, :], vtok[:, tb, hd * P:(hd + 1) * P],
                                    start=True, stop=True)
                ins.then_inc(N["u"], 1)
                pe.wait_ge(N["tts"], 2 * u + 2)
                for hd in range(NH):
                    ins = pe.matmul(gview(z, 2)[half(hd % 2), hd // 2, :], ktk[:, tb, hd * C:(hd + 1) * C], BX[:, z, hd, :],
                                    start=True, stop=True)
                ins.then_inc(N["wt"], 1)
            for st in range(2):
                for z, u in us:
                    c = st if z == 0 else 1 - st
                    s = 4 * p + 2 * st + z
                    if st == 0:
                        pe.wait_ge(N["uc"], u + 1)
                        pe.wait_ge(N["wtc"], u + 1)
                    if s >= 2:
                        pe.wait_ge(N["ss"], s - 1)
                        for par in range(2):
                            for hp in range(4):
                                ins = pe.matmul(gview(z, par)[half(c), hp, :], WT(z, c)[half(par), hp, :],
                                                state(2 * p + st, z, hp, half(par)), start=True, stop=True)
                        ins.then_inc(N["ws"], 1)
                for z, u in us:
                    c = st if z == 0 else 1 - st
                    s = 4 * p + 2 * st + z
                    if not (p == 3 and st == 1):
                        pe.wait_ge(N["vn"], s + 1)
                        pe.wait_ge(N["kend"], u + 1)
                        for hd in range(NH):
                            ins = pe.matmul(zb(z, 2)[half(hd % 2), (hd // 2) * P:(hd // 2 + 1) * P],
                                            kends[half(c), z, hd, :], U[half(c), z, hd, :], start=True, stop=True)
                        ins.then_inc(N["su"], 1)
            if lat:
                pe.wait_ge(N["vn"], 4 * (p + 1))
                pe.wait_ge(N["qdec"], 2 * (p - 1))
                pe.wait_ge(N["qkt"], 2 * (p - 1))
                for b in range(4):
                    par, h2 = b // 2, b % 2
                    o = obank(b)
                    for i in range(2):
                        hd = 2 * (2 * h2 + i) + par
                        for z in range(2):
                            pe.matmul(o[:, (2 * i + z) * P:(2 * i + z + 1) * P], U[:, z, hd, :], QKT[:, z, hd, :],
                                      start=i == 0 and z == 0, stop=False, skip_group_check=True)
                    for i in range(2):
                        hp = 2 * h2 + i
                        for z in range(2):
                            for st in range(2):
                                c = st if z == 0 else 1 - st
                                at = (2 * i + z) * P + c * C
                                ins = pe.matmul(o[:, at:at + C], state(2 * p + st, z, hp, half(par)),
                                                qdc[half(par), z, hp, c * C:(c + 1) * C], start=False,
                                                stop=i == 1 and z == 1 and st == 1, skip_group_check=True)
                    ins.then_inc(N["o"], 1)

        def obank(b):
            return bank[(0, 1, 4, 5)[b]]

        def act_pair(act, p):
            lat = p >= 2
            us = [(z, 2 * p + z) for z in range(2)]
            for z, u in us:
                if lat:
                    act.wait_ge(N["d"], u + 1)
                    if p == 3:
                        act.wait_ge(N["o"], 4)
                    for par in range(2):
                        for hq in range(2):
                            src = gview(z, hq).rearrange("p (h r) i -> p h r i", r=2)[half(par), :, par, :]
                            ins = nc.scalar.activation(qdc[half(par), z, 2 * hq:2 * hq + 2, :], src, ACT.Exp)
                    ins.then_inc(N["qe"], 1)
            for z, u in us:
                act.wait_ge(N["clamp"], u + 1)
                nc.scalar.activation(BA[:, z], BA[:, z], ACT.Exp, scale=-1.0).then_inc(N["e"], 1)
                if lat:
                    nc.scalar.activation(BT[:, z], BT[:, z], ACT.Exp).then_inc(N["e"], 1)
            for z, u in us:
                act.wait_ge(N["at"], u + 1)
                if lat:
                    act.wait_ge(N["qkt"], u - 3)
                nc.scalar.activation(BT[:, z].rearrange("p h c -> p (h c)"), zb(z, 0)[:, :], ACT.Copy).then_inc(N["atc"], 1)
            for lv in range(LEVELS):
                for z, u in us:
                    v = LEVELS * 2 * p + 2 * lv + z
                    act.wait_ge(N["y"], v + 1)
                    if lv >= 1:
                        act.wait_ge(N["zt"], v - 1)
                    for hq in range(2):
                        ins = nc.scalar.activation(BY[:, z, 4 * hq:4 * hq + 4, :], gview(z, hq), ACT.Copy)
                    ins.then_inc(N["yc"], 1)
            for z, u in us:
                act.wait_ge(N["u"], u + 1)
                for hq in range(2):
                    ins = nc.scalar.activation(U[:, z, 4 * hq:4 * hq + 4, :], gview(z, hq), ACT.Copy)
                ins.then_inc(N["uc"], 1)
                act.wait_ge(N["wt"], u + 1)
                for c in range(2):
                    ins = nc.scalar.activation(WT(z, c), gview(z, 2)[:, :, c * C:(c + 1) * C], ACT.Copy)
                ins.then_inc(N["wtc"], 1)

        def dve_pair(dve, p):
            lat = p >= 2

            def below(lv, z):
                for c in range(2):
                    ins = nc.vector.tensor_tensor(BC[half(c), z, :, c * C:(c + 1) * C], BT[half(c), z],
                                                  heads(levels[:, z, lv, :])[half(c)], ALU.mult)
                ins.then_inc(N["ct"], 1)

            us = [(z, 2 * p + z) for z in range(2)]
            if p == 0:
                dve.wait_ge(gdn_tables.sem, 16)
                dve.wait_ge(N["clear"], 1)
            for z, u in us:
                dve.wait_ge(N["g"], u + 1)
                if p >= 1:
                    dve.wait_ge(N["su"], 4 * p)
                for c in range(2):
                    for hq in range(2):
                        col = gsum[half(c), TBS[p][z], z * NH + 4 * hq:z * NH + 4 * hq + 4]\
                            .rearrange("p (h o) -> p h o", o=1).broadcast_to((C, 4, C))
                        ins = nc.vector.tensor_tensor(BA[half(c), z, 4 * hq:4 * hq + 4, :],
                                                      gview(z, hq)[half(c), :, c * C:(c + 1) * C], col, ALU.subtract)
                ins.then_inc(N["d"], 1)
            for z, u in us:
                dve.wait_ge(N["d"], u + 1)
                if lat:
                    nc.vector.tensor_scalar(BT[:, z], BA[:, z], 0.0, None, ALU.min)
                nc.vector.tensor_scalar(BA[:, z], BA[:, z], 0.0, None, ALU.max).then_inc(N["clamp"], 1)
            for z, u in us:
                dve.wait_ge(N["e"], 2 * u - 3 if lat else u + 1)
                dve.wait_ge(N["eb"], u + 1)
                nc.vector.tensor_tensor(BA[:, z], BA[:, z], beta_below(z), ALU.mult).then_inc(N["em"], 1)
                dve.wait_ge(N["em"], u + 1)
                dve.wait_ge(N["kk"], u + 1)
                for par in range(2):
                    e = BA[:, z].rearrange("p (h r) c -> p h r c", r=2)[:, :, par, :]
                    ins = nc.vector.tensor_tensor(e, hb(zb(z, 2 + par)), e, ALU.mult)
                ins.then_inc(N["aa"], 1)
                if lat:
                    dve.wait_ge(N["aa"], u + 1)
                link_x(dve, BX, BA, z, pairs[:, z, :], N["xb"], N["aa"], u)
                if lat:
                    dve.wait_ge(N["qk"], u - 3)
                    dve.wait_ge(N["clear"], u - 2)
                    if p == 3:
                        dve.wait_ge(N["o"], 4)
                    for par in range(2):
                        for c in range(2):
                            e = BT[half(c), z].rearrange("p (h r) c -> p h r c", r=2)[:, :, par, :]
                            dst = QKT[half(c), z].rearrange("p (h r) i -> p h r i", r=2)[:, :, par, c * C:(c + 1) * C]
                            ins = nc.vector.tensor_tensor(dst, hb(zb(z, 2 + par))[half(c)], e, ALU.mult)
                    ins.then_inc(N["qkt"], 1)
            for z, u in us:
                dve.wait_ge(N["atc"], u + 1)
                below(0, z)
            for z, u in us:
                link_x(dve, BXT, BT, z, pairs[:, 1 - z, :], N["xtb"], N["atc"], u)
            for lv in range(LEVELS):
                for z, u in us:
                    if lv + 1 < LEVELS:
                        dve.wait_ge(N["y"], LEVELS * 2 * p + 2 * lv + z + 1)
                        below(lv + 1, z)
                for z, u in us:
                    v = LEVELS * 2 * p + 2 * lv + z
                    if lv < LEVELS - 1:
                        w = (LEVELS - 1) * 2 * p + 2 * lv + z
                        dve.wait_ge(N["zx"], w + 1)
                        for hq in range(2):
                            x = BX[:, z, 4 * hq:4 * hq + 4, :]
                            ins = nc.vector.tensor_tensor(x, x, gview(z, 2 + hq), ALU.subtract)
                        ins.then_inc(N["xs"], 1)
                    dve.wait_ge(N["zt"], v + 1)
                    for hq in range(2):
                        x = BXT[:, z, 4 * hq:4 * hq + 4, :]
                        ins = nc.vector.tensor_tensor(x, x, gview(z, hq), ALU.subtract)
                    ins.then_inc(N["xts"], 1)
                    if lv == LEVELS - 1:
                        dve.wait_ge(N["xts"], v + 1)
                        for dst, col in ((BY, beta), (BX, betaw)):
                            nc.vector.tensor_tensor(dst[:, z], BXT[:, z], per_head(col[:, TBS[p][z], z * NH:(z + 1) * NH], P),
                                                    ALU.mult).then_inc(N["tts"], 1)
            for st in range(2):
                for z, u in us:
                    c = st if z == 0 else 1 - st
                    s = 4 * p + 2 * st + z
                    dve.wait_ge(N["uc"], u + 1)
                    if s >= 2:
                        dve.wait_ge(N["ws"], s - 1)
                        for par in range(2):
                            x = U[half(c), z].rearrange("p (h r) v -> p h r v", r=2)[:, :, par, :]
                            ins = nc.vector.tensor_tensor(x, x, gview(z, par)[half(c)], ALU.subtract)
                        ins.then_inc(N["vn"], 1)
                    else:
                        dve.sem_inc(N["vn"], 1)
                for z, u in us:
                    c = st if z == 0 else 1 - st
                    s = 4 * p + 2 * st + z
                    if p == 3 and st == 1:
                        continue
                    dve.wait_ge(N["su"], s + 1)
                    if p == 3:
                        dve.wait_ge(N["o"], 4)
                    if s >= 2:
                        dve.wait_ge(N["ss"], s - 1)
                    for hp in range(4):
                        add = zb(z, 2)[:, hp * P:(hp + 1) * P]
                        old, new = state(2 * p + st, z, hp), state(2 * p + st + 1, z, hp)
                        if s < 2:
                            ins = nc.vector.tensor_copy(new, add)
                        else:
                            g = gend[:, 2 * TBS[p][z] + c, z, hp:hp + 1]
                            ins = nc.vector.scalar_tensor_tensor(out=new, in0=old, scalar=g, in1=add,
                                                                 op0=ALU.mult, op1=ALU.add)
                    ins.then_inc(N["ss"], 1)
            if lat:
                for b in range(4):
                    par, h2 = b // 2, b % 2
                    dve.wait_ge(N["o"], 4 * (p - 2) + b + 1)
                    for z in range(2):
                        t = slice(TBS[p][z] * P, (TBS[p][z] + 1) * P)
                        dst = mix[:, :, t].rearrange("p (h r) t -> p h r t", r=2)[:, 2 * h2:2 * h2 + 2, par, :]
                        src = obank(b)[:, :].rearrange("p (h z t) -> p h z t", h=2, z=2)[:, :, z, :]
                        if p == 2:
                            ins = nc.vector.tensor_copy(dst, src)
                        else:
                            ins = nc.vector.tensor_tensor(dst, dst, src, ALU.add)
                    ins.then_inc(N["oc"], 1)

        def link_x(dve, dst, src, z, mask, signal, source, u):
            dve.wait_ge(source, u + 1)
            for c in range(2):
                x = dst[half(c), z, :, c * C:(c + 1) * C]
                ins = nc.vector.tensor_tensor(x, src[half(c), z], heads(mask)[half(c)], ALU.mult)
            link(dve, ins)
            for c in range(2):
                x = dst[half(c), z, :, c * C:(c + 1) * C]
                ins = nc.vector.tensor_tensor(x, heads(eye64)[half(c)], x, ALU.subtract)
            ins.then_inc(signal, 1)

        def beta_below(z):
            return BY[:, z, :, 0:C]

        def pool_pair(pool, p):
            lat = p >= 2
            us = [(z, 2 * p + z) for z in range(2)]
            if p == 0:
                pool.wait_ge(gdn_tables.sem, 16)
                pool.wait_ge(evac_act.sem, sg_lin.base + VB)
                pool.wait_ge(OS["cums"], 1)
                pool.wait_ge(OS["cumsd"], 2)
                for x in (BX, BXT, BC):
                    nc.gpsimd.memset(x, 0.0)
                nc.gpsimd.memset(QKT, 0.0).then_inc(N["clear"], 1)
            for z, u in us:
                if p >= 1:
                    pool.wait_ge(N["u"], u - 1)
                nc.gpsimd.tensor_tensor(beta_below(z), heads(strict[:, z, :]),
                                        per_head(beta[:, TBS[p][z], z * NH:(z + 1) * NH]), ALU.mult).then_inc(N["eb"], 1)
            for z, u in us:
                if lat:
                    pool.wait_ge(N["e"], 2 * u - 2)
                    nc.gpsimd.tensor_tensor(BT[:, z], BT[:, z], heads(upto64[:, z, :]), ALU.mult).then_inc(N["clear"], 1)
            for z, u in us:
                tb = TBS[p][z]
                if lat:
                    pool.wait_ge(N["qe"], u - 3)
                    nc.gpsimd.tensor_tensor(qdc[:, z], qdc[:, z], qf[:, :, tb * P:(tb + 1) * P], ALU.mult)\
                        .then_inc(N["qdec"], 1)
            for z, u in us:
                tb = TBS[p][z]
                pool.wait_ge(OS["ge"], 3)
                pool.wait_ge(N["xb"], u + 1)
                pool.wait_ge(N["at"], u + 1)
                nc.gpsimd.tensor_tensor(kends[:, z], ktk[:, tb, :].rearrange("p (h c) -> p h c", h=NH),
                                        per_head(kef[:, tb, z * NH:(z + 1) * NH]), ALU.mult).then_inc(N["kend"], 1)

        OT = {n: sig("odd_out_" + n).sem for n in ("squares", "sums", "roots", "merged")}
        osq, oroot = a[:, 0:4, :], a[:, 4:8, :]

        def obuf(x, i):
            return x[:, i, :]

        def two_heads(i):
            return mix[:, 2 * i:2 * i + 2, 0:LAT]

        def as_heads(x):
            return x.rearrange("p (h t) -> p h t", h=2)

        def pe_odd_out(pe):
            for i in range(4):
                pe.wait_ge(OT["squares"], i + 1)
                pe.matmul(bank[i][:, :], ones, obuf(osq, i), start=True, stop=True).then_inc(OT["sums"], 1)

        def act_odd_out(act):
            act.wait_ge(N["oc"], 8)
            for i in range(4):
                nc.scalar.activation(as_heads(obuf(osq, i)), two_heads(i), ACT.Square).then_inc(OT["squares"], 1)
            for i in range(4):
                act.wait_ge(OT["sums"], 4 if i >= 2 else i + 1)
                nc.scalar.activation(obuf(oroot, i), bank[i][:, :], ACT.Ln, scale=1.0 / NDV, bias=eps_col)\
                    .then_inc(OT["roots"], 1)
            for i in range(4):
                act.wait_ge(OT["roots"], i + 1)
                nc.scalar.activation(obuf(oroot, i), obuf(oroot, i), ACT.Exp, scale=-0.5).then_inc(OT["roots"], 1)

        def dve_odd_out(dve):
            for i in range(4):
                dve.wait_ge(OT["roots"], 4 + i + 1)
                link(dve, nc.vector.scalar_tensor_tensor(out=two_heads(i), in0=two_heads(i), scalar=vector("gdn_o_norm"),
                                                         in1=as_heads(obuf(oroot, i)), op0=ALU.mult, op1=ALU.mult))
                nc.vector.tensor_tensor(two_heads(i), two_heads(i), sg[:, 2 * i:2 * i + 2, :], ALU.mult)\
                    .then_inc(OT["merged"], 1)

        odd_x = Operand(lambda k: mix[:, k, 0:LAT], KB, slice(0, LAT))
        odd_out = Projection(lambda n, r: dyn(d["gdn_w_out"][0], n * P), whole(), KB, LAT, split_x(LAT), evac_dve)
        odd_res = Residual(odd_out, 1, 0)
        mlp1 = Mlp(1, LAT)
        final = Norm(lambda k: h[:, k, 0:LAT], lambda k: a[:, k, 0:LAT], KB, LAT, D)

        def pe_layer1(pe):
            n3.norm.pe_sums(pe)
            pe_odd_in(pe)
            for p in range(4):
                pe_pair(pe, p)
            pe_odd_out(pe)
            odd_out.pe(pe, lambda k: odd_x.ready(pe, k))
            mlp1.norm.norm.pe_sums(pe)
            mlp1.pe(pe)
            final.pe_sums(pe)

        def act_layer1(act):
            n3.norm.act_squares(act, squares_ready(mlp0.last()))
            n3.norm.act_root(act)
            n3.act(act)
            act_odd_in(act)
            for p in range(4):
                act_pair(act, p)
            act_odd_out(act)
            for k in range(KB):
                act.wait_ge(OT["merged"], k // 2 + 1)
                odd_x.act(act, k)
            odd_out.walk(act, split_hi)
            mlp1.norm.norm.act_squares(act, squares_ready(odd_out.lin.base + KB))
            mlp1.norm.norm.act_root(act)
            mlp1.norm.act(act)
            mlp1.act(act)
            final.act_squares(act, squares_ready(mlp1.last()))
            final.act_root(act)

        def dve_layer1(dve):
            n3.norm.dve_squares(dve, squares_ready(mlp0.last()))
            n3.dve(dve)
            dve_odd_in(dve)
            for p in range(4):
                dve_pair(dve, p)
            dve_odd_out(dve)
            for k in range(KB):
                odd_x.dve(dve, k)
            odd_res.dve(dve)
            mlp1.norm.norm.dve_squares(dve, squares_ready(odd_out.lin.base + KB))
            mlp1.norm.dve(dve)
            mlp1.dve(dve)
            final.dve_squares(dve, squares_ready(mlp1.last()))
            final.wait(dve)
            for k in range(KB):
                nc.vector.scalar_tensor_tensor(out=h[:, k, 0:LAT], in0=h[:, k, 0:LAT], scalar=vector("final_norm")[:, k:k + 1],
                                               in1=rstd[:, 0:LAT], op0=ALU.mult, op1=ALU.mult).then_inc(entered.sem, 1)

        def pool_layer1(pool):
            for p in range(4):
                pool_pair(pool, p)

        entered = sig("entered")

        ca = Carve()
        hid_b = tuple(x[:, 0:F2B * LAT].rearrange("p (n t) -> p n t", t=LAT) for x in (hid_hi, hid_lo))
        xc, gr, gi = (ca(LB, LAT) for _ in range(3))
        shk = ca(4, LAT)
        assert ca.at <= F2B * LAT
        ca.at = F2B * LAT
        mk, mv = ca(2, 2, NMEM), ca(2, NMEM // P, MEMH * HD)
        lam8 = ca(3, LB)
        nsink = ca(SQH)
        assert ca.at <= HIDDEN
        ca.at = HIDDEN
        ga, gm, gelu = (ca(LB, LAT) for _ in range(3))
        shv = ca(2, SKH * HD)
        mq = ca(2, LAT)
        att_room = [ca(T) for _ in range(4)] + [tmp[:, 0, :], tmp[:, 1, :]]
        qs = xc
        assert ca.at <= 2 * HIDDEN
        w_gates = [mix[:, 0:LB, LAT + z * P:LAT + (z + 1) * P] for z in range(2)]
        b2_names = ("mem", "memn", "pre", "post", "scaled", "lr_c", "lr_g", "lr_a", "lr_m", "lr_s", "rot", "roped", "small", "ffn", "ffn_values", "gate_w", "gate_mm")
        B = {n: sig("b2_" + n) for n in b2_names}
        mem = [h[:, k, LAT:T] for k in range(KB)]
        memn = [a[:, k, LAT:T] for k in range(KB)]

        class Weighted:

            def __init__(self, w):
                self.w = w
                self.norm = Norm(lambda k: h[:, k, 0:LAT], lambda k: a[:, k, 0:LAT], KB, LAT, D)
                self.base = B["pre"].take(KB)
                self.x = Operand(lambda k: a[:, k, 0:LAT], KB, slice(0, LAT))

            def dve(self, dve):
                self.norm.wait(dve)
                for k in range(KB + 1):
                    if k < KB:
                        nc.vector.scalar_tensor_tensor(out=a[:, k, 0:LAT], in0=h[:, k, 0:LAT], scalar=self.w[:, k:k + 1],
                                                       in1=rstd[:, 0:LAT], op0=ALU.mult, op1=ALU.mult)\
                            .then_inc(B["pre"].sem, 1)
                    if k >= 1:
                        if k == 1:
                            dve.wait_ge(B["pre"].sem, self.base + 1)
                        self.x.dve(dve, k - 1)

            def act(self, act):
                self.norm.act_root(act)
                for k in range(KB):
                    act.wait_ge(B["pre"].sem, self.base + k + 1)
                    self.x.act(act, k)

            def ready(self, pe, k):
                self.x.ready(pe, k)

        class Post:

            def __init__(self, proj, w):
                self.proj, self.w = proj, w
                self.norm = Norm(lambda k: a[:, k, 0:LAT], lambda k: mix[:, k, LAT:T], KB, LAT, D)
                self.base = B["post"].take(KB)

            def act_copies(self, act):
                def empty(i, n, b):
                    act.wait_ge(block_done.sem, self.proj.done(n))
                    nc.scalar.activation(a[:, bass.ds(n, 1), 0:LAT].rearrange("p o t -> p (o t)"),
                                         self.proj.lin.bank(b)[:, 0:LAT], ACT.Copy).then_inc(evac_act.sem, 1)
                self.proj.walk(act, split_hi, empty)

            def copied(self, eng, k):
                if k < 2:
                    eng.wait_ge(evac_act.sem, self.proj.lin.base + KB)

            def act(self, act):
                self.act_copies(act)
                self.norm.act_squares(act, self.copied)
                self.norm.act_root(act)

            def dve(self, dve):
                self.proj.walk(dve, split_lo)
                self.norm.dve_squares(dve, self.copied)
                self.norm.wait(dve)
                for k in range(KB):
                    link(dve, nc.vector.scalar_tensor_tensor(out=a[:, k, 0:LAT], in0=a[:, k, 0:LAT], scalar=self.w[:, k:k + 1],
                                                             in1=rstd[:, 0:LAT], op0=ALU.mult, op1=ALU.mult))
                    nc.vector.tensor_tensor(h[:, k, 0:LAT], h[:, k, 0:LAT], a[:, k, 0:LAT], ALU.add)\
                        .then_inc(B["post"].sem, 1)

            def ready(self, eng, k):
                eng.wait_ge(B["post"].sem, self.base + k + 1)

        class Blocks:

            def __init__(self, weight, blocks, start=0, tokens=()):
                self.blocks, self.tokens, self.start = blocks, tokens, start
                self.tiles = Tiles(len(blocks) + (2 if tokens else 0), lambda t: cols_of(weight, P * t, P))
                self.n = len(blocks) + len(tokens)
                self.lin = Linear(evac_act, self.n)

            def pe(self, pe, ready):
                m = len(self.blocks)
                for n in range(2):
                    self.tiles.wait(pe, n)
                    self.lin.free(pe, n)
                for ins in split_products(pe, [self.lin.bank(n)[:, 0:LAT] for n in range(2)],
                                          [self.tiles.parts(n) for n in range(2)], split_x(LAT, self.start), KB,
                                          lambda k: ready(pe, k)):
                    ins.then_inc(block_done.sem, UNITS)
                for n in range(2, self.n):
                    self.lin.free(pe, n)
                    o = self.lin.bank(n)
                    if n < m:
                        self.tiles.wait(pe, n)
                        split_product(pe, o[:, 0:LAT], self.tiles.parts(n), split_x(LAT, self.start), KB)\
                            .then_inc(block_done.sem, UNITS)
                    else:
                        if n == m:
                            self.tiles.wait(pe, m)
                            self.tiles.wait(pe, m + 1)
                        split_product(pe, o[:, 0:256].rearrange("p (b c) -> p b c", b=2), split_x(P, self.start + (n - m) * P),
                                      self.tiles.two(m), KB).then_inc(block_done.sem, 1 if n + 1 < self.n else 2 * UNITS - 1)

            def done(self, n):
                m = len(self.blocks)
                return self.tiles.done(n) if n < m else self.tiles.done(m, 0 if n + 1 < self.n else 2 * UNITS - 1)

            def act(self, act, n, extra=None):
                m = len(self.blocks)
                act.wait_ge(block_done.sem, self.done(n))
                o = self.lin.bank(n)[:, 0:LAT]
                if extra is not None and n < m:
                    extra(n, o)
                dst, func = self.blocks[n] if n < m else (self.tokens[n - m], ACT.Copy)
                nc.scalar.activation(dst, o, func).then_inc(evac_act.sem, 1)
                self.ahead(act, n)

            def ahead(self, act, n):
                m = len(self.blocks)
                if n < m:
                    split_hi(act, self.tiles.first + n + AHEAD)
                elif n + 1 == self.n:
                    for t in range(m, m + 2):
                        split_hi(act, self.tiles.first + t + AHEAD)

        pre_a = Weighted(vector("norm_mix_pre_2")[:, 0:KB])
        mem_norm = Norm(lambda k: mem[k], lambda k: memn[k], KB, NMEM, D)
        mem_x = Operand(lambda k: memn[k], KB, slice(LAT, T))
        in_a = Blocks(d["w_in_a_2"][0], [(xc[:, i, :], ACT.Identity) for i in range(LB)]
                      + [(gelu[:, i, :], ACT.Gelu_apprx_tanh) for i in range(LB)] + [(mq[:, i, :], ACT.Copy) for i in range(2)])
        gate_lin = Linear(evac_act, 2 * LB)
        mem_blocks = [Blocks(d["w_mem_kv_2"][l], [(mk[:, l, i, :], ACT.Copy) for i in range(2)], LAT,
                             [mv[:, l, i, :] for i in range(2)]) for l in range(2)]

        def memory_units(l):
            return [dict(q=mq[half(hd % 2), hd // 2, q:q + P], k=mk[half(hd % 2), l, hd // 2, :],
                         v=[mv[:, l, b, hd * HD:(hd + 1) * HD] for b in range(2)], rows=half(hd % 2),
                         out=mix[half(hd % 2), 6 + hd // 2, q:q + P]) for hd in range(MEMH) for q in (0, P)]

        mem_att_a = Attention(memory_units(0), HD ** -0.5, att_room)

        class Ffn:

            def __init__(self, l):
                self.pre = Weighted(vector("norm_ffn_pre_2")[:, l * KB:(l + 1) * KB])
                w = d["w_ffn_in_2"][l]
                self.up = Projection(None, whole(), 2 * F2B, LAT, split_x(LAT), evac_dve, banks=4)
                self.up.tiles.place = lambda i, t: dyn(w, i * (2 * P) + (P * (t // 2) + FF2 * (t % 2)))
                self.down = Projection(lambda n, r: dyn(d["w_ffn_out_2"][l], n * P, r[0] * P, r[1]), whole(F2B), KB, LAT,
                                       tuple((lambda k, x=x: x[:, k, :]) for x in hid_b), evac_act, body=3 * AHEAD)
                self.post = Post(self.down, vector("norm_ffn_post_2")[:, l * KB:(l + 1) * KB])
                self.silus, self.values = B["ffn"].take(F2B), B["ffn_values"].take(2 * F2B)

            def pe(self, pe):
                self.pre.norm.pe_sums(pe)
                self.up.pe(pe, lambda k: self.pre.ready(pe, k))
                pe.wait_ge(evac_dve.sem, self.up.lin.base + 2 * F2B)
                self.down.pe(pe)
                self.post.norm.pe_sums(pe)

            def act(self, act, ready):
                self.pre.norm.act_squares(act, ready)
                self.pre.act(act)

                def empty(i, n, b):
                    if b % 2 == 0:
                        act.wait_ge(block_done.sem, self.up.done(n))
                        act.wait_ge(evac_dve.sem, n + (self.up.lin.base - 2))
                        nc.scalar.activation(tmp[:, b // 2, 0:LAT], bank[b][:, 0:LAT], ACT.Silu).then_inc(B["ffn"].sem, 1)
                self.up.walk(act, split_hi, empty)
                self.post.act(act)

            def dve(self, dve, ready):
                self.pre.norm.dve_squares(dve, ready)
                self.pre.dve(dve)

                def empty(i, n, b):
                    if b % 2 == 0:
                        return
                    u = b // 2
                    j = i * 2 + u
                    at, val = bass.ds(j, 1), B["ffn_values"].sem
                    hi, lo = (x[:, at, :].rearrange("p o t -> p (o t)") for x in hid_b)
                    dve.wait_ge(B["ffn"].sem, j + (self.silus + 1))
                    dve.wait_ge(block_done.sem, self.up.done(n))
                    nc.vector.tensor_tensor(a[:, u, 0:LAT], tmp[:, u, 0:LAT], bank[b][:, 0:LAT], ALU.mult).then_inc(val, 1)
                    dve.wait_ge(val, j * 2 + (self.values + 1))
                    nc.vector.tensor_copy(hi, a[:, u, 0:LAT]).then_inc(val, 1)
                    dve.wait_ge(val, j * 2 + (self.values + 2))
                    nc.vector.tensor_tensor(lo, a[:, u, 0:LAT], hi.bitcast(F32), ALU.subtract).then_inc(evac_dve.sem, 2)
                self.up.walk(dve, split_lo, empty)
                self.post.dve(dve)

        out_x = [Operand(lambda k: mix[:, k, 0:LAT], KB, slice(0, LAT))]
        out_a = Projection(lambda n, r: dyn(d["w_out_2"][0], n * P), whole(), KB, LAT, split_x(LAT), evac_act)
        post_a = Post(out_a, vector("norm_mix_post_2")[:, 0:KB])
        ffn_a = Ffn(0)
        pre_kv = Weighted(vector("norm_kv_2"))
        kv_sh = Blocks(d["w_kv_shared_2"], [(shk[:, i, :], ACT.Copy) for i in range(2)], 0, [shv[:, i, :] for i in range(2)])
        pre_b = Weighted(vector("norm_mix_pre_2")[:, KB:2 * KB])
        in_b = Blocks(d["w_in_b_2"][0], [(qs[:, i, :], ACT.Copy) for i in range(6)] + [(mq[:, i, :], ACT.Copy) for i in range(2)])
        window = table("window")
        sinks = vector("sinks_2")
        swa_units = []
        for hd in range(SQH):
            kv, par = hd // (SQH // SKH), hd % 2
            kx = kv // 2 + (0 if kv % 2 == par else 2)
            for qb in range(2):
                nk = (qb + 1) * P
                swa_units.append(dict(q=qs[half(par), hd // 2, qb * P:(qb + 1) * P], k=shk[half(par), kx, 0:nk],
                                      v=[shv[:, b, kv * HD:(kv + 1) * HD] for b in range(qb + 1)], rows=half(par),
                                      out=mix[half(par), hd // 2, qb * P:(qb + 1) * P], mask=window[:, 2 * P - nk:2 * P],
                                      sink=(sinks[:, hd:hd + 1], nsink[:, hd:hd + 1])))
        att_b = Attention(swa_units + memory_units(1), HD ** -0.5, att_room)
        out_x.append(Operand(lambda k: mix[:, k, 0:LAT], KB, slice(0, LAT)))
        out_b = Projection(lambda n, r: dyn(d["w_out_2"][1], n * P), whole(), KB, LAT, split_x(LAT), evac_act)
        post_b = Post(out_b, vector("norm_mix_post_2")[:, KB:2 * KB])
        ffn_b = Ffn(1)
        scos, ssin = table("swa_rope")[:, 0:LAT], table("swa_rope")[:, LAT:2 * LAT]
        srot = table("swa_rope")[:, 2 * LAT:2 * LAT + P]

        def pe_rotate(pe, x, groups, base, evac_total):
            pe.wait_ge(evac_act.sem, evac_total)
            for g in range(groups):
                pe.matmul(bank[2 + g][:, :], srot, x[:, 2 * g:2 * g + 2, :], start=True, stop=True).then_inc(B["rot"].sem, 1)

        def dve_rotate(dve, x, groups, base):
            cos = scos.rearrange("p (o t) -> p o t", o=1).broadcast_to((P, 2, LAT))
            sin = ssin.rearrange("p (o t) -> p o t", o=1).broadcast_to((P, 2, LAT))
            for g in range(groups):
                y = x[:, 2 * g:2 * g + 2, :]
                s = tmp[:, g % 2, :].rearrange("p (h t) -> p h t", h=2)
                dve.wait_ge(B["rot"].sem, base + g + 1)
                nc.vector.tensor_tensor(s, bank[2 + g][:, :].rearrange("p (h t) -> p h t", h=2), sin, ALU.mult)
                link(dve, nc.vector.tensor_tensor(y, y, cos, ALU.mult))
                ins = nc.vector.tensor_tensor(y, y, s, ALU.add)
                ins.then_inc(B["roped"].sem, 1)
                dve.wait_ge(B["roped"].sem, base + g + 1)

        def entered_ready(eng, k):
            eng.wait_ge(entered.sem, k + 1)

        def pe_second(pe):
            pre_a.norm.pe_sums(pe)
            in_a.pe(pe, pre_a.ready)
            mem_norm.pe_sums(pe)
            for j in range(2):
                if j == 0:
                    pe.wait_ge(B["gate_w"].sem, 32)
                for n in range(LB):
                    if j == 0:
                        pe.wait_ge(B["lr_c"].sem, n + 1)
                    gate_lin.free(pe, LB * j + n)
                    pe.matmul(gate_lin.bank(LB * j + n)[:, 0:LAT], w_gates[j][:, n, :], xc[:, n, :],
                              start=True, stop=True).then_inc(B["gate_mm"].sem, 1)
            for m in mem_blocks:
                m.pe(pe, mem_x.ready)
            mem_att_a.pe(pe, lambda pe, i: None)
            out_a.pe(pe, lambda k: out_x[0].ready(pe, k))
            post_a.norm.pe_sums(pe)
            ffn_a.pe(pe)
            pre_kv.norm.pe_sums(pe)
            kv_sh.pe(pe, pre_kv.ready)
            pe_rotate(pe, shk, 2, 0, kv_sh.lin.base + 4)
            pre_b.norm.pe_sums(pe)
            in_b.pe(pe, pre_b.ready)
            pe_rotate(pe, qs, 3, 2, in_b.lin.base + 8)
            att_b.pe(pe, lambda pe, i: pe.wait_ge(B["roped"].sem, 5) if i == 0 else None)
            out_b.pe(pe, lambda k: out_x[1].ready(pe, k))
            post_b.norm.pe_sums(pe)
            ffn_b.pe(pe)

        def act_second(act):
            pre_a.norm.act_squares(act, entered_ready)
            pre_a.act(act)
            mem_norm.act_squares(act, lambda e, k: e.wait_ge(B["mem"].sem, 32))
            cw = vector("conv_w_2").rearrange("p (t n) -> p t n", t=4)
            for n in range(LB):
                act.wait_ge(block_done.sem, in_a.done(n))
                nc.scalar.activation(xc[:, n, :], in_a.lin.bank(n)[:, 0:LAT], ACT.Identity, scale=cw[:, 3, n:n + 1],
                                     bias=vector("conv_b_2")[:, n:n + 1]).then_inc(B["scaled"].sem, 1)
                act.wait_ge(B["lr_c"].sem, n + 1)
                act.sem_inc(evac_act.sem, 1)
                in_a.ahead(act, n)
            for n in range(LB, 2 * LB + 2):
                in_a.act(act, n)
            mem_norm.act_root(act)
            for k in range(KB):
                act.wait_ge(B["memn"].sem, k + 1)
                mem_x.act(act, k)
            nc.scalar.activation(lam8[:, 0, :], vector("lru_lambda_2"), ACT.Abs).then_inc(B["small"].sem, 1)
            act.wait_ge(B["small"].sem, 1)
            nc.scalar.activation(lam8[:, 0, :], lam8[:, 0, :], ACT.Exp, scale=-1.0).then_inc(B["small"].sem, 1)
            act.wait_ge(B["small"].sem, 2)
            nc.scalar.activation(lam8[:, 0, :], lam8[:, 0, :], ACT.Ln, bias=1.0).then_inc(B["small"].sem, 1)
            for j, (dst, name) in enumerate(((gr, "b_gate_r_2"), (gi, "b_gate_i_2"))):
                for n in range(LB):
                    act.wait_ge(B["gate_mm"].sem, LB * j + n + 1)
                    nc.scalar.activation(dst[:, n, :], gate_lin.bank(LB * j + n)[:, 0:LAT], ACT.Sigmoid,
                                         bias=vector(name)[:, n:n + 1]).then_inc(evac_act.sem, 1)
            act.wait_ge(B["small"].sem, 4)
            act.wait_ge(evac_act.sem, gate_lin.base + 2 * LB)
            for n in range(LB):
                nc.scalar.activation(ga[:, n, :], gr[:, n, :], ACT.Exp, scale=lam8[:, 1, n:n + 1])
                nc.scalar.activation(gm[:, n, :], gr[:, n, :], ACT.Exp, scale=lam8[:, 2, n:n + 1]).then_inc(B["lr_a"].sem, 1)
            act.wait_ge(B["lr_m"].sem, 1)
            nc.scalar.activation(gm[:, :, :], gm[:, :, :], ACT.Sqrt).then_inc(B["lr_g"].sem, 1)
            for m in mem_blocks:
                for n in range(4):
                    m.act(act, n)
            mem_att_a.act(act)
            act.wait_ge(B["lr_s"].sem, 1)
            act.wait_ge(att_out.sem, mem_att_a.b[att_out.sem] + len(mem_att_a.units))
            for k in range(KB):
                out_x[0].act(act, k)
            post_a.act(act)
            ffn_a.act(act, post_a.ready)
            pre_kv.norm.act_squares(act, ffn_a.post.ready)
            pre_kv.act(act)

            def swapped(n, o):
                for x in range(2):
                    nc.scalar.activation(shk[half(1 - x), 2 + n, :], o[half(x), :], ACT.Copy)
            for n in range(4):
                kv_sh.act(act, n, swapped)
            pre_b.norm.act_squares(act)
            pre_b.act(act)
            for n in range(8):
                in_b.act(act, n)
            att_b.act(act)
            act.wait_ge(att_out.sem, att_b.b[att_out.sem] + len(att_b.units))
            for k in range(KB):
                out_x[1].act(act, k)
            post_b.act(act)
            ffn_b.act(act, post_b.ready)

        def dve_second(dve):
            pre_a.norm.dve_squares(dve, entered_ready)
            pre_a.dve(dve)
            mem_norm.dve_squares(dve, lambda e, k: e.wait_ge(B["mem"].sem, 32))
            cw = vector("conv_w_2").rearrange("p (t n) -> p t n", t=4)
            for n in range(LB):
                dve.wait_ge(B["scaled"].sem, n + 1)
                x = in_a.lin.bank(n)[:, 0:LAT]
                for s in (1, 2, 3):
                    ins = nc.vector.scalar_tensor_tensor(out=xc[:, n, s:], in0=x[:, 0:LAT - s], scalar=cw[:, 3 - s, n:n + 1],
                                                         in1=xc[:, n, s:], op0=ALU.mult, op1=ALU.add)
                    if s < 3:
                        link(dve, ins)
                ins.then_inc(B["lr_c"].sem, 1)
                split_lo(dve, in_a.tiles.first + n + AHEAD)
            for n in range(LB, in_a.tiles.n):
                split_lo(dve, in_a.tiles.first + n + AHEAD)
            mem_norm.wait(dve)
            for k in range(KB):
                nc.vector.scalar_tensor_tensor(out=memn[k], in0=mem[k], scalar=vector("mem_norm_2")[:, k:k + 1],
                                               in1=rstd[:, 0:LAT], op0=ALU.mult, op1=ALU.mult).then_inc(B["memn"].sem, 1)
                if k >= 1:
                    mem_x.dve(dve, k - 1)
            mem_x.dve(dve, KB - 1)
            dve.wait_ge(B["small"].sem, 3)
            link(dve, nc.vector.tensor_scalar(lam8[:, 2, :], vector("lru_lambda_2"), 0.0, None, ALU.min))
            link(dve, nc.vector.tensor_tensor(lam8[:, 2, :], lam8[:, 2, :], lam8[:, 0, :], ALU.subtract))
            nc.vector.tensor_scalar(lam8[:, 1, :], lam8[:, 2, :], 8.0, None, ALU.mult)
            link(dve, nc.vector.tensor_scalar(lam8[:, 2, :], lam8[:, 2, :], 16.0, None, ALU.mult))
            nc.vector.tensor_scalar(nsink, sinks, -1.0, None, ALU.mult).then_inc(B["small"].sem, 1)
            dve.wait_ge(evac_act.sem, gate_lin.base + 2 * LB)
            link(dve, nc.vector.tensor_tensor(gi[:, :, :], gi[:, :, :], xc[:, :, :], ALU.mult))
            dve.wait_ge(B["lr_a"].sem, LB)
            link(dve, nc.vector.tensor_scalar(gm[:, :, :], gm[:, :, :], -1.0, 1.0, ALU.mult, ALU.add))
            nc.vector.tensor_scalar(gm[:, :, :], gm[:, :, :], 0.0, None, ALU.max).then_inc(B["lr_m"].sem, 1)
            dve.wait_ge(B["lr_g"].sem, 1)
            link(dve, nc.vector.memset(gm[:, :, 0:1], 1.0))
            link(dve, nc.vector.tensor_tensor(gi[:, :, :], gi[:, :, :], gm[:, :, :], ALU.mult))
            for n in range(LB):
                ins = nc.vector.tensor_tensor_scan(gr[:, n, :], ga[:, n, :], gi[:, n, :], 0.0, ALU.mult, ALU.add)
            link(dve, ins)
            nc.vector.tensor_tensor(mix[:, 0:LB, 0:LAT], gr[:, :, :], gelu[:, :, :], ALU.mult).then_inc(B["lr_s"].sem, 1)
            for m in mem_blocks:
                follow(dve, split_lo, m.tiles)
            mem_att_a.dve(dve)
            for k in range(KB):
                out_x[0].dve(dve, k)
            post_a.dve(dve)
            ffn_a.dve(dve, post_a.ready)
            pre_kv.norm.dve_squares(dve, ffn_a.post.ready)
            pre_kv.dve(dve)
            follow(dve, split_lo, kv_sh.tiles)
            dve_rotate(dve, shk, 2, 0)
            pre_b.norm.dve_squares(dve)
            pre_b.dve(dve)
            follow(dve, split_lo, in_b.tiles)
            dve_rotate(dve, qs, 3, 2)
            att_b.dve(dve)
            for k in range(KB):
                out_x[1].dve(dve, k)
            post_b.dve(dve)
            ffn_b.dve(dve, post_b.ready)

        def sp_end(sp):
            for k in range(0, KB, 4):
                sp.wait_ge(B["post"].sem, ffn_b.post.base + k + 4)
                sp.dma_start(out[:, k:k + 4, :], h[:, k:k + 4, 0:LAT]).then_inc(stored.sem, 16)
            sp.wait_ge(stored.sem, 32)

        stored = sig("stored")


        def sp_tiles(sp, g):
            def load(t, source, loop=None):
                at = g.first + t
                dst = g.landing(t)
                if g.body is not None:
                    dst = dst[:, 0:g.rows[t % len(g.rows)][1], :]
                if at >= RAW:
                    sp.wait_ge(lo_done[(at - RAW) % AHEAD].sem, after((at - RAW) // AHEAD + 1, loop, 1 / AHEAD))
                sp.dma_start(dst, source).then_inc(here[at % RAW].sem, 16)

            if g.body is None:
                for t in range(g.n):
                    if g is ada_a_tiles and t == RAW:
                        sp.dma_start(h[:, :, :], d["xt"]).then_inc(loaded.sem, 16)
                        sp.dma_start(tab[:, 0:TURN_AT + TURN_SIZES[0]], d["tab"]).then_inc(loaded.sem, 16)
                    load(t, g.source(t))
            else:
                with sp.Fori(0, g.n // g.body) as i:
                    for t in range(g.body):
                        load(t, g.place(i, t), (i, g.body))

        def turn(i):
            return tab[:, TURN_AT:TURN_AT + TURN_SIZES[i]]

        def arrived(eng, k):
            if k < 2:
                eng.wait_ge(loaded.sem, 16 * SMALL)

        block = ctx.enter_context(nc.Block())

        @block.sync
        def _(sp):
            sp.dma_start(vec[:, :], d["vec"]).then_inc(vec_here.sem, 16)
            for group in Tiles.every:
                if group is even_tiles:
                    sp.dma_start(w_uq, cols_of(d["mla_w_uq"][0], 0, MH * MQK, kb=QB)).then_inc(mla_here.sem, 16)
                    sp.dma_start(w_ukv, cols_of(d["mla_w_ukv"][0], 0, MH * (NOPE + MV), kb=KVB)).then_inc(mla_here.sem, 16)
                if group is odd_tiles:
                    sp.wait_ge(G["merged"], GH)
                    sp.dma_start(turn(1), d["tab1"]).then_inc(gdn_tables.sem, 16)
                if group is mlp1.parts[0][0].tiles:
                    sp.wait_ge(scaled.sem, n3.scaled + KB)
                    sp.dma_start(h[:, :, LAT:T], d["memt"]).then_inc(B["mem"].sem, 16)
                    sp.wait_ge(N["oc"], 8)
                    sp.dma_start(turn(2), d["tab2"]).then_inc(B["mem"].sem, 16)
                    for z, name in enumerate(("w_gate_r_2", "w_gate_i_2")):
                        sp.dma_start(w_gates[z], d[name][0].rearrange("h i j -> i h j")).then_inc(B["gate_w"].sem, 16)
                sp_tiles(sp, group)
            sp_end(sp)


        @block.gpsimd
        def _(pool):
            pool_glow_ones(pool)
            pool_shared_key(pool)
            pool_layer1(pool)

        @block.scalar
        def _(act):
            act_silu_c(act)
            for g in range(AHEAD):
                split_hi(act, g)
            ada_a.act(act, lambda: n1.norm.act_squares(act, arrived), lambda: n1.norm.act_root(act))
            n1.act(act)
            act_even_in(act)
            norm_q.act_squares(act)
            norm_q.act_root(act)
            norm_kv.act_squares(act)
            norm_kv.act_root(act)
            act_mla_project(act)
            act_mla(act)
            act_gla(act)
            act_rest0(act)
            act_layer1(act)
            act_second(act)

        @block.vector
        def _(dve):
            dve_silu_c(dve)
            for g in range(AHEAD):
                split_lo(dve, g)
            ada_a.dve(dve, lambda: n1.norm.dve_squares(dve, arrived))
            n1.dve(dve)
            dve_even_in(dve)
            norm_q.dve_squares(dve, lambda e, k: e.wait_ge(evac_act.sem, even_lin.base + 5))
            dve_ranks(dve)
            dve_rope(dve)
            dve_mla(dve)
            dve_gla(dve)
            dve_rest0(dve)
            dve_layer1(dve)
            dve_second(dve)

        @block.tensor
        def _(pe):
            ada_a.pe(pe, lambda: n1.norm.pe_sums(pe))
            pe_even_in(pe)
            norm_q.pe_sums(pe)
            norm_kv.pe_sums(pe)
            pe_mla_project(pe)
            pe_mla(pe)
            pe_gla(pe)
            pe_rest0(pe)
            pe_layer1(pe)
            pe_second(pe)


SMALL = 2
WEIGHTS = ["ada_w", "mlp_w1", "mlp_w2", "even_w_in", "mla_w_uq", "mla_w_ukv", "even_w_out", "gdn_w_in", "gdn_w_out",
           "w_mem_kv_2", "w_in_a_2", "w_gate_r_2", "w_gate_i_2", "w_kv_shared_2", "w_in_b_2", "w_out_2",
           "w_ffn_in_2", "w_ffn_out_2"]


def feature_major(v):
    v = np.asarray(v)
    v = v.reshape(-1, v.shape[-1] // P, P) if v.shape[-1] % P == 0 else v.reshape(-1, 1, P)
    return np.ascontiguousarray(v.transpose(2, 0, 1).reshape(P, -1))


def laid_out(inputs):
    cols = []
    for name, n in VECTORS:
        if name == "c":
            v = np.stack([np.asarray(inputs["c"])[0], np.asarray(inputs["c_ctx"])])
            v = feature_major(v).reshape(P, 2, KB).transpose(0, 2, 1).reshape(P, -1)
        elif name in ("gdn_a_log", "gdn_dt_bias", "sinks_2"):
            v = np.repeat(np.asarray(inputs[name]).reshape(1, -1), P, 0)
        elif name == "eps":
            v = np.full((P, 1), EPS, np.float32)
        elif name in ("c_ctx",):
            continue
        else:
            v = feature_major(inputs[name])
        assert v.shape == (P, n), (name, v.shape, n)
        cols.append(v)
    maps = {"vec": np.ascontiguousarray(np.concatenate(cols, 1))}
    tokens = np.concatenate([np.asarray(inputs["x"])[0], np.asarray(inputs["ctx"])[0]], 0)
    maps["xt"] = np.ascontiguousarray(tokens.T.reshape(KB, P, T).transpose(1, 0, 2))
    maps["memt"] = np.ascontiguousarray(np.asarray(inputs["mem_2"])[0].T.reshape(KB, P, NMEM).transpose(1, 0, 2))
    tab = np.concatenate([TABLES[n] for n in LASTING + TURNS[0]], 1)
    for i in (1, 2):
        maps[f"tab{i}"] = np.ascontiguousarray(np.concatenate([TABLES[n] for n in TURNS[i]], 1))
    up, bias = np.asarray(inputs["gla_gate_up"])[0], np.asarray(inputs["gla_gate_bias"])[0]
    at = TCOL["mla_rope"][0]
    tab[0:GRANK + 1, at:at + 2 * GH * GDK] = np.concatenate([up, bias[:, None, :]], 1).transpose(1, 0, 2).reshape(GRANK + 1, -1)
    maps["tab"] = np.ascontiguousarray(tab)
    for name in WEIGHTS:
        maps[name] = np.ascontiguousarray(inputs[name])
    return maps


def kernel(**inputs):
    import concourse.bacc as bacc
    from concourse.bass_utils import run_bass_kernel_spmd

    nc = bacc.Bacc("TRN2", target_bir_lowering=False, num_devices=1)
    arrays = laid_out(inputs)
    d = {n: nc.dram_tensor(n, v.shape, mybir.dt.from_np(v.dtype), kind="ExternalInput").ap() for n, v in arrays.items()}
    out = nc.dram_tensor("out_t", (P, KB, LAT), F32, kind="ExternalOutput").ap()
    two_block_kernel(nc, d, out)
    r = run_bass_kernel_spmd(nc, [arrays], core_ids=[0])
    got = r.results[0]["out_t"]
    return np.ascontiguousarray(got.transpose(2, 1, 0).reshape(1, LAT, D))
```
